# Optimizing a Trainium2 kernel written in Bass

```python
import math
import jax, jax.numpy as jnp
from jax import lax
import numpy as np

D_MODEL = 1024
BATCH = 1
SEQ = 2048
DEPTH = 2
DEC_BATCH = 8
DEC_SEQ = 1
PAST_LEN = 4096
PAGE_SIZE = 128

N_EVEN = (DEPTH + 1) // 2
N_ODD = DEPTH // 2
D_MIX = D_MODEL
D_A = D_MIX // 2
HD_A = 64
H_A = D_A // HD_A
R_W = 64
R_A = 64
D_B = D_MIX - D_A
S5_GROUP = 16
G_B = D_B // S5_GROUP
P_B = 64
D_C = D_MIX // 2
HD_C = 64
H_C = D_C // HD_C
Q_BLOCK = 128
SB_BIAS_HI = 4.0
SB_BIAS_LO = 8.0
D_D = D_MIX - D_C
H_D = 4
DV_D = D_D // H_D
DK_D = DV_D // 2
R_G = 16
GLA_TAU = 16.0
GLA_CHUNK = 64
N_SHIFT = 3 * D_A + R_W + R_A
N_PROJ_E = N_SHIFT + D_A + 2 * D_B
N_PROJ_O = 4 * D_C + 2 * H_D * DK_D + D_D + R_G + D_D
DEEPNORM_ALPHA = (2.0 * DEPTH) ** 0.25
DEEPNORM_BETA = (8.0 * DEPTH) ** -0.25
LN_EPS = 1e-5
GN_EPS = 64e-5
RMS_EPS = 1e-5

kernel_name = 'hybrid_rwkv7_s5_stickbreak_gla_decode_step'

def _offsets(widths):
    out, acc = [], 0
    for w in widths[:-1]:
        acc += w
        out.append(acc)
    return out

def heads(a, hd):
    return a.reshape(a.shape[:-1] + (a.shape[-1] // hd, hd))

def layer_norm(x, g, b):
    xf = x.astype(jnp.float32)
    mu = xf.mean(-1, keepdims=True)
    var = jnp.square(xf - mu).mean(-1, keepdims=True)
    return ((xf - mu) * lax.rsqrt(var + LN_EPS) * g + b).astype(x.dtype)

def rwkv7_scan(r, decay, k, v, aa, bb, s0):
    def step(s, inp):
        r_t, w_t, k_t, v_t, a_t, b_t = inp
        sa = jnp.einsum('bhvk,bhk->bhv', s, a_t)
        s = s * w_t[:, :, None, :] + sa[..., None] * b_t[:, :, None, :] + v_t[..., None] * k_t[:, :, None, :]
        return s, jnp.einsum('bhvk,bhk->bhv', s, r_t)
    xs = tuple(jnp.moveaxis(a.astype(jnp.float32), 1, 0) for a in (r, decay, k, v, aa, bb))
    s_fin, ys = lax.scan(step, s0.astype(jnp.float32), xs)
    return jnp.moveaxis(ys, 0, 1), s_fin

def _cplx_combine(e1, e2):
    a1r, a1i, b1r, b1i = e1
    a2r, a2i, b2r, b2i = e2
    return (a2r * a1r - a2i * a1i,
            a2r * a1i + a2i * a1r,
            a2r * b1r - a2i * b1i + b2r,
            a2r * b1i + a2i * b1r + b2i)

def s5_mixer(u, h0_re, h0_im, lam_re, lam_im, log_dt, b_re, b_im, c_re, c_im, d_skip, glu_w, glu_b):
    f32 = jnp.float32
    bsz, t, _ = u.shape
    dt = jnp.exp(log_dt.astype(f32))[:, None]
    lr, li = lam_re.astype(f32), lam_im.astype(f32)
    mag = jnp.exp(lr * dt)
    abar_re, abar_im = mag * jnp.cos(li * dt), mag * jnp.sin(li * dt)
    den = lr * lr + li * li
    nr, ni = abar_re - 1.0, abar_im
    f_re, f_im = (nr * lr + ni * li) / den, (ni * lr - nr * li) / den
    bb_re = f_re[..., None] * b_re - f_im[..., None] * b_im
    bb_im = f_re[..., None] * b_im + f_im[..., None] * b_re
    ug = u.astype(f32).reshape(bsz, t, G_B, S5_GROUP)
    bu_re = jnp.einsum('btgc,gpc->btgp', ug, bb_re)
    bu_im = jnp.einsum('btgc,gpc->btgp', ug, bb_im)
    a_re = jnp.broadcast_to(abar_re, (1, t, G_B, P_B))
    a_im = jnp.broadcast_to(abar_im, (1, t, G_B, P_B))
    cr, ci, sr, si = lax.associative_scan(_cplx_combine, (a_re, a_im, bu_re, bu_im), axis=1)
    h0r = h0_re.astype(f32)[:, None]
    h0i = h0_im.astype(f32)[:, None]
    h_re = sr + cr * h0r - ci * h0i
    h_im = si + cr * h0i + ci * h0r
    y = jnp.einsum('btgp,gcp->btgc', h_re, c_re) - jnp.einsum('btgp,gcp->btgc', h_im, c_im)
    y = y.reshape(bsz, t, D_B) + d_skip * u.astype(f32)
    y = jax.nn.gelu(y)
    y = y * jax.nn.sigmoid(y @ glu_w + glu_b)
    return y, h_re[:, -1], h_im[:, -1]

def even_layer(x, st_rwkv, st_shift, st_re, st_im, w_in, mu_shift, w0, w2, a0, a2, k_k, k_a, r_k,
               gn_g, gn_b, lam_re, lam_im, log_dt, b_re, b_im, c_re, c_im, d_skip, glu_w, glu_b, w_out):
    f32 = jnp.float32
    bsz, t, _ = x.shape
    proj = jnp.einsum('btd,dn->btn', x, w_in).astype(f32)
    z, gate_a, u, gate_b = jnp.split(proj, _offsets([N_SHIFT, D_A, D_B, D_B]), axis=-1)
    z_prev = jnp.concatenate([st_shift.astype(f32)[:, None, :], z[:, :-1]], axis=1)
    zm = z + mu_shift * (z_prev - z)
    r, k, v, wd, ad = jnp.split(zm, _offsets([D_A, D_A, D_A, R_W, R_A]), axis=-1)
    w = -jax.nn.softplus(-(w0 + jnp.tanh(wd) @ w2)) - 0.5
    decay = jnp.exp(-jnp.exp(w))
    a = jax.nn.sigmoid(a0 + ad @ a2)
    kk = heads(k * k_k, HD_A)
    kk = kk / jnp.maximum(jnp.sqrt(jnp.sum(kk * kk, -1, keepdims=True)), 1e-12)
    k = k * (1.0 + (a - 1.0) * k_a)
    r_h, k_h, v_h, a_h, dec_h = (heads(e, HD_A) for e in (r, k, v, a, decay))
    y, s_fin = rwkv7_scan(r_h, dec_h, k_h, v_h, -kk, kk * a_h, st_rwkv)
    mu = y.mean(-1, keepdims=True)
    var = jnp.square(y - mu).mean(-1, keepdims=True)
    y = ((y - mu) * lax.rsqrt(var + GN_EPS)).reshape(bsz, t, D_A) * gn_g + gn_b
    y = y + (jnp.sum(r_h * k_h * r_k, -1, keepdims=True) * v_h).reshape(bsz, t, D_A)
    out_a = y * jax.nn.silu(gate_a)
    y_b, h_re, h_im = s5_mixer(u, st_re, st_im, lam_re, lam_im, log_dt, b_re, b_im, c_re, c_im, d_skip, glu_w, glu_b)
    out_b = y_b * jax.nn.silu(gate_b)
    out = jnp.concatenate([out_a, out_b], axis=-1).astype(x.dtype) @ w_out
    return out, s_fin, z[:, -1], h_re, h_im

def stick_breaking(q, k, v, bias, q_offset):
    f32 = jnp.float32
    bsz, tq, h, d = q.shape
    tk = k.shape[1]
    qb = math.gcd(Q_BLOCK, tq)
    nb = tq // qb
    qf = jnp.moveaxis((q.astype(f32) * d ** -0.5).reshape(bsz, nb, qb, h, d), 1, 0)
    kf, vf = k.astype(f32), v.astype(f32)
    bf = bias.astype(f32)[None, :, None, None]
    key_pos = jnp.arange(tk)

    def block(args):
        qblk, i = args
        qpos = q_offset + i * qb + jnp.arange(qb)
        z = jnp.einsum('bqhd,bkhd->bhqk', qblk, kf) + bf
        causal = key_pos[None, :] < qpos[:, None]
        log_1mb = jnp.where(causal, jax.nn.log_sigmoid(-z), 0.0)
        suffix = lax.cumsum(log_1mb, axis=3, reverse=True)
        excl = jnp.concatenate([suffix[..., 1:], jnp.zeros_like(suffix[..., :1])], axis=-1)
        att = jnp.where(causal, jnp.exp(jax.nn.log_sigmoid(z) + excl), 0.0)
        return jnp.einsum('bhqk,bkhd->bqhd', att, vf)

    out = lax.map(block, (qf, jnp.arange(nb)))
    return jnp.moveaxis(out, 0, 1).reshape(bsz, tq, h, d)

def gla_chunked(q, k, v, log_a, s0):
    f32 = jnp.float32
    bsz, t, h, _ = q.shape
    dv = v.shape[-1]
    c = math.gcd(GLA_CHUNK, t)
    n = t // c

    def to_chunks(a):
        return jnp.moveaxis(a.astype(f32).reshape(bsz, n, c, h, a.shape[-1]), 1, 0)

    qc, kc, vc, gc = (to_chunks(e) for e in (q, k, v, log_a))
    mask = jnp.tril(jnp.ones((c, c), dtype=bool))[None, :, :, None, None]

    def step(s, inp):
        qi, ki, vi, gi = inp
        b = jnp.cumsum(gi, axis=1)
        inter = jnp.einsum('bthk,bhkv->bthv', qi * jnp.exp(b), s)
        diff = jnp.where(mask, b[:, :, None] - b[:, None, :], -jnp.inf)
        scores = jnp.einsum('bthk,bshk,btshk->bhts', qi, ki, jnp.exp(diff))
        intra = jnp.einsum('bhts,bshv->bthv', scores, vi)
        b_last = b[:, -1]
        k_dec = ki * jnp.exp(b_last[:, None] - b)
        s_new = jnp.exp(b_last)[..., None] * s + jnp.einsum('bshk,bshv->bhkv', k_dec, vi)
        return s_new, inter + intra

    s_fin, out = lax.scan(step, s0.astype(f32), (qc, kc, vc, gc))
    return jnp.moveaxis(out, 0, 1).reshape(bsz, t, h, dv), s_fin

def odd_layer(x, k_past, v_past, st_gla, w_in, sb_bias, alpha_w, alpha_b, gn_g, w_out):
    f32 = jnp.float32
    bsz, t, _ = x.shape
    proj = jnp.einsum('btd,dn->btn', x, w_in)
    q_c, k_c, v_c, g_c, q_d, k_d, v_d, a_d, g_d = jnp.split(
        proj, _offsets([D_C, D_C, D_C, D_C, H_D * DK_D, H_D * DK_D, D_D, R_G, D_D]), axis=-1)
    k_new, v_new = heads(k_c, HD_C), heads(v_c, HD_C)
    if k_past is None:
        k_all, v_all, offset = k_new, v_new, 0
    else:
        k_all = jnp.concatenate([k_past.astype(k_new.dtype), k_new], axis=1)
        v_all = jnp.concatenate([v_past.astype(v_new.dtype), v_new], axis=1)
        offset = k_past.shape[1]
    o_c = stick_breaking(heads(q_c, HD_C), k_all, v_all, sb_bias, offset).reshape(bsz, t, D_C)
    log_a = jax.nn.log_sigmoid((a_d @ alpha_w + alpha_b).astype(f32)) / GLA_TAU
    o_d, s_fin = gla_chunked(heads(q_d.astype(f32) * DK_D ** -0.5, DK_D), heads(k_d, DK_D),
                             heads(v_d, DV_D), heads(log_a, DK_D), st_gla)
    o_d = (o_d * lax.rsqrt(jnp.mean(o_d * o_d, -1, keepdims=True) + RMS_EPS)).reshape(bsz, t, D_D) * gn_g
    out = jnp.concatenate([o_c * jax.nn.silu(g_c.astype(f32)), o_d * jax.nn.silu(g_d.astype(f32))], axis=-1)
    return out.astype(x.dtype) @ w_out, k_new, v_new, s_fin

def setup_inputs(seed: int = 0) -> dict:
    key = jax.random.key(seed)
    ks = iter(jax.random.split(key, 48))
    f32 = jnp.float32

    def nrm(shape, scale=1.0):
        return jax.random.normal(next(ks), shape, f32) * scale

    n_pages = PAST_LEN // PAGE_SIZE
    n_phys = (DEC_BATCH * n_pages * 5) // 4
    x_prompt = nrm((BATCH, SEQ, D_MODEL))
    x_sample = nrm((DEC_BATCH, DEC_SEQ, D_MODEL))
    state_rwkv = nrm((N_EVEN, DEC_BATCH, H_A, HD_A, HD_A), 0.5)
    state_shift = nrm((N_EVEN, DEC_BATCH, N_SHIFT))
    state_s5_re = nrm((N_EVEN, DEC_BATCH, G_B, P_B), 0.3)
    state_s5_im = nrm((N_EVEN, DEC_BATCH, G_B, P_B), 0.3)
    cache_k = nrm((N_ODD, n_phys, PAGE_SIZE, H_C, HD_C))
    cache_v = nrm((N_ODD, n_phys, PAGE_SIZE, H_C, HD_C))
    state_gla = nrm((N_ODD, DEC_BATCH, H_D, DK_D, DV_D), 0.3)
    page_table = jax.random.permutation(next(ks), n_phys)[: DEC_BATCH * n_pages].reshape(DEC_BATCH, n_pages).astype(jnp.int32)
    ln_g = 1.0 + nrm((DEPTH, D_MODEL), 0.05)
    ln_b = nrm((DEPTH, D_MODEL), 0.01)
    w_in_e = nrm((N_EVEN, D_MODEL, N_PROJ_E), D_MODEL ** -0.5)
    mu_shift = jax.random.uniform(next(ks), (N_EVEN, N_SHIFT), f32)
    ramp = jnp.arange(D_A, dtype=f32) / (D_A - 1)
    rwkv_w0 = -6.0 + 5.0 * ramp ** 1.5 + nrm((N_EVEN, D_A), 0.1)
    rwkv_w2 = nrm((N_EVEN, R_W, D_A), 0.1 * R_W ** -0.5)
    rwkv_a0 = nrm((N_EVEN, D_A), 0.1)
    rwkv_a2 = nrm((N_EVEN, R_A, D_A), 0.1 * R_A ** -0.5)
    rwkv_k_k = 0.85 + nrm((N_EVEN, D_A), 0.05)
    rwkv_k_a = 1.0 + nrm((N_EVEN, D_A), 0.05)
    rwkv_r_k = nrm((N_EVEN, H_A, HD_A), 0.1)
    rwkv_gn_g = 1.0 + nrm((N_EVEN, D_A), 0.05)
    rwkv_gn_b = nrm((N_EVEN, D_A), 0.01)
    s5_lambda_re = -0.5 + nrm((N_EVEN, G_B, P_B), 0.01)
    s5_lambda_im = math.pi * jnp.arange(P_B, dtype=f32) + nrm((N_EVEN, G_B, P_B), 0.01)
    s5_log_dt = jax.random.uniform(next(ks), (N_EVEN, G_B), f32, math.log(0.001), math.log(0.1))
    s5_b_re = nrm((N_EVEN, G_B, P_B, S5_GROUP), (2.0 * S5_GROUP) ** -0.5)
    s5_b_im = nrm((N_EVEN, G_B, P_B, S5_GROUP), (2.0 * S5_GROUP) ** -0.5)
    s5_c_re = nrm((N_EVEN, G_B, S5_GROUP, P_B), (2.0 * P_B) ** -0.5)
    s5_c_im = nrm((N_EVEN, G_B, S5_GROUP, P_B), (2.0 * P_B) ** -0.5)
    s5_d = nrm((N_EVEN, D_B))
    s5_glu_w = nrm((N_EVEN, D_B, D_B), D_B ** -0.5)
    s5_glu_b = nrm((N_EVEN, D_B), 0.01)
    w_out_e = nrm((N_EVEN, D_MIX, D_MODEL), DEEPNORM_BETA * D_MIX ** -0.5)
    w_in_o = nrm((N_ODD, D_MODEL, N_PROJ_O), D_MODEL ** -0.5)
    sb_bias = -jnp.linspace(SB_BIAS_HI, SB_BIAS_LO, H_C, dtype=f32)[None, :] + nrm((N_ODD, H_C), 0.05)
    gla_alpha_w = nrm((N_ODD, R_G, H_D * DK_D), R_G ** -0.5)
    gla_alpha_b = nrm((N_ODD, H_D * DK_D), 0.5)
    gla_gn_g = 1.0 + nrm((N_ODD, D_D), 0.05)
    w_out_o = nrm((N_ODD, D_MIX, D_MODEL), DEEPNORM_BETA * D_MIX ** -0.5)
    return {'x_prompt': x_prompt, 'x_sample': x_sample, 'state_rwkv': state_rwkv, 'state_shift': state_shift,
            'state_s5_re': state_s5_re, 'state_s5_im': state_s5_im, 'cache_k': cache_k, 'cache_v': cache_v,
            'state_gla': state_gla, 'page_table': page_table, 'ln_g': ln_g, 'ln_b': ln_b,
            'w_in_e': w_in_e, 'mu_shift': mu_shift, 'rwkv_w0': rwkv_w0, 'rwkv_w2': rwkv_w2,
            'rwkv_a0': rwkv_a0, 'rwkv_a2': rwkv_a2, 'rwkv_k_k': rwkv_k_k, 'rwkv_k_a': rwkv_k_a,
            'rwkv_r_k': rwkv_r_k, 'rwkv_gn_g': rwkv_gn_g, 'rwkv_gn_b': rwkv_gn_b,
            's5_lambda_re': s5_lambda_re, 's5_lambda_im': s5_lambda_im, 's5_log_dt': s5_log_dt,
            's5_b_re': s5_b_re, 's5_b_im': s5_b_im, 's5_c_re': s5_c_re, 's5_c_im': s5_c_im,
            's5_d': s5_d, 's5_glu_w': s5_glu_w, 's5_glu_b': s5_glu_b, 'w_out_e': w_out_e,
            'w_in_o': w_in_o, 'sb_bias': sb_bias, 'gla_alpha_w': gla_alpha_w, 'gla_alpha_b': gla_alpha_b,
            'gla_gn_g': gla_gn_g, 'w_out_o': w_out_o}

def reference(x_prompt, x_sample, state_rwkv, state_shift, state_s5_re, state_s5_im, cache_k, cache_v,
              state_gla, page_table, ln_g, ln_b, w_in_e, mu_shift, rwkv_w0, rwkv_w2, rwkv_a0, rwkv_a2,
              rwkv_k_k, rwkv_k_a, rwkv_r_k, rwkv_gn_g, rwkv_gn_b, s5_lambda_re, s5_lambda_im, s5_log_dt,
              s5_b_re, s5_b_im, s5_c_re, s5_c_im, s5_d, s5_glu_w, s5_glu_b, w_out_e,
              w_in_o, sb_bias, gla_alpha_w, gla_alpha_b, gla_gn_g, w_out_o):
    f32 = jnp.float32
    bp = x_prompt.shape[0]
    bs = x_sample.shape[0]
    n_pages = page_table.shape[1]
    xp, xs = x_prompt, x_sample
    rw_p, rw_s, sh_p, sh_s, re_p, re_s, im_p, im_s = [], [], [], [], [], [], [], []
    kr_p, kr_s, vr_p, vr_s, gl_p, gl_s = [], [], [], [], [], []
    for l in range(DEPTH):
        i = l // 2
        if l % 2 == 0:
            wts = (w_in_e[i], mu_shift[i], rwkv_w0[i], rwkv_w2[i], rwkv_a0[i], rwkv_a2[i], rwkv_k_k[i],
                   rwkv_k_a[i], rwkv_r_k[i], rwkv_gn_g[i], rwkv_gn_b[i], s5_lambda_re[i], s5_lambda_im[i],
                   s5_log_dt[i], s5_b_re[i], s5_b_im[i], s5_c_re[i], s5_c_im[i], s5_d[i], s5_glu_w[i],
                   s5_glu_b[i], w_out_e[i])
            yp, a1, a2, a3, a4 = even_layer(
                xp, jnp.zeros((bp, H_A, HD_A, HD_A), f32), jnp.zeros((bp, N_SHIFT), f32),
                jnp.zeros((bp, G_B, P_B), f32), jnp.zeros((bp, G_B, P_B), f32), *wts)
            ys, b1, b2, b3, b4 = even_layer(xs, state_rwkv[i], state_shift[i], state_s5_re[i], state_s5_im[i], *wts)
            rw_p.append(a1); sh_p.append(a2); re_p.append(a3); im_p.append(a4)
            rw_s.append(b1); sh_s.append(b2); re_s.append(b3); im_s.append(b4)
        else:
            wts = (w_in_o[i], sb_bias[i], gla_alpha_w[i], gla_alpha_b[i], gla_gn_g[i], w_out_o[i])
            yp, k1, v1, g1 = odd_layer(xp, None, None, jnp.zeros((bp, H_D, DK_D, DV_D), f32), *wts)
            k_past = cache_k[i][page_table].reshape(bs, n_pages * PAGE_SIZE, H_C, HD_C)
            v_past = cache_v[i][page_table].reshape(bs, n_pages * PAGE_SIZE, H_C, HD_C)
            ys, k2, v2, g2 = odd_layer(xs, k_past, v_past, state_gla[i], *wts)
            kr_p.append(k1); vr_p.append(v1); gl_p.append(g1)
            kr_s.append(k2); vr_s.append(v2); gl_s.append(g2)
        xp = layer_norm(DEEPNORM_ALPHA * xp + yp, ln_g[l], ln_b[l])
        xs = layer_norm(DEEPNORM_ALPHA * xs + ys, ln_g[l], ln_b[l])
    return (xp, xs,
            jnp.stack(rw_p), jnp.stack(rw_s), jnp.stack(sh_p), jnp.stack(sh_s),
            jnp.stack(re_p), jnp.stack(re_s), jnp.stack(im_p), jnp.stack(im_s),
            jnp.stack(kr_p), jnp.stack(kr_s), jnp.stack(vr_p), jnp.stack(vr_s),
            jnp.stack(gl_p), jnp.stack(gl_s))


_drawn_inputs = setup_inputs


def setup_inputs(seed=0):
    import zlib

    import numpy as np

    out = dict(_drawn_inputs(seed))
    spreads = {}
    factors = {'cache_k': 4.813,
     'cache_v': 3.775,
     'ln_b': 3.796,
     'rwkv_w2': 8.0,
     'rwkv_gn_g': 5.799,
     'rwkv_gn_b': 24.131,
     's5_lambda_re': 16.05,
     's5_c_re': 4.083,
     's5_c_im': 3.897,
     's5_glu_b': 64.0,
     'sb_bias': 4.687,
     'gla_gn_g': 7.686}
    for name, (base, spread) in spreads.items():
        noise = np.random.default_rng([zlib.crc32(name.encode()), seed]).standard_normal(out[name].shape)
        drawn = base * np.exp(spread * noise) if base else spread * noise
        out[name] = __import__('jax').numpy.asarray(drawn.astype(out[name].dtype))
    for name, factor in factors.items():
        out[name] = (out[name] * factor).astype(out[name].dtype)
    return out
```

```python
from contextlib import ExitStack

import numpy as np
import concourse.bass as bass
from concourse import mybir

F32 = mybir.dt.float32
I32 = mybir.dt.int32
ALU = mybir.AluOpType
ACT = mybir.ActivationFunctionType
AX = mybir.AxisListType

P = 128
D = 1024
KT = D // P
SEQ = 2048
NS = 8
COLS = SEQ + NS
TT = SEQ // P
CH = 64
NCH = SEQ // CH
PAGES = 32
BLK = 412
NBLK = -(-COLS // BLK)
ALPHA = 4.0 ** 0.25
LN_EPS = 1e-5
GN_EPS = 64e-5
RMS_EPS = 1e-5
ds = bass.ds
LN_EXP = "natural_log_exp_and_others"


class Chain:

    def __init__(self, eng, sem):
        self.eng, self.sem, self.base, self.n = eng, sem, 0, 0

    def start(self, base):
        self.base, self.n = base, 0

    def __call__(self, ins):
        self.n += 1
        ins.then_inc(self.sem, 1)
        self.eng.wait_ge(self.sem, self.base + self.n)


class Stage:

    def __init__(self, nc, name):
        self.nc, self.name, self.ctx, self.sems = nc, name, ExitStack(), []

    def __enter__(self):
        self.ctx.__enter__()
        return self

    def __exit__(self, *a):
        self.ctx.__exit__(*a)
        self.nc.clear_and_free_semaphores(self.sems)
        self.nc.all_engine_barrier()

    def sb(self, name, shape, dt=F32):
        return self.ctx.enter_context(self.nc.sbuf_tensor(f"{self.name}_{name}", shape, dt))

    def ps(self, name, shape):
        return self.ctx.enter_context(self.nc.psum_tensor(f"{self.name}_{name}", shape, F32))

    def sem(self, name):
        self.sems.append(self.nc.alloc_semaphore(name=f"{self.name}_{name}"))
        return self.sems[-1]

    def block(self):
        return self.ctx.enter_context(self.nc.Block())


def project_channels(nc, name, xT, w, out, n_tiles):
    with Stage(nc, name) as s:
        x = s.sb("x", [P, KT, COLS])
        wt = s.sb("w", [P, 2, KT, P])
        ot = s.sb("o", [P, 2, COLS])
        acc = s.ps("acc", [P, NBLK, 512])
        x_ready = [s.sem(f"x_ready{k}") for k in range(KT)]
        w_ready = [s.sem("w_ready0"), s.sem("w_ready1")]
        blk_done, blk_free = s.sem("blk_done"), s.sem("blk_free")
        o_free = [s.sem("o_free0"), s.sem("o_free1")]
        LEAD = 2 * NBLK
        pairs = n_tiles // 2
        block = s.block()

        def loop(eng, step):
            with eng.Fori(0, pairs) as m:
                for h in (0, 1):
                    step(m * 2 + h, h, m)
            for h in range(n_tiles % 2):
                step(2 * pairs, 0, pairs)

        @block.sync
        def _(sp):
            for k in range(KT):
                sp.dma_start(x[:, k, :], xT[:, k, :]).then_inc(x_ready[k], 16)

            def step(n, h, m):
                sp.wait_ge(blk_done, (n + 1) * NBLK)
                sp.dma_start(wt[:, h], w[ds(n, 1)].rearrange("o p k c -> p (o k) c")).then_inc(w_ready[h], 16)
            loop(sp, step)

        @block.tensor
        def _(pe):
            pe.sem_inc(blk_done, LEAD)
            for k in range(KT):
                pe.wait_ge(x_ready[k], 16)

            def step(n, h, m):
                pe.wait_ge(w_ready[h], 16 * m + 16)
                for b in range(NBLK):
                    width = min(BLK, COLS - b * BLK)
                    pe.wait_ge(blk_free, n * NBLK + b + 1)
                    for k in range(KT):
                        mm = pe.matmul(acc[:, b, 0:width], wt[:, h, k, :], x[:, k, b * BLK:b * BLK + width],
                                       start=(k == 0), stop=(k == KT - 1))
                    mm.then_inc(blk_done, 1)
            loop(pe, step)

        @block.vector
        def _(dve):
            dve.sem_inc(blk_free, NBLK)
            dve.sem_inc(o_free[0], 16)
            dve.sem_inc(o_free[1], 16)

            def step(n, h, m):
                dve.wait_ge(o_free[h], 16 * m + 16)
                for b in range(NBLK):
                    width = min(BLK, COLS - b * BLK)
                    dve.wait_ge(blk_done, LEAD + n * NBLK + b + 1)
                    cp = dve.tensor_copy(ot[:, h, b * BLK:b * BLK + width], acc[:, b, 0:width])
                    cp.then_inc(blk_free, 1)
            loop(dve, step)

        @block.scalar
        def _(act):
            def step(n, h, m):
                act.wait_ge(blk_free, NBLK + (n + 1) * NBLK)
                act.dma_start(out[ds(n, 1)].rearrange("o p c -> p (o c)"), ot[:, h, :]).then_inc(o_free[h], 16)
            loop(act, step)
            act.wait_ge(o_free[0], 16 * (1 + pairs + n_tiles % 2))
            act.wait_ge(o_free[1], 16 * (1 + pairs))


def token_tiles(eng, step):
    with eng.Fori(0, TT // 2) as m:
        for h in (0, 1):
            step(m * 2 + h, h, m, P)
    step(TT, 0, TT // 2, NS)


def project_tokens(nc, name, src, w, width, out):
    halves = width // 512
    with Stage(nc, name) as s:
        wt = s.sb("w", [P, KT, width])
        xt = s.sb("x", [P, 2, KT, P])
        ot = s.sb("o", [P, 2, width])
        acc = s.ps("acc", [P, 2, halves, 512])
        w_ready = s.sem("w_ready")
        x_ready = [s.sem("x_ready0"), s.sem("x_ready1")]
        acc_done, acc_free = s.sem("acc_done"), s.sem("acc_free")
        o_free = [s.sem("o_free0"), s.sem("o_free1")]
        block = s.block()

        @block.sync
        def _(sp):
            sp.dma_start(wt[:, :, :], w).then_inc(w_ready, 16)

            def step(t, h, m, rows):
                sp.wait_ge(acc_done, t + 1)
                sp.dma_start(xt[:, h, :, 0:rows], src(t, rows)).then_inc(x_ready[h], 16)
            token_tiles(sp, step)

        @block.tensor
        def _(pe):
            pe.sem_inc(acc_done, 2)
            pe.wait_ge(w_ready, 16)

            def step(t, h, m, rows):
                pe.wait_ge(x_ready[h], 16 * m + 16)
                pe.wait_ge(acc_free, t + 1)
                for q in range(halves):
                    for k in range(KT):
                        mm = pe.matmul(acc[0:rows, h, q, :], xt[:, h, k, 0:rows], wt[:, k, q * 512:q * 512 + 512],
                                       start=(k == 0), stop=(k == KT - 1))
                mm.then_inc(acc_done, 1)
            token_tiles(pe, step)

        @block.vector
        def _(dve):
            dve.sem_inc(acc_free, 2)
            dve.sem_inc(o_free[0], 16)
            dve.sem_inc(o_free[1], 16)

            def step(t, h, m, rows):
                dve.wait_ge(acc_done, 2 + t + 1)
                dve.wait_ge(o_free[h], 16 * m + 16)
                cp = dve.tensor_copy(ot[0:rows, h, :], acc[0:rows, h].rearrange("p q c -> p (q c)"))
                cp.then_inc(acc_free, 1)
            token_tiles(dve, step)

        @block.scalar
        def _(act):
            def step(t, h, m, rows):
                act.wait_ge(acc_free, 2 + t + 1)
                act.dma_start(out[ds(t, 1), 0:rows].rearrange("o p c -> p (o c)"),
                              ot[0:rows, h, :]).then_inc(o_free[h], 16)
            token_tiles(act, step)
            act.wait_ge(o_free[0], 16 * (TT // 2 + 2))
            act.wait_ge(o_free[1], 16 * (TT // 2 + 1))


def out_projection(nc, name, catT, w, x_res, gain, shift, ident, y_tok, xT_out):
    with Stage(nc, name) as s:
        wt = s.sb("w", [P, KT, D])
        idt = s.sb("ident", [P, P])
        g = s.sb("gain", [P, D])
        b = s.sb("shift", [P, D])
        ct = s.sb("cat", [P, 2, KT, P])
        xr = s.sb("res", [P, 2, D])
        y = s.sb("y", [P, 2, D])
        st = s.sb("stats", [P, 2, 2, 6])
        mv = s.sb("mean_var", [P, 2, 2])
        sd = s.sb("std", [P, 2, 2])
        yT = s.sb("yT", [P, 2, KT, P])
        acc = s.ps("acc", [P, 2, 2, 512])
        tr = s.ps("tr", [P, 2, 2, 512])
        w_ready = s.sem("w_ready")
        c_ready = [s.sem("c_ready0"), s.sem("c_ready1")]
        c_free, acc_done, acc_free = s.sem("c_free"), s.sem("acc_done"), s.sem("acc_free")
        var_ready, std_ready, y_ready, y_free = (s.sem("var_ready"), s.sem("std_ready"), s.sem("y_ready"),
                                                 s.sem("y_free"))
        tr_done, yT_ready, yT_free = s.sem("tr_done"), s.sem("yT_ready"), s.sem("yT_free")
        own = s.sem("own")
        block = s.block()
        both = xT_out is not None

        @block.sync
        def _(sp):
            sp.dma_start(wt[:, :, :], w).then_inc(w_ready, 16)
            sp.dma_start(g[:, :], gain.broadcast_to([P, D])).then_inc(w_ready, 16)
            sp.dma_start(b[:, :], shift.broadcast_to([P, D])).then_inc(w_ready, 16)
            sp.dma_start(idt[:, :], ident).then_inc(w_ready, 16)

            def step(t, h, m, rows):
                sp.wait_ge(c_free, t + 1)
                sp.dma_start(ct[:, h, :, 0:rows],
                             catT[:, :, ds(t * P, rows)].rearrange("k p c -> p k c")).then_inc(c_ready[h], 16)
                sp.dma_start(xr[0:rows, h, :], x_res[ds(t * P, rows), :]).then_inc(c_ready[h], 16)
            token_tiles(sp, step)

        @block.tensor
        def _(pe):
            pe.wait_ge(w_ready, 64)

            def transpose(t, h, rows):
                pe.wait_ge(y_ready, t + 1)
                pe.wait_ge(yT_ready, t)
                for k in range(KT):
                    mm = pe.transpose(tr[:, h, k // 4, (k % 4) * P:(k % 4) * P + rows],
                                      y[0:rows, h, k * P:(k + 1) * P], idt[0:rows, 0:rows])
                mm.then_inc(tr_done, 1)

            def step(t, h, m, rows):
                pe.wait_ge(c_ready[h], 32 * m + 32)
                pe.wait_ge(acc_free, t + 1)
                for q in range(2):
                    for k in range(KT):
                        mm = pe.matmul(acc[0:rows, h, q, :], ct[:, h, k, 0:rows], wt[:, k, q * 512:q * 512 + 512],
                                       start=(k == 0), stop=(k == KT - 1))
                mm.then_inc(acc_done, 1)
                if both:
                    transpose(t, h, rows)
            token_tiles(pe, step)

        K = 6

        @block.vector
        def _(dve):
            link = Chain(dve, own)
            dve.sem_inc(acc_free, 2)
            dve.sem_inc(c_free, 2)
            dve.wait_ge(w_ready, 64)

            def step(t, h, m, rows):
                link.start(t * K)
                dve.wait_ge(acc_done, t + 1)
                dve.wait_ge(c_ready[h], 32 * m + 32)
                dve.wait_ge(y_free, 16 * t)
                r = slice(0, rows)
                link(dve.scalar_tensor_tensor(out=y[r, h, :], in0=xr[r, h, :], scalar=ALPHA,
                                              in1=acc[r, h].rearrange("p q c -> p (q c)"),
                                              op0=ALU.mult, op1=ALU.add))
                dve.bn_stats(st[r, h, 0, :], y[r, h, 0:512])
                link(dve.bn_stats(st[r, h, 1, :], y[r, h, 512:1024]))
                dve.sem_inc(acc_free, 1)
                dve.sem_inc(c_free, 1)
                link(dve.bn_aggr(mv[r, h, :], st[r, h].rearrange("p a b -> p (a b)")))
                dve.tensor_scalar(sd[r, h, 0:1], mv[r, h, 1:2], LN_EPS, None, ALU.add).then_inc(var_ready, 1)
                dve.wait_ge(std_ready, t + 1)
                link(dve.reciprocal(sd[r, h, 0:1], sd[r, h, 1:2]))
                link(dve.tensor_scalar(y[r, h, :], y[r, h, :], mv[r, h, 0:1], sd[r, h, 0:1],
                                       ALU.subtract, ALU.mult))
                link(dve.tensor_tensor(y[r, h, :], y[r, h, :], g[r, :], ALU.mult))
                assert link.n == K
                dve.tensor_tensor(y[r, h, :], y[r, h, :], b[r, :], ALU.add).then_inc(y_ready, 1)
            token_tiles(dve, step)

        @block.scalar
        def _(act):
            def step(t, h, m, rows):
                r = slice(0, rows)
                act.wait_ge(var_ready, t + 1)
                act.activation(sd[r, h, 1:2], sd[r, h, 0:1], ACT.Sqrt).then_inc(std_ready, 1)
                if both:
                    act.wait_ge(tr_done, t + 1)
                    act.wait_ge(yT_free, 16 * t)
                    act.copy(yT[:, h, :, 0:rows],
                             tr[:, h].rearrange("p q (k c) -> p (q k) c", c=P)[:, :, 0:rows]).then_inc(yT_ready, 1)
            token_tiles(act, step)

        @block.gpsimd
        def _(pool):
            def step(t, h, m, rows):
                pool.wait_ge(y_ready, t + 1)
                pool.dma_start(y_tok[ds(t * P, rows), :], y[0:rows, h, :]).then_inc(y_free, 16)
                if both:
                    pool.wait_ge(yT_ready, t + 1)
                    pool.dma_start(xT_out[:, :, ds(t * P, rows)], yT[:, h, :, 0:rows]).then_inc(yT_free, 16)
            token_tiles(pool, step)
            pool.wait_ge(y_free, 16 * (TT + 1))
            if both:
                pool.wait_ge(yT_free, 16 * (TT + 1))


A_T, R_T, B_T, K_T, V_, B_H, K_H = range(7)
MU_R, MU_K, MU_V, W0, A0, KK_, KA_, RK_, GN_G, GN_B = range(10)
S_R, S_W, S_B, S_K, S_A, S_V = range(6)
NEG_EXP_HALF = -float(np.exp(-0.5))


def rwkv_operands(nc, z, z_last, mu_low, prm, w2, a2, const, ops, wc, bonus, sample_vecs):
    with Stage(nc, "rp") as s:
        big = lambda n: s.sb(n, [P, COLS])
        low, mask = big("low"), big("mask")
        r, k, v, t1, t2, t3, a, ld, c = (big(n) for n in ("r", "k", "v", "t1", "t2", "t3", "a", "ld", "c"))
        ep, en, ec, kk, kp, ka, rk = (big(n) for n in ("ep", "en", "ec", "kk", "kp", "ka", "rk"))
        pr = s.sb("prm", [P, 4, 10])
        pj = s.sb("prj", [P, 10])
        omka = s.sb("omka", [P, 1])
        mul = s.sb("mul", [P, 1])
        w2t, a2t, ones, idt = s.sb("w2", [P, 512]), s.sb("a2", [P, 512]), s.sb("ones", [P, P]), s.sb("id", [P, P])
        w2j, a2j = s.sb("w2j", [P, P]), s.sb("a2j", [P, P])
        vec = s.sb("vec", [P, 16, NS])
        vecT = s.sb("vecT", [6 * NS, P])
        wce = s.sb("wce", [P, NCH])
        acc = s.ps("acc", [P, NBLK, 512])
        acb = s.ps("acb", [P, 2, 512])
        trp = s.ps("trp", [P, 512])
        names = ("cst", "low_in", "low_z", "low_t", "zin", "pool_d", "rkv", "mm", "mm_free", "sgm", "scan", "pool_cw",
                 "sq", "ce", "exps", "kkp", "pool_kp", "rkr", "bmm", "bfree", "pout", "dout", "vecs", "vtr", "vst",
                 "stored", "own", "pown", "lora", "init")
        q = {n: s.sem(n) for n in names}
        blocks = [(b * BLK, min(BLK, COLS - b * BLK)) for b in range(NBLK)]
        block = s.block()
        NST = 10

        @block.sync
        def _(sp):
            for dst, src in ((pr[:, :, :], prm), (mul[:, :], mu_low), (w2t[:, :], w2), (a2t[:, :], a2),
                             (ones[:, :], const["bones"]), (idt[:, :], const["ident"]), (mask[:, :], const["reset"])):
                sp.dma_start(dst, src).then_inc(q["cst"], 16)
            sp.wait_ge(q["init"], 1)
            sp.dma_start(low[:, :], z[12]).then_inc(q["low_in"], 16)
            sp.dma_start(c[:, 1:SEQ], z[12][:, 0:SEQ - 1]).then_inc(q["low_in"], 16)
            sp.dma_start(c[:, SEQ:COLS], z_last[:, 12, :]).then_inc(q["low_in"], 16)
            with sp.Fori(0, 4) as j:
                sp.wait_ge(q["stored"], j * 16 * NST)
                for n, (t, d) in enumerate(((r, t1), (k, t2), (v, t3))):
                    sp.dma_start(t[:, :], z[ds(j + 4 * n, 1)].rearrange("o p c -> p (o c)")).then_inc(q["zin"], 16)
                    sp.dma_start(d[:, 1:SEQ], z[ds(j + 4 * n, 1), :, 0:SEQ - 1]
                                 .rearrange("o p c -> p (o c)")).then_inc(q["zin"], 16)
                    sp.dma_start(d[:, SEQ:COLS], z_last[:, ds(j + 4 * n, 1), :]
                                 .rearrange("p o c -> p (o c)")).then_inc(q["zin"], 16)
                sp.wait_ge(q["dout"], 4 * j + 4)
                sp.wait_ge(q["pout"], 3 * j + 3)
                for n, t in ((A_T, t3), (B_T, t1), (K_T, en), (R_T, ep), (V_, v), (B_H, ka), (K_H, ec)):
                    sp.dma_start(ops[:, n, ds(j, 1), :].rearrange("p o c -> p (o c)"),
                                 t[:, 0:SEQ]).then_inc(q["stored"], 16)
                sp.dma_start(bonus[ds(j, 1)].rearrange("o p c -> p (o c)"), ld[:, :]).then_inc(q["stored"], 16)
                sp.dma_start(wc[:, ds(j, 1), :].rearrange("p o c -> p (o c)"), wce[:, :]).then_inc(q["stored"], 16)
                sp.wait_ge(q["vst"], j + 1)
                sp.dma_start(sample_vecs[:, :, ds(j * P, P)].rearrange("v b c -> (v b) c"),
                             vecT[:, :]).then_inc(q["stored"], 16)
            sp.wait_ge(q["stored"], 4 * 16 * NST)

        @block.tensor
        def _(pe):
            pe.sem_inc(q["mm_free"], NBLK)
            pe.sem_inc(q["bfree"], 2)
            pe.wait_ge(q["cst"], 7 * 16)
            pe.wait_ge(q["low_t"], 1)
            with pe.Fori(0, 4) as j:
                def product(n, w, x):
                    for b, (at, width) in enumerate(blocks):
                        pe.wait_ge(q["mm_free"], j * 3 * NBLK + n * NBLK + b + 1)
                        pe.matmul(acc[:, b, 0:width], w, x[:, at:at + width], start=True,
                                  stop=True).then_inc(q["mm"], 1)
                pe.wait_ge(q["lora"], 2 * j + 2)
                product(0, w2j[:, :], low)
                product(1, a2j[:, :], low)
                pe.wait_ge(q["sq"], j + 1)
                product(2, ones[:, :], t1)
                pe.wait_ge(q["rkr"], j + 1)
                for b, (at, width) in enumerate(blocks):
                    pe.wait_ge(q["bfree"], j * NBLK + b + 1)
                    pe.matmul(acb[:, b % 2, 0:width], ones[:, :], rk[:, at:at + width], start=True,
                              stop=True).then_inc(q["bmm"], 1)
                pe.wait_ge(q["vecs"], j + 1)
                pe.transpose(trp[:, 0:P], vec[:, :, :].rearrange("p v b -> p (v b)"),
                             idt[:, :]).then_inc(q["vtr"], 1)

        @block.scalar
        def _(act):
            act.wait_ge(q["cst"], 7 * 16)
            act.wait_ge(q["low_z"], 1)
            act.activation(low[0:64, :], low[0:64, :], ACT.Tanh).then_inc(q["low_t"], 1)
            with act.Fori(0, 4) as j:

                def blocks_of(n, func, dst, bias):
                    for b, (at, width) in enumerate(blocks):
                        act.wait_ge(q["mm"], j * 3 * NBLK + n * NBLK + b + 1)
                        act.activation(dst[:, at:at + width], acc[:, b, 0:width], func,
                                       bias=bias).then_inc(q["mm_free"], 1)
                act.wait_ge(q["rkv"], 3 * j + 3)
                blocks_of(0, ACT.Sigmoid, ld, pj[:, W0:W0 + 1])
                blocks_of(1, ACT.Sigmoid, a, pj[:, A0:A0 + 1])
                act.activation(t1[:, :], k[:, :], ACT.Square, scale=pj[:, KK_:KK_ + 1]).then_inc(q["sq"], 1)
                blocks_of(2, ACT.Sqrt, t2, 0.0)
                act.wait_ge(q["scan"], j + 1)
                act.activation(ep[:, :], c[:, :], ACT.Exp).then_inc(q["exps"], 1)
                act.activation(en[:, :], c[:, :], ACT.Exp, scale=-1.0).then_inc(q["exps"], 1)
                act.wait_ge(q["pool_cw"], j + 1)
                act.activation(t3[:, :], t3[:, :], ACT.Exp).then_inc(q["exps"], 1)
                act.wait_ge(q["ce"], j + 1)
                act.activation(ec[:, :], ec[:, :], ACT.Exp).then_inc(q["exps"], 1)
                act.activation(wce[:, :], c[:, CH - 1:SEQ:CH], ACT.Exp).then_inc(q["exps"], 1)
                act.wait_ge(q["vtr"], j + 1)
                act.copy(vecT[:, :], trp[0:6 * NS, 0:P]).then_inc(q["vst"], 1)

        @block.vector
        def _(dve):
            link = Chain(dve, q["own"])
            link.start(0)
            dve.memset(c[:, 0:1], 0.0)
            link(dve.memset(vec[:, :, :], 0.0))
            dve.sem_inc(q["init"], 1)
            dve.wait_ge(q["cst"], 7 * 16)
            dve.wait_ge(q["low_in"], 48)
            link(dve.tensor_tensor(c[:, :], c[:, :], low[:, :], ALU.subtract))
            dve.scalar_tensor_tensor(out=low[:, :], in0=c[:, :], scalar=mul[:, 0:1], in1=low[:, :],
                                     op0=ALU.mult, op1=ALU.add).then_inc(q["low_z"], 1)
            FIRST, K = 2, 11
            assert link.n == FIRST
            with dve.Fori(0, 4) as j:
                link.start(FIRST + j * K)
                dve.wait_ge(q["stored"], j * 16 * NST)
                link(dve.tensor_copy(pj[:, :], pr[:, ds(j, 1), :].rearrange("p o c -> p (o c)")))
                link(dve.tensor_scalar(omka[:, :], pj[:, KA_:KA_ + 1], -1.0, 1.0, ALU.mult, ALU.add))
                dve.tensor_copy(w2j[:, :], w2t[:, ds(j * P, P)]).then_inc(q["lora"], 1)
                dve.tensor_copy(a2j[:, :], a2t[:, ds(j * P, P)]).then_inc(q["lora"], 1)
                for n, (t, d) in enumerate(((r, t1), (k, t2), (v, t3))):
                    dve.wait_ge(q["pool_d"], 3 * j + n + 1)
                    dve.scalar_tensor_tensor(out=t[:, :], in0=d[:, :], scalar=pj[:, MU_R + n:MU_R + n + 1], in1=t[:, :],
                                             op0=ALU.mult, op1=ALU.add).then_inc(q["rkv"], 1)
                dve.wait_ge(q["mm_free"], NBLK + j * 3 * NBLK + NBLK)
                link(dve.tensor_scalar(ld[:, :], ld[:, :], NEG_EXP_HALF, None, ALU.mult))
                dve.tensor_tensor_scan(c[:, :], mask[:, :], ld[:, :], 0.0, ALU.mult,
                                       ALU.add).then_inc(q["scan"], 1)
                dve.wait_ge(q["scan"], j + 1)
                ends = c[:, CH - 1:SEQ:CH].rearrange("p (n o) -> p n o", o=1).broadcast_to([P, NCH, CH])
                link(dve.tensor_tensor(ec[:, 0:SEQ].rearrange("p (n t) -> p n t", t=CH), ends,
                                       c[:, 0:SEQ].rearrange("p (n t) -> p n t", t=CH), ALU.subtract))
                dve.memset(ec[:, SEQ:COLS], 0.0).then_inc(q["ce"], 1)
                dve.wait_ge(q["mm_free"], NBLK + j * 3 * NBLK + 2 * NBLK)
                link(dve.tensor_scalar(kp[:, :], a[:, :], pj[:, KA_:KA_ + 1], omka[:, 0:1], ALU.mult, ALU.add))
                link(dve.tensor_tensor(kp[:, :], k[:, :], kp[:, :], ALU.mult))
                dve.scalar_tensor_tensor(out=rk[:, :], in0=r[:, :], scalar=pj[:, RK_:RK_ + 1], in1=kp[:, :],
                                         op0=ALU.mult, op1=ALU.mult).then_inc(q["rkr"], 1)
                dve.wait_ge(q["mm_free"], NBLK + j * 3 * NBLK + 3 * NBLK)
                link(dve.tensor_scalar(t2[:, :], t2[:, :], 1e-12, None, ALU.max))
                link(dve.reciprocal(t2[:, :], t2[:, :]))
                link(dve.scalar_tensor_tensor(out=kk[:, :], in0=k[:, :], scalar=pj[:, KK_:KK_ + 1], in1=t2[:, :],
                                              op0=ALU.mult, op1=ALU.mult))
                link(dve.tensor_tensor(ka[:, :], kk[:, :], a[:, :], ALU.mult))
                dve.sem_inc(q["kkp"], 1)
                dve.wait_ge(q["exps"], 5 * j + 5)
                dve.tensor_copy(vec[:, S_R, :], r[:, SEQ:COLS])
                link(dve.tensor_copy(vec[:, S_W, :], ep[:, SEQ:COLS]))
                dve.sem_inc(q["kkp"], 1)
                dve.scalar_tensor_tensor(out=t3[:, :], in0=kk[:, :], scalar=-1.0, in1=t3[:, :],
                                         op0=ALU.mult, op1=ALU.mult).then_inc(q["dout"], 1)
                dve.tensor_tensor(t1[:, :], ka[:, :], en[:, :], ALU.mult).then_inc(q["dout"], 1)
                dve.wait_ge(q["dout"], 4 * j + 2)
                dve.tensor_copy(vec[:, S_B, :], ka[:, SEQ:COLS])
                dve.tensor_copy(vec[:, S_K, :], kp[:, SEQ:COLS])
                dve.tensor_copy(vec[:, S_A, :], t3[:, SEQ:COLS])
                dve.tensor_copy(vec[:, S_V, :], v[:, SEQ:COLS]).then_inc(q["vecs"], 1)
                dve.wait_ge(q["vecs"], j + 1)
                dve.tensor_tensor(ka[:, :], ka[:, :], ec[:, :], ALU.mult).then_inc(q["dout"], 1)
                for b, (at, width) in enumerate(blocks):
                    dve.wait_ge(q["bmm"], j * NBLK + b + 1)
                    cp = dve.tensor_tensor(ld[:, at:at + width], acb[:, b % 2, 0:width], v[:, at:at + width],
                                           ALU.mult)
                    if b < NBLK - 1:
                        cp.then_inc(q["bfree"], 1)
                    else:
                        cp.then_inc(q["dout"], 1)
                dve.wait_ge(q["dout"], 4 * j + 4)
                dve.sem_inc(q["bfree"], 1)
                assert link.n == K, link.n

        @block.gpsimd
        def _(pool):
            with pool.Fori(0, 4) as j:
                pool.wait_ge(q["zin"], 144 * j + 144)
                for t, d in ((r, t1), (k, t2), (v, t3)):
                    pool.tensor_tensor(d[:, 1:COLS], d[:, 1:COLS], t[:, 1:COLS], ALU.subtract)
                    pool.tensor_scalar(d[:, 0:1], t[:, 0:1], -1.0, None, ALU.mult).then_inc(q["pool_d"], 1)
                pool.wait_ge(q["rkv"], 3 * j + 3)
                pool.wait_ge(q["scan"], j + 1)
                pool.tensor_tensor(t3[:, :], c[:, :], ld[:, :], ALU.subtract).then_inc(q["pool_cw"], 1)
                pool.wait_ge(q["kkp"], 2 * j + 2)
                pool.tensor_tensor(ep[:, :], r[:, :], ep[:, :], ALU.mult).then_inc(q["pout"], 1)
                pool.wait_ge(q["dout"], 4 * j + 2)
                pool.tensor_tensor(en[:, :], kp[:, :], en[:, :], ALU.mult).then_inc(q["pout"], 1)
                pool.wait_ge(q["dout"], 4 * j + 3)
                pool.tensor_tensor(ec[:, :], kp[:, :], ec[:, :], ALU.mult).then_inc(q["pout"], 1)


LEVELS = 5


def rwkv_chunks(nc, ops, wc, const, y, s_out):
    COUNT = dict(ops_in=32, m4_pe=4, m4=4, tm_pe=4, tm=4, ct=LEVELS, xt_sb=LEVELS + 1, xt_pe=LEVELS,
                 x_pe=LEVELS, x_sb=LEVELS, u_pe=LEVELS, u_sb=LEVELS, w_pe=1, w_sb=1, gh_pe=2, gh_sb=2,
                 g5_pe=2, rp=2, mt=4, y_pe=1, s_pe=1, y_sb=1, y_st=16, own=1)
    with Stage(nc, "rc") as s:
        two = lambda n, shape: [s.sb(f"{n}{q}", shape) for q in (0, 1)]
        opx = two("opx", [P, 7, 4, P])
        m4 = two("m4", [P, 4, 4, P])
        aw = two("aw", [P, 4, 2, P])
        vbk = two("vbk", [P, 4, 3, P])
        ct = two("ct", [P, LEVELS, 4, P])
        xt = two("xt", [P, 2, 4, P])
        xx = two("xx", [P, 4, P])
        uu = two("uu", [P, 4, P])
        gh = two("gh", [P, 4, 2, P])
        rpt = two("rpt", [P, 4, P])
        mt = two("mt", [P, 4, P])
        yb = two("yb", [P, 4, CH])
        st = two("st", [P, 4, P])
        mask4 = s.sb("mask4", [P, 4 * P])
        lev = s.sb("lev", [P, 6, P])
        idt = s.sb("id", [P, P])
        wct = s.sb("wc", [P, 4, NCH])
        bank = [[s.ps(f"bank{q}{n}", [P, 512]) for n in range(4)] for q in (0, 1)]
        sem = {n: [s.sem(f"{n}{q}") for q in (0, 1)] for n in COUNT}
        cst, zero, s_sb, s_st = s.sem("cst"), s.sem("zero"), s.sem("s_sb"), s.sem("s_st")
        block = s.block()

        def wait(eng, name, q, m, k):
            eng.wait_ge(sem[name][q], m * COUNT[name] + k)

        four = lambda ap: ap.rearrange("p (j c) -> p j c", j=4)
        every = lambda ap, n: ap.rearrange("p (o c) -> p o c", o=1).broadcast_to([P, n, P])

        @block.sync
        def _(sp):
            for dst, src in ((mask4[:, :], const["mask4"]), (lev[:, :, :], const["levels"]),
                             (idt[:, :], const["ident"]), (wct[:, :, :], wc)):
                sp.dma_start(dst, src).then_inc(cst, 16)
            sp.wait_ge(zero, 4)
            with sp.Fori(0, NCH // 2) as m:
                for q in (0, 1):
                    wait(sp, "mt", q, m, 0)
                    for h in (0, 1):
                        r = slice(64 * h, 64 * h + 64)
                        sp.dma_start(opx[q][r, :, :, r].rearrange("p n j c -> p (n j) c"),
                                     ops[r, :, :, ds((m * 2 + q) * CH, CH)].rearrange("p n j c -> p (n j) c")
                                     ).then_inc(sem["ops_in"][q], 16)
            sp.wait_ge(s_sb, NCH + 1)
            for h in (0, 1):
                r = slice(64 * h, 64 * h + 64)
                sp.dma_start(s_out[:, h].rearrange("j k v -> k j v"), st[0][r, :, r]).then_inc(s_st, 16)
            sp.wait_ge(s_st, 32)

        @block.tensor
        def _(pe):
            pe.wait_ge(cst, 64)
            with pe.Fori(0, NCH // 2) as m:
                for q in (0, 1):
                    wait(pe, "ops_in", q, m, 32)
                    wait(pe, "y_sb", q, m, 0)
                    wait(pe, "rp", q, m, 0)
                    wait(pe, "mt", q, m, 0)
                    pe.wait_ge(s_sb, m * 2 + q)
                    for j in range(4):
                        ar = opx[q][:, A_T:R_T + 1, j, :]
                        pe.matmul(bank[q][j][:, 0:256], opx[q][:, B_T, j, :], ar, start=True, stop=True)
                        pe.matmul(bank[q][j][:, 256:512], opx[q][:, K_T, j, :], ar, start=True,
                                  stop=True).then_inc(sem["m4_pe"][q], 1)
                for q in (0, 1):
                    for j in range(4):
                        wait(pe, "m4", q, m, j + 1)
                        for n, o in enumerate((A_T, V_, B_H, K_H)):
                            mm = pe.transpose(bank[q][j][:, n * P:(n + 1) * P], opx[q][:, o, j, :], idt[:, :])
                        mm.then_inc(sem["tm_pe"][q], 1)
                for q in (0, 1):
                    wait(pe, "xt_sb", q, m, 1)
                    wait(pe, "tm", q, m, 4)
                    for j in range(4):
                        mm = pe.transpose(bank[q][0][:, j * P:(j + 1) * P], xt[q][:, 0, j, :], idt[:, :])
                    mm.then_inc(sem["x_pe"][q], 1)
                    for j in range(4):
                        mm = pe.matmul(bank[q][3][:, j * P:(j + 1) * P], m4[q][:, j, 2, :], vbk[q][:, j, 0, :],
                                       start=True, stop=True)
                    mm.then_inc(sem["w_pe"][q], 1)
                for n in range(LEVELS):
                    for q in (0, 1):
                        wait(pe, "x_sb", q, m, n + 1)
                        wait(pe, "ct", q, m, n + 1)
                        for j in range(4):
                            mm = pe.matmul(bank[q][0][:, j * P:(j + 1) * P], ct[q][:, n, j, :], xx[q][:, j, :],
                                           start=True, stop=True)
                        mm.then_inc(sem["u_pe"][q], 1)
                    for q in (0, 1):
                        wait(pe, "u_sb", q, m, n + 1)
                        wait(pe, "xt_sb", q, m, n + 1)
                        for j in range(4):
                            mm = pe.matmul(bank[q][2][:, j * P:(j + 1) * P], uu[q][:, j, :], xt[q][:, n % 2, j, :],
                                           start=True, stop=True)
                        mm.then_inc(sem["xt_pe"][q], 1)
                        if n < LEVELS - 1:
                            for j in range(4):
                                mm = pe.matmul(bank[q][1][:, j * P:(j + 1) * P], xt[q][:, n % 2, j, :],
                                               uu[q][:, j, :], start=True, stop=True)
                            mm.then_inc(sem["x_pe"][q], 1)
                for q in (0, 1):
                    wait(pe, "xt_sb", q, m, LEVELS + 1)
                    wait(pe, "w_sb", q, m, 1)
                    for j in range(4):
                        mm = pe.matmul(bank[q][j // 2][:, (j % 2) * 256:(j % 2) * 256 + 256],
                                       xt[q][:, LEVELS % 2, j, :], aw[q][:, j, :, :], start=True, stop=True)
                        if j % 2:
                            mm.then_inc(sem["gh_pe"][q], 1)
                for q in (0, 1):
                    for j in range(4):
                        wait(pe, "gh_sb", q, m, j // 2 + 1)
                        at = (j % 2) * 256
                        pe.matmul(bank[q][2 + j // 2][:, at:at + P], gh[q][:, j, 0, :], m4[q][:, j, 1, :],
                                  start=True, stop=True)
                        mm = pe.matmul(bank[q][2 + j // 2][:, at + P:at + 2 * P], gh[q][:, j, 0, :],
                                       vbk[q][:, j, 1, :], start=True, stop=True)
                        if j % 2:
                            mm.then_inc(sem["g5_pe"][q], 1)
                for q in (0, 1):
                    wait(pe, "rp", q, m, 2)
                    wait(pe, "mt", q, m, 4)
                    pe.wait_ge(s_sb, m * 2 + q + 1)
                    for j in range(4):
                        o = bank[q][1][:, j * P:(j + 1) * P]
                        pe.matmul(o, vbk[q][:, j, 1, :], gh[q][:, j, 1, :], start=True, stop=False)
                        pe.matmul(o, vbk[q][:, j, 2, :], vbk[q][:, j, 0, :], start=False, stop=False)
                        mm = pe.matmul(o, mt[q][:, j, :], st[q][:, j, :], start=False, stop=True)
                    mm.then_inc(sem["s_pe"][q], 1)
                    for j in range(4):
                        o = bank[q][0][:, j * P:(j + 1) * P]
                        pe.matmul(o, gh[q][:, j, 1, :], m4[q][:, j, 1, :], start=True, stop=False)
                        pe.matmul(o, vbk[q][:, j, 0, :], m4[q][:, j, 3, :], start=False, stop=False)
                        mm = pe.matmul(o, st[q][:, j, :], rpt[q][:, j, :], start=False, stop=True)
                    mm.then_inc(sem["y_pe"][q], 1)

        @block.scalar
        def _(act):
            with act.Fori(0, NCH // 2) as m:
                for q in (0, 1):
                    wait(act, "y_pe", q, m, 0)
                    for j in range(4):
                        wait(act, "tm_pe", q, m, j + 1)
                        act.copy(aw[q][:, j, 0, :], bank[q][j][:, 0:P])
                        act.copy(vbk[q][:, j].rearrange("p n c -> p (n c)"),
                                 bank[q][j][:, P:4 * P]).then_inc(sem["tm"][q], 1)
                for q in (0, 1):
                    wait(act, "w_pe", q, m, 1)
                    act.copy(aw[q][:, :, 1, :], four(bank[q][3][:, :])).then_inc(sem["w_sb"][q], 1)
                for n in range(LEVELS):
                    for q in (0, 1):
                        wait(act, "u_pe", q, m, n + 1)
                        act.copy(uu[q][:, :, :], four(bank[q][0][:, :])).then_inc(sem["u_sb"][q], 1)
                for q in (0, 1):
                    for h in (0, 1):
                        wait(act, "gh_pe", q, m, h + 1)
                        act.copy(gh[q][:, 2 * h:2 * h + 2].rearrange("p j n c -> p (j n c)"),
                                 bank[q][h][:, :]).then_inc(sem["gh_sb"][q], 1)
                for q in (0, 1):
                    wait(act, "y_pe", q, m, 1)
                    wait(act, "y_st", q, m, 0)
                    act.copy(yb[q][0:64, :, :], four(bank[q][0][0:64, :])[:, :, 0:64])
                    act.copy(yb[q][64:128, :, :], four(bank[q][0][64:128, :])[:, :, 64:128]
                             ).then_inc(sem["y_sb"][q], 1)
                    wait(act, "y_sb", q, m, 1)
                    act.dma_start(y[:, :, ds((m * 2 + q) * CH, CH)], yb[q][:, :, :]).then_inc(sem["y_st"][q], 16)
            for q in (0, 1):
                act.wait_ge(sem["y_st"][q], 16 * NCH // 2)

        @block.vector
        def _(dve):
            dve.memset(opx[0][:, :, :, :], 0.0).then_inc(zero, 1)
            dve.memset(opx[1][:, :, :, :], 0.0).then_inc(zero, 1)
            dve.memset(st[1][:, :, :], 0.0).then_inc(zero, 1)
            dve.memset(st[0][:, :, :], 0.0).then_inc(zero, 1)
            dve.wait_ge(zero, 4)
            dve.sem_inc(s_sb, 1)
            dve.wait_ge(cst, 64)
            with dve.Fori(0, NCH // 2) as m:
                for q in (0, 1):
                    wait(dve, "y_pe", q, m, 0)
                    for j in range(4):
                        wait(dve, "m4_pe", q, m, j + 1)
                        dve.tensor_tensor(m4[q][:, j].rearrange("p n c -> p (n c)"), bank[q][j][:, :],
                                          mask4[:, :], ALU.mult).then_inc(sem["m4"][q], 1)
                for q in (0, 1):
                    wait(dve, "m4", q, m, 4)
                    dve.tensor_tensor(xt[q][:, 0], m4[q][:, :, 0, :], every(lev[:, 0, :], 4),
                                      ALU.mult).then_inc(sem["own"][q], 1)
                    wait(dve, "own", q, m, 1)
                    dve.tensor_tensor(xt[q][:, 0], xt[q][:, 0], every(idt[:, :], 4),
                                      ALU.add).then_inc(sem["xt_sb"][q], 1)
                for q in (0, 1):
                    wait(dve, "x_pe", q, m, 1)
                    dve.tensor_copy(xx[q][:, :, :], four(bank[q][0][:, :])).then_inc(sem["x_sb"][q], 1)
                for n in range(LEVELS):
                    for q in (0, 1):
                        wait(dve, "xt_pe", q, m, n + 1)
                        wait(dve, "xt_sb", q, m, n + 1)
                        dve.tensor_tensor(xt[q][:, (n + 1) % 2], xt[q][:, n % 2], four(bank[q][2][:, :]),
                                          ALU.add).then_inc(sem["xt_sb"][q], 1)
                        if n < LEVELS - 1:
                            wait(dve, "x_pe", q, m, n + 2)
                            wait(dve, "x_sb", q, m, n + 1)
                            dve.tensor_tensor(xx[q][:, :, :], xx[q][:, :, :], four(bank[q][1][:, :]),
                                              ALU.add).then_inc(sem["x_sb"][q], 1)
                for q in (0, 1):
                    for h in (0, 1):
                        wait(dve, "g5_pe", q, m, h + 1)
                        b = bank[q][2 + h][:, :].rearrange("p (j n c) -> p j n c", j=2, n=2)
                        dve.tensor_tensor(rpt[q][:, 2 * h:2 * h + 2, :], opx[q][:, R_T, 2 * h:2 * h + 2, :],
                                          b[:, :, 0, :], ALU.add).then_inc(sem["rp"][q], 1)
                        for j in (0, 1):
                            dve.scalar_tensor_tensor(
                                out=mt[q][:, 2 * h + j, :], in0=idt[:, :],
                                scalar=wct[:, 2 * h + j, ds(m * 2 + q, 1)], in1=b[:, j, 1, :],
                                op0=ALU.mult, op1=ALU.add).then_inc(sem["mt"][q], 1)
                for q in (0, 1):
                    wait(dve, "s_pe", q, m, 1)
                    wait(dve, "y_pe", 1 - q, m, q)
                    dve.tensor_copy(st[1 - q][:, :, :], four(bank[q][1][:, :])).then_inc(s_sb, 1)

        @block.gpsimd
        def _(pool):
            pool.wait_ge(cst, 64)
            with pool.Fori(0, NCH // 2) as m:
                for q in (0, 1):
                    wait(pool, "m4", q, m, 4)
                    wait(pool, "gh_pe", q, m, 0)
                    for n in range(LEVELS):
                        pool.tensor_tensor(ct[q][:, n], m4[q][:, :, 0, :], every(lev[:, n + 1, :], 4),
                                           ALU.mult).then_inc(sem["ct"][q], 1)


def rwkv_samples(nc, vecs, state, ident, state_out, y):
    BH = NS * 8
    with Stage(nc, "rs") as s:
        S = s.sb("S", [BH, 64, 64])
        T = s.sb("T", [BH, 64, 64])
        vt = s.sb("vec", [BH, 6, 64])
        sa, yt = s.sb("sa", [BH, 64]), s.sb("yt", [BH, 64])
        yc = s.sb("yc", [P, 4, NS])
        idt = s.sb("id", [P, P])
        tr = s.ps("tr", [P, 512])
        ready, own, out, y_done, tr_done, yc_done = (s.sem(n) for n in ("ready", "own", "out", "y_done", "tr", "yc"))
        block = s.block()

        @block.sync
        def _(sp):
            sp.dma_start(S[:, :, :], state).then_inc(ready, 16)
            sp.dma_start(idt[:, :], ident).then_inc(ready, 16)
            sp.dma_start(vt[:, :, :], vecs.rearrange("n b (h c) -> (b h) n c", c=64)).then_inc(ready, 16)
            sp.wait_ge(own, 7)
            sp.dma_start(state_out, S[:, :, :]).then_inc(out, 16)
            sp.wait_ge(yc_done, 2)
            sp.dma_start(y[:, :, SEQ:COLS], yc[:, :, :]).then_inc(out, 16)
            sp.wait_ge(out, 32)

        @block.vector
        def _(dve):
            link = Chain(dve, own)
            row = lambda n: vt[:, n:n + 1, :].broadcast_to([BH, 64, 64])
            col = lambda ap: ap.rearrange("p (v o) -> p v o", o=1).broadcast_to([BH, 64, 64])
            dve.wait_ge(ready, 48)
            link(dve.tensor_tensor(T[:, :, :], S[:, :, :], row(S_A), ALU.mult))
            link(dve.tensor_reduce(sa[:, :], T[:, :, :], AX.X, ALU.add))
            link(dve.tensor_tensor(S[:, :, :], S[:, :, :], row(S_W), ALU.mult))
            link(dve.tensor_tensor(T[:, :, :], col(sa[:, :]), row(S_B), ALU.mult))
            link(dve.tensor_tensor(S[:, :, :], S[:, :, :], T[:, :, :], ALU.add))
            link(dve.tensor_tensor(T[:, :, :], col(vt[:, S_V, :]), row(S_K), ALU.mult))
            link(dve.tensor_tensor(S[:, :, :], S[:, :, :], T[:, :, :], ALU.add))
            link(dve.tensor_tensor(T[:, :, :], S[:, :, :], row(S_R), ALU.mult))
            dve.tensor_reduce(yt[:, :], T[:, :, :], AX.X, ALU.add).then_inc(y_done, 1)
            dve.wait_ge(tr_done, 1)
            for h in (0, 1):
                src = tr[0:64, 0:BH].rearrange("v (b j h) -> v h j b", j=4, h=2)[:, h]
                dve.tensor_copy(yc[64 * h:64 * h + 64, :, :], src).then_inc(yc_done, 1)

        @block.tensor
        def _(pe):
            pe.wait_ge(ready, 48)
            pe.wait_ge(y_done, 1)
            pe.transpose(tr[0:64, 0:BH], yt[:, :], idt[0:BH, 0:BH]).then_inc(tr_done, 1)


def rwkv_output(nc, y, bonus, gate, prm, ones, cat):
    with Stage(nc, "ro") as s:
        two = lambda n: [s.sb(f"{n}{q}", [P, COLS]) for q in (0, 1)]
        yt, bt, gt, sq, rs = two("y"), two("b"), two("g"), two("sq"), two("rs")
        pr = s.sb("prm", [P, 4, 10])
        on = s.sb("ones", [P, P])
        acc = s.ps("acc", [P, NBLK, 512])
        cst = s.sem("cst")
        names = ("in", "mm", "mu", "sq", "lnv", "rstd", "gate", "own", "out", "stored", "biased")
        sem = {n: [s.sem(f"{n}{q}") for q in (0, 1)] for n in names}
        free = s.sem("free")
        blocks = [(b * BLK, min(BLK, COLS - b * BLK)) for b in range(NBLK)]
        block = s.block()
        eps = s.sb("eps", [P, 1])
        eps_set = s.sem("eps_set")

        @block.sync
        def _(sp):
            sp.dma_start(pr[:, :, :], prm).then_inc(cst, 16)
            sp.dma_start(on[:, :], ones).then_inc(cst, 16)
            for j in range(4):
                q, m = j % 2, j // 2
                sp.wait_ge(sem["stored"][q], 16 * m)
                for t, src in ((yt, y[:, j, :]), (bt, bonus[j]), (gt, gate[j])):
                    sp.dma_start(t[q][:, :], src).then_inc(sem["in"][q], 16)

        @block.tensor
        def _(pe):
            pe.wait_ge(cst, 32)
            for j in range(4):
                q, m = j % 2, j // 2
                for n, (x, ready, count) in enumerate(((yt, "in", 48), (sq, "sq", 1))):
                    pe.wait_ge(sem[ready][q], count * (m + 1))
                    for b, (at, width) in enumerate(blocks):
                        if j or n:
                            pe.wait_ge(free, (2 * j + n - 1) * NBLK + b + 1)
                        pe.matmul(acc[:, b, 0:width], on[:, :], x[q][:, at:at + width], start=True,
                                  stop=True).then_inc(sem["mm"][q], 1)

        @block.vector
        def _(dve):
            dve.memset(eps[:, :], GN_EPS).then_inc(eps_set, 1)
            dve.wait_ge(cst, 32)
            for j in range(4):
                q, m = j % 2, j // 2
                pj = lambda n: pr[:, j, n:n + 1]
                dve.wait_ge(sem["in"][q], 48 * (m + 1))
                for b, (at, width) in enumerate(blocks):
                    dve.wait_ge(sem["mm"][q], m * 2 * NBLK + b + 1)
                    dve.scalar_tensor_tensor(out=yt[q][:, at:at + width], in0=acc[:, b, 0:width], scalar=-1.0 / 64,
                                             in1=yt[q][:, at:at + width], op0=ALU.mult,
                                             op1=ALU.add).then_inc(free, 1)
                dve.wait_ge(sem["rstd"][q], m + 1)
                dve.tensor_tensor(yt[q][:, :], yt[q][:, :], rs[q][:, :], ALU.mult).then_inc(sem["own"][q], 1)
                dve.wait_ge(sem["own"][q], 2 * m + 1)
                dve.tensor_scalar(yt[q][:, :], yt[q][:, :], pj(GN_G), pj(GN_B), ALU.mult,
                                  ALU.add).then_inc(sem["own"][q], 1)
                dve.wait_ge(sem["biased"][q], m + 1)
                dve.wait_ge(sem["gate"][q], m + 1)
                dve.tensor_tensor(yt[q][:, :], yt[q][:, :], gt[q][:, :], ALU.mult).then_inc(sem["out"][q], 1)

        @block.gpsimd
        def _(pool):
            for j in range(4):
                q, m = j % 2, j // 2
                pool.wait_ge(sem["own"][q], 2 * m + 2)
                pool.tensor_tensor(yt[q][:, :], yt[q][:, :], bt[q][:, :], ALU.add).then_inc(sem["biased"][q], 1)

        @block.scalar
        def _(act):
            act.wait_ge(eps_set, 1)
            for j in range(4):
                q, m = j % 2, j // 2
                act.wait_ge(sem["in"][q], 48 * (m + 1))
                act.activation(gt[q][:, :], gt[q][:, :], ACT.Silu).then_inc(sem["gate"][q], 1)
                act.wait_ge(free, 2 * j * NBLK + NBLK)
                act.activation(sq[q][:, :], yt[q][:, :], ACT.Square).then_inc(sem["sq"][q], 1)
                act.preload_act_table_set(LN_EXP)
                for b, (at, width) in enumerate(blocks):
                    act.wait_ge(sem["mm"][q], m * 2 * NBLK + NBLK + b + 1)
                    act.activation(rs[q][:, at:at + width], acc[:, b, 0:width], ACT.Ln, scale=1.0 / 64,
                                   bias=eps[:, 0:1]).then_inc(free, 1)
                act.wait_ge(free, 2 * (j + 1) * NBLK)
                act.activation(rs[q][:, :], rs[q][:, :], ACT.Exp, scale=-0.5).then_inc(sem["rstd"][q], 1)
                act.wait_ge(sem["out"][q], m + 1)
                act.dma_start(cat[j], yt[q][:, :]).then_inc(sem["stored"][q], 16)
            for q in (0, 1):
                act.wait_ge(sem["stored"][q], 32)


G, SP_, GC = 32, 64, 16
T8 = 8
NC8 = SEQ // T8
TWO_PI = (6.28125, 1.93500518798828125e-3, 3.0199159819e-7)
ROUND = 1.5 * 2.0 ** 23


def s5_prompt(nc, u, par, mats, dcol, const, yT, fin, kept_l, kept_m,
              kept_a):
    with Stage(nc, "s5") as s:
        ut = s.sb("u", [P, 2, T8, 512])
        co, si = s.sb("cos", [P, G, NC8]), s.sb("sin", [P, G, NC8])
        L = s.sb("L", [P, G, T8, GC])
        D1, D2 = s.sb("D1", [P, G, T8, GC]), s.sb("D2", [P, G, T8, GC])
        jl = s.sb("jl", [P, 2, G, GC])
        tmp = s.sb("tmp", [P, 2, G, GC])
        m1, m2 = s.sb("m1", [P, G, GC]), s.sb("m2", [P, G, GC])
        pt = s.sb("par", [P, 3, G])
        raw = s.sb("raw", [P, 2, G, GC])
        sc = s.sb("sc", [P, 24, G])
        dc = s.sb("dcol", [P, G])
        sg = s.sb("sgn", [P, 1])
        idt, jm = s.sb("id", [P, P]), s.sb("jm", [P, P])
        lx = [s.sb(f"lx{q}", [P, 15, GC]) for q in (0, 1)]
        xg = [s.sb(f"xg{q}", [P, 2, T8, GC]) for q in (0, 1)]
        xT = [s.sb(f"xT{q}", [P, NC8]) for q in (0, 1)]
        tp = [s.sb(f"tp{q}", [P, P]) for q in (0, 1)]
        bi = [s.sb(f"bi{q}", [P, 2, P]) for q in (0, 1)]
        xr = [s.sb(f"xr{q}", [P, 2, NC8]) for q in (0, 1)]
        gs = [s.sb(f"gs{q}", [P, NC8]) for q in (0, 1)]
        hc = [s.sb(f"hc{q}", [P, NC8]) for q in (0, 1)]
        hs = [s.sb(f"hs{q}", [P, NC8]) for q in (0, 1)]
        gl = s.sb("glast", [P, G])
        fo = s.sb("fo", [P, 4, G])
        ye = co[:, :, :].rearrange("p g n -> p (g n)").rearrange("p (k c) -> p k c", k=4)
        bk = [[s.ps(f"bk{q}{n}", [P, 512]) for n in range(4)] for q in (0, 1)]
        COUNT = dict(cp=1, cpl=1, xT_pe=1, tb_pe=1, tb=2, xT=1, x_pe=1, rot=1, scan=1, hc=1, hs=1, y_pe=1, y=1, own=1)
        sem = {n: [s.sem(f"{n}{q}") for q in (0, 1)] for n in COUNT}
        (cst, u_in, own, pown, angles, trig, tab_v, tab_p, mats_v, mats_p, zed, act0, ftr, fout, gel, ytr, yev,
         kst, flast, held) = (s.sem(n) for n in (
             "cst", "u_in", "own", "pown", "angles", "trig", "tab_v", "tab_p", "mats_v", "mats_p", "zed", "act0",
             "ftr", "fout", "gel", "ytr", "yev", "kst", "flast", "held"))
        block = s.block()
        c_ = lambda n: sc[:, n, :]
        (DT, MAG, TH, KR, R_, SI, SH, CO, AR, AI, DEN, FR, FI, NR, X0, X1, PC, PS, PC2, PS2, RHO, X2, X3, X4) = range(24)
        gb = lambda ap: ap.rearrange("p (g o) -> p g o", o=1).broadcast_to([P, G, GC])

        def wait(eng, name, q, m, k):
            eng.wait_ge(sem[name][q], m * COUNT[name] + k)

        @block.sync
        def _(sp):
            for dst, src in ((pt[:, :, :], par), (raw[:, :, :, :], mats[:, 0:2]), (m1[:, :, :], mats[:, 2]),
                             (m2[:, :, :], mats[:, 3]), (dc[:, :], dcol), (sg[:, :], const["sgn"]),
                             (idt[:, :], const["ident"]), (jm[:, :], const["jm"])):
                sp.dma_start(dst, src).then_inc(cst, 16)
            sp.dma_start(ut[:, :, :, :].rearrange("p b s c -> p (b s) c"),
                         u[0:TT].rearrange("t p c -> p t c")).then_inc(u_in, 16)
            sp.wait_ge(mats_v, 1)
            for dst, src in ((kept_l, L[:, :, T8 - 1, :]), (kept_m, m1[:, :, :]), (kept_a, sc[:, AR:AI + 1, :])):
                sp.dma_start(dst, src).then_inc(kst, 16)
            sp.wait_ge(fout, 1)
            sp.dma_start(fin, fo[:, 3, :]).then_inc(kst, 16)
            sp.wait_ge(yev, 2 * T8)
            sp.dma_start(yT[:, :, 0:SEQ], ye).then_inc(kst, 16)
            sp.wait_ge(kst, 80)

        @block.scalar
        def _(act):
            act.wait_ge(cst, 128)
            act.activation(c_(DT), pt[:, 2, :], ACT.Exp).then_inc(act0, 1)
            act.wait_ge(angles, 1)
            act.activation(c_(MAG), c_(X0), ACT.Exp)
            act.activation(c_(RHO), c_(X0), ACT.Exp, scale=float(T8)).then_inc(act0, 1)
            act.wait_ge(angles, 2)
            act.activation(c_(SI), c_(R_), ACT.Sin)
            act.activation(c_(SH), c_(R_), ACT.Sin, scale=0.5).then_inc(act0, 1)
            act.wait_ge(u_in, 16)
            with act.Fori(0, G // 2) as m:
                for q in (0, 1):
                    g = m * 2 + q
                    wait(act, "xT_pe", q, m, 0)
                    act.sem_inc(held, 1)
                    act.copy(xg[q][:, :, :, :].rearrange("p b s c -> p (b s) c"),
                             ut[:, :, :, ds(g * GC, GC)].rearrange("p b s c -> p (b s) c")
                             ).then_inc(sem["cp"][q], 1)
                for q in (0, 1):
                    wait(act, "tb_pe", q, m, 1)
                    wait(act, "y_pe", q, m, 0)
                    act.copy(xT[q][:, :], bk[q][0][:, 0:NC8]).then_inc(sem["xT"][q], 1)
                    act.copy(bi[q][:, :, :].rearrange("p a c -> p (a c)"), bk[q][0][:, NC8:2 * NC8]
                             ).then_inc(sem["tb"][q], 1)
                for q in (0, 1):
                    g = m * 2 + q
                    wait(act, "y_pe", q, m, 1)
                    act.sem_inc(held, 1)
                    act.copy(ut[:, :, :, ds(g * GC, GC)].rearrange("p b s c -> p (b s) c"),
                             bk[q][3][:, 0:2 * P].rearrange("p (n c) -> p n c", c=GC)).then_inc(sem["y"][q], 1)
            for q in (0, 1):
                act.wait_ge(sem["y"][q], G // 2)
            for b in (0, 1):
                act.activation(ut[:, b].rearrange("p s c -> p (s c)"), ut[:, b].rearrange("p s c -> p (s c)"),
                               ACT.Gelu_apprx_tanh).then_inc(gel, 1)

        @block.vector
        def _(dve):
            link = Chain(dve, own)
            tt = lambda o, a, b, op: link(dve.tensor_tensor(o, a, b, op))
            ts = lambda o, a, s1, s2, o1, o2=ALU.bypass: link(
                dve.tensor_scalar(o, a, s1, s2, o1, o2) if s2 is not None else dve.tensor_scalar(o, a, s1, None, o1))
            for q in (0, 1):
                dve.memset(lx[q][:, :, :], 0.0).then_inc(zed, 1)
                dve.memset(hc[q][:, :], 0.0).then_inc(zed, 1)
                dve.memset(hs[q][:, :], 0.0).then_inc(zed, 1)
            link(dve.memset(co[:, :, 0:1], 1.0))
            link(dve.memset(si[:, :, 0:1], 0.0))
            dve.wait_ge(cst, 128)
            dve.wait_ge(act0, 1)
            dve.tensor_tensor(c_(X0), pt[:, 0, :], c_(DT), ALU.mult).then_inc(angles, 1)
            tt(c_(TH), pt[:, 1, :], c_(DT), ALU.mult)
            ts(c_(KR), c_(TH), 1.0 / (2 * np.pi), None, ALU.mult)
            ts(c_(KR), c_(KR), ROUND, None, ALU.add)
            ts(c_(KR), c_(KR), -ROUND, None, ALU.add)
            for part in TWO_PI:
                src = c_(TH) if part == TWO_PI[0] else c_(R_)
                link(dve.scalar_tensor_tensor(out=c_(R_), in0=c_(KR), scalar=-part, in1=src, op0=ALU.mult,
                                              op1=ALU.add))
            ts(c_(R_), c_(R_), 3.1415925, -3.1415925, ALU.min, ALU.max)
            dve.sem_inc(angles, 1)
            dve.wait_ge(act0, 3)
            tt(c_(CO), c_(SH), c_(SH), ALU.mult)
            ts(c_(CO), c_(CO), -2.0, 1.0, ALU.mult, ALU.add)
            tt(c_(AR), c_(MAG), c_(CO), ALU.mult)
            tt(c_(AI), c_(MAG), c_(SI), ALU.mult)
            pc, ps = CO, SI
            for _n in range(3):
                tt(c_(X1), c_(pc), c_(pc), ALU.mult)
                tt(c_(X2), c_(ps), c_(ps), ALU.mult)
                tt(c_(X3), c_(pc), c_(ps), ALU.mult)
                tt(c_(PC), c_(X1), c_(X2), ALU.subtract)
                ts(c_(PS), c_(X3), 2.0, None, ALU.mult)
                pc, ps = PC, PS
            for n in range(8):
                w = 1 << n
                b = lambda x: c_(x).rearrange("p (g o) -> p g o", o=1).broadcast_to([P, G, w])
                t = D1[:, :, :, :].rearrange("p g s c -> p g (s c)")[:, :, 0:w]
                if n:
                    dve.wait_ge(tab_p, n)
                    tt(c_(X1), c_(PC), c_(PC), ALU.mult)
                    tt(c_(X2), c_(PS), c_(PS), ALU.mult)
                    tt(c_(X3), c_(PC), c_(PS), ALU.mult)
                    tt(c_(PC), c_(X1), c_(X2), ALU.subtract)
                    ts(c_(PS), c_(X3), 2.0, None, ALU.mult)
                dve.sem_inc(tab_v, 1)
                dve.tensor_tensor(co[:, :, w:2 * w], co[:, :, 0:w], b(PC), ALU.mult)
                tt(t, si[:, :, 0:w], b(PS), ALU.mult)
                tt(co[:, :, w:2 * w], co[:, :, w:2 * w], t, ALU.subtract)
            ts(c_(NR), c_(AR), -1.0, None, ALU.add)
            tt(c_(X1), pt[:, 0, :], pt[:, 0, :], ALU.mult)
            tt(c_(X2), pt[:, 1, :], pt[:, 1, :], ALU.mult)
            tt(c_(DEN), c_(X1), c_(X2), ALU.add)
            link(dve.reciprocal(c_(DEN), c_(DEN)))
            tt(c_(X1), c_(NR), pt[:, 0, :], ALU.mult)
            tt(c_(X2), c_(AI), pt[:, 1, :], ALU.mult)
            tt(c_(X1), c_(X1), c_(X2), ALU.add)
            tt(c_(FR), c_(X1), c_(DEN), ALU.mult)
            tt(c_(X1), c_(AI), pt[:, 0, :], ALU.mult)
            tt(c_(X2), c_(NR), pt[:, 1, :], ALU.mult)
            tt(c_(X1), c_(X1), c_(X2), ALU.subtract)
            tt(c_(FI), c_(X1), c_(DEN), ALU.mult)
            link(dve.tensor_scalar(raw[:, 1], raw[:, 1], sg[:, 0:1], None, ALU.mult))
            link(dve.tensor_scalar(m1[:, :, :], m1[:, :, :], sg[:, 0:1], -1.0, ALU.mult, ALU.mult))
            ts(m2[:, :, :], m2[:, :, :], -1.0, None, ALU.mult)

            def turn(re, im, x, jx, ox, ojx):
                dve.tensor_tensor(tmp[:, 0], x, gb(re), ALU.mult)
                tt(tmp[:, 1], jx, gb(im), ALU.mult)
                tt(ox, tmp[:, 0], tmp[:, 1], ALU.add)
                dve.tensor_tensor(tmp[:, 0], jx, gb(re), ALU.mult)
                tt(tmp[:, 1], x, gb(im), ALU.mult)
                tt(ojx, tmp[:, 0], tmp[:, 1], ALU.subtract)
            turn(c_(FR), c_(FI), raw[:, 0], raw[:, 1], L[:, :, 7, :], jl[:, 0])
            for n in range(1, T8):
                turn(c_(AR), c_(AI), L[:, :, 8 - n, :], jl[:, (n - 1) % 2], L[:, :, 7 - n, :], jl[:, n % 2])
            dve.wait_ge(tab_p, 8)
            turn(c_(AR), c_(AI), m1[:, :, :], m2[:, :, :], D1[:, :, 0, :], D2[:, :, 0, :])
            for n in range(1, T8):
                turn(c_(AR), c_(AI), D1[:, :, n - 1, :], D2[:, :, n - 1, :], D1[:, :, n, :], D2[:, :, n, :])
            dve.sem_inc(mats_v, 1)
            with dve.Fori(0, G // 2) as m:
                for q in (0, 1):
                    g = m * 2 + q
                    wait(dve, "tb_pe", q, m, 1)
                    wait(dve, "y_pe", q, m, 0)
                    dve.scalar_tensor_tensor(out=tp[q][:, :], in0=idt[:, :], scalar=dc[:, ds(g, 1)],
                                             in1=bk[q][1][:, 0:P], op0=ALU.mult, op1=ALU.add
                                             ).then_inc(sem["tb"][q], 1)
                for q in (0, 1):
                    g = m * 2 + q
                    tab = lambda t: t[:, ds(g, 1), :].rearrange("p o c -> p (o c)")
                    wait(dve, "x_pe", q, m, 1)
                    dve.tensor_tensor(xr[q][:, 0, :], bk[q][2][:, 0:NC8], tab(co), ALU.mult)
                    dve.tensor_tensor(xr[q][:, 1, :], bk[q][2][:, NC8:2 * NC8], tab(si), ALU.mult
                                      ).then_inc(sem["rot"][q], 1)
                    wait(dve, "rot", q, m, 1)
                    dve.tensor_tensor(xr[q][:, 0, :], xr[q][:, 0, :], xr[q][:, 1, :], ALU.add
                                      ).then_inc(sem["own"][q], 1)
                    wait(dve, "own", q, m, 1)
                    wait(dve, "hs", q, m, 0)
                    dve.tensor_tensor_scan(gs[q][:, :], c_(RHO)[:, ds(g, 1)].broadcast_to([P, NC8]), xr[q][:, 0, :],
                                           0.0, ALU.mult, ALU.add).then_inc(sem["scan"][q], 1)
                    wait(dve, "scan", q, m, 1)
                    wait(dve, "y_pe", q, m, 0)
                    dve.tensor_tensor(hc[q][:, 1:NC8], gs[q][:, 0:NC8 - 1], tab(co)[:, 0:NC8 - 1], ALU.mult)
                    dve.tensor_copy(gl[:, ds(g, 1)], gs[q][:, NC8 - 1:NC8]).then_inc(sem["hc"][q], 1)
            for q in (0, 1):
                dve.wait_ge(sem["hc"][q], G // 2)
            dve.tensor_tensor(fo[:, 0, :], gl[:, :], co[:, :, NC8 - 1], ALU.mult).then_inc(flast, 1)
            dve.tensor_tensor(fo[:, 1, :], gl[:, :], si[:, :, NC8 - 1], ALU.mult).then_inc(flast, 1)
            dve.wait_ge(ftr, 1)
            dve.tensor_tensor(fo[:, 3, :], fo[:, 0, :], bk[0][0][:, 0:G], ALU.subtract).then_inc(fout, 1)
            for n in range(2 * T8):
                b, t = divmod(n, T8)
                dve.wait_ge(ytr, n + 1)
                dve.tensor_copy(ye[:, :, b * SEQ // 2 + t:(b + 1) * SEQ // 2:T8],
                                bk[1][n % 2][:, :].rearrange("p (k c) -> p k c", k=4)).then_inc(yev, 1)

        @block.gpsimd
        def _(pool):
            for n in range(8):
                w = 1 << n
                b = lambda x: c_(x).rearrange("p (g o) -> p g o", o=1).broadcast_to([P, G, w])
                t = D2[:, :, :, :].rearrange("p g s c -> p g (s c)")[:, :, 0:w]
                pool.wait_ge(tab_v, n + 1)
                pool.tensor_tensor(si[:, :, w:2 * w], si[:, :, 0:w], b(PC), ALU.mult).then_inc(pown, 1)
                pool.tensor_tensor(t, co[:, :, 0:w], b(PS), ALU.mult).then_inc(pown, 1)
                pool.wait_ge(pown, 2 * n + 2)
                pool.tensor_tensor(si[:, :, w:2 * w], si[:, :, w:2 * w], t, ALU.add).then_inc(tab_p, 1)
            pool.wait_ge(mats_v, 1)
            pool.wait_ge(zed, 6)
            with pool.Fori(0, G // 2) as m:
                for q in (0, 1):
                    g = m * 2 + q
                    wait(pool, "tb_pe", q, m, 0)
                    pool.tensor_copy(lx[q][:, 0:T8, :], L[:, ds(g, 1), :, :].rearrange("p o s c -> p (o s) c")
                                     ).then_inc(sem["cpl"][q], 1)
                for q in (0, 1):
                    g = m * 2 + q
                    wait(pool, "scan", q, m, 1)
                    wait(pool, "y_pe", q, m, 0)
                    pool.tensor_tensor(hs[q][:, 1:NC8], gs[q][:, 0:NC8 - 1],
                                       si[:, ds(g, 1), 0:NC8 - 1].rearrange("p o c -> p (o c)"),
                                       ALU.mult).then_inc(sem["hs"][q], 1)

        @block.tensor
        def _(pe):
            pe.wait_ge(cst, 128)
            pe.wait_ge(mats_v, 1)
            pe.wait_ge(zed, 6)
            with pe.Fori(0, G // 2) as m:
                for q in (0, 1):
                    g = m * 2 + q
                    wait(pe, "cp", q, m, 1)
                    wait(pe, "xT", q, m, 0)
                    for b in (0, 1):
                        mm = pe.transpose(bk[q][0][:, b * P:(b + 1) * P],
                                          xg[q][:, b].rearrange("p s c -> p (s c)"), idt[:, :])
                    mm.then_inc(sem["xT_pe"][q], 1)
                    wait(pe, "cpl", q, m, 1)
                    wait(pe, "tb", q, m, 0)
                    lf = lx[q][:, :, :].rearrange("p s c -> p (s c)")
                    for t in range(T8):
                        pe.matmul(bk[q][1][:, t * GC:(t + 1) * GC], lf[:, (7 - t) * GC:(7 - t) * GC + P],
                                  m1[:, ds(g, 1), :].rearrange("p o c -> p (o c)"), start=True, stop=True)
                    pe.transpose(bk[q][0][:, NC8:NC8 + P], lf[:, 0:P], idt[:, :])
                    pe.matmul(bk[q][0][:, NC8 + P:2 * NC8], lf[:, 0:P], jm[:, :], start=True,
                              stop=True).then_inc(sem["tb_pe"][q], 1)
                for q in (0, 1):
                    wait(pe, "tb", q, m, 2)
                    wait(pe, "xT", q, m, 1)
                    wait(pe, "rot", q, m, 0)
                    for a in (0, 1):
                        mm = pe.matmul(bk[q][2][:, a * NC8:(a + 1) * NC8], bi[q][:, a, :], xT[q][:, :],
                                       start=True, stop=True)
                    mm.then_inc(sem["x_pe"][q], 1)
                for q in (0, 1):
                    g = m * 2 + q
                    dg = lambda t: t[:, ds(g, 1), :, :].rearrange("p o s c -> p (o s c)")
                    wait(pe, "hc", q, m, 1)
                    wait(pe, "hs", q, m, 1)
                    wait(pe, "y", q, m, 0)
                    for b in (0, 1):
                        o = bk[q][3][:, b * P:(b + 1) * P]
                        r = slice(b * P, (b + 1) * P)
                        pe.matmul(o, xT[q][:, r], tp[q][:, :], start=True, stop=False)
                        pe.matmul(o, hc[q][:, r], dg(D1), start=False, stop=False)
                        mm = pe.matmul(o, hs[q][:, r], dg(D2), start=False, stop=True)
                    mm.then_inc(sem["y_pe"][q], 1)
            pe.wait_ge(flast, 2)
            pe.matmul(bk[0][0][:, 0:G], jm[:, :], fo[:, 1, :], start=True, stop=True).then_inc(ftr, 1)
            for n in range(2 * T8):
                b, t = divmod(n, T8)
                pe.wait_ge(gel, b + 1)
                if n > 1:
                    pe.wait_ge(yev, n - 1)
                for k in range(4):
                    mm = pe.transpose(bk[1][n % 2][:, k * P:(k + 1) * P], ut[:, b, t, k * P:(k + 1) * P], idt[:, :])
                mm.then_inc(ytr, 1)


def s5_samples(nc, u, par, h_in, kept_l, kept_m, kept_a, d_row, const, yT, h_out):
    with Stage(nc, "ss") as s:
        ub = s.sb("u", [P, NS, G, GC])
        t = s.sb("t", [P, NS, G, GC])
        lt, mt, at = s.sb("l", [P, G, GC]), s.sb("m", [P, G, GC]), s.sb("a", [P, 2, G])
        h = s.sb("h", [P, 2, NS, G])
        bu, w = s.sb("bu", [P, NS, G]), s.sb("w", [P, NS, G])
        hn = s.sb("hn", [P, NS, G])
        ur, dr, y = s.sb("ur", [NS, 512]), s.sb("dr", [NS, 512]), s.sb("y", [NS, 512])
        yc = s.sb("yc", [P, 4, NS])
        sg, idt = s.sb("sgn", [P, 1]), s.sb("id", [P, P])
        yp, tr = s.ps("yp", [P, 512]), s.ps("tr", [P, 512])
        ready, own, new, mm_, pre, gel, trd, ycd, out = (s.sem(n) for n in (
            "ready", "own", "new", "mm", "pre", "gel", "trd", "ycd", "out"))
        block = s.block()

        @block.sync
        def _(sp):
            loads = ((ub[:, :, :, :].rearrange("p b g c -> p (b g c)"),
                      u.rearrange("(o b) c -> o (b c)", o=1).broadcast_to([P, NS * 512])),
                     (lt[:, :, :], kept_l), (mt[:, :, :], kept_m), (at[:, :, :], kept_a), (h[:, :, :, :], h_in),
                     (ur[:, :], u), (dr[:, :], d_row.broadcast_to([NS, 512])), (sg[:, :], const["sgn"]),
                     (idt[:, :], const["ident"]))
            for dst, src in loads:
                sp.dma_start(dst, src).then_inc(ready, 16)
            sp.wait_ge(new, 1)
            sp.dma_start(h_out, hn[:, :, :]).then_inc(out, 16)
            sp.wait_ge(ycd, 1)
            sp.dma_start(yT[:, :, SEQ:COLS], yc[:, :, :]).then_inc(out, 16)
            sp.wait_ge(out, 32)

        @block.vector
        def _(dve):
            link = Chain(dve, own)
            tt = lambda o, a, b, op: link(dve.tensor_tensor(o, a, b, op))
            row = lambda ap: ap.rearrange("p (o g) -> p o g", o=1).broadcast_to([P, NS, G])
            dve.wait_ge(ready, 144)
            lb = lt[:, :, :].rearrange("p (o g) c -> p o (g c)", o=1).broadcast_to([P, NS, G * GC])
            tt(t[:, :, :, :].rearrange("p b g c -> p b (g c)"), ub[:, :, :, :].rearrange("p b g c -> p b (g c)"),
               lb, ALU.mult)
            link(dve.tensor_reduce(bu[:, :, :], t[:, :, :, :], AX.X, ALU.add))
            tt(w[:, :, :], h[:, 0], row(at[:, 0, :]), ALU.mult)
            tt(bu[:, :, :], bu[:, :, :], w[:, :, :], ALU.add)
            link(dve.tensor_scalar(h[:, 1], h[:, 1], sg[:, 0:1], None, ALU.mult))
            tt(w[:, :, :], h[:, 1], row(at[:, 1, :]), ALU.mult)
            dve.tensor_tensor(hn[:, :, :], bu[:, :, :], w[:, :, :], ALU.add).then_inc(new, 1)
            tt(ur[:, :], ur[:, :], dr[:, :], ALU.mult)
            dve.wait_ge(mm_, 1)
            dve.tensor_tensor(y[:, :], ur[:, :], yp[0:NS, :], ALU.add).then_inc(pre, 1)
            dve.wait_ge(trd, 1)
            dve.tensor_copy(yc[:, :, :], tr[:, 0:4 * NS].rearrange("p (k b) -> p k b", k=4)).then_inc(ycd, 1)

        @block.tensor
        def _(pe):
            pe.wait_ge(ready, 144)
            pe.wait_ge(new, 1)
            for g in range(G):
                mm = pe.matmul(yp[0:NS, g * GC:(g + 1) * GC], hn[:, :, g], mt[:, g, :], start=True, stop=True)
            mm.then_inc(mm_, 1)
            pe.wait_ge(gel, 1)
            for k in range(4):
                mm = pe.transpose(tr[:, k * NS:(k + 1) * NS], y[:, k * P:(k + 1) * P], idt[0:NS, 0:NS])
            mm.then_inc(trd, 1)

        @block.scalar
        def _(act):
            act.wait_ge(pre, 1)
            act.activation(y[:, :], y[:, :], ACT.Gelu_apprx_tanh).then_inc(gel, 1)


def s5_glu(nc, yT, gate, w, bias, cat):
    with Stage(nc, "sg") as s:
        y = s.sb("y", [P, 4, COLS])
        wt, bt = s.sb("w", [P, 4, 512]), s.sb("b", [P, 4])
        gt = [s.sb(f"g{q}", [P, COLS]) for q in (0, 1)]
        sg = [s.sb(f"s{q}", [P, COLS]) for q in (0, 1)]
        acc = s.ps("acc", [P, NBLK, 512])
        cst, mm_, free, silu, half, outp = (s.sem(n) for n in ("cst", "mm", "free", "silu", "half", "outp"))
        g_in = [s.sem(f"g_in{q}") for q in (0, 1)]
        stored = [s.sem(f"stored{q}") for q in (0, 1)]
        blocks = [(b * BLK, min(BLK, COLS - b * BLK)) for b in range(NBLK)]
        block = s.block()

        @block.sync
        def _(sp):
            for dst, src in ((y[:, :, :], yT), (wt[:, :, :], w), (bt[:, :], bias)):
                sp.dma_start(dst, src).then_inc(cst, 16)
            for n in range(4):
                if n > 1:
                    sp.wait_ge(stored[n % 2], 16 * (n // 2))
                sp.dma_start(gt[n % 2][:, :], gate[n]).then_inc(g_in[n % 2], 16)

        @block.tensor
        def _(pe):
            pe.wait_ge(cst, 48)
            for n in range(4):
                for b, (at, width) in enumerate(blocks):
                    if n:
                        pe.wait_ge(free, (n - 1) * NBLK + b + 1)
                    for k in range(4):
                        mm = pe.matmul(acc[:, b, 0:width], wt[:, k, n * P:(n + 1) * P], y[:, k, at:at + width],
                                       start=(k == 0), stop=(k == 3))
                    mm.then_inc(mm_, 1)

        @block.scalar
        def _(act):
            act.wait_ge(cst, 48)
            for n in range(4):
                q = n % 2
                act.wait_ge(g_in[q], 16 * (n // 2 + 1))
                act.activation(gt[q][:, :], gt[q][:, :], ACT.Silu).then_inc(silu, 1)
                if n > 1:
                    act.wait_ge(outp, n - 1)
                for b, (at, width) in enumerate(blocks):
                    act.wait_ge(mm_, n * NBLK + b + 1)
                    act.activation(sg[q][:, at:at + width], acc[:, b, 0:width], ACT.Sigmoid,
                                   bias=bt[:, n:n + 1]).then_inc(free, 1)

        @block.vector
        def _(dve):
            for n in range(4):
                q = n % 2
                dve.wait_ge(free, (n + 1) * NBLK)
                dve.wait_ge(silu, n + 1)
                dve.tensor_tensor(sg[q][:, :], sg[q][:, :], y[:, n, :], ALU.mult).then_inc(half, 1)
                dve.wait_ge(half, n + 1)
                if n > 1:
                    dve.wait_ge(stored[q], 16 * (n // 2))
                dve.tensor_tensor(gt[q][:, :], sg[q][:, :], gt[q][:, :], ALU.mult).then_inc(outp, 1)

        @block.gpsimd
        def _(pool):
            for n in range(4):
                pool.wait_ge(outp, n + 1)
                pool.dma_start(cat[4 + n], gt[n % 2][:, :]).then_inc(stored[n % 2], 16)
            for q in (0, 1):
                pool.wait_ge(stored[q], 32)


HC, DC = 8, 64
STEPS = [(i, g) for i in range(TT) for g in range(i // 4, -1, -1)]
CLAMP = 2.0 ** 60


def stick_prompt(nc, z, v, bias, const, cat):
    with Stage(nc, "sp") as s:
        two = lambda n, shape: [s.sb(f"{n}{q}", shape) for q in (0, 1)]
        kT, qT = two("k", [DC + 1, SEQ]), two("q", [DC + 1, SEQ])
        vt, oT, gt = two("v", [P, TT, DC]), two("o", [DC, SEQ]), two("g", [DC, SEQ])
        e, S, att, aT = (s.sb(n, [P, 4, 512]) for n in ("e", "S", "att", "aT"))
        sp_ = s.sb("sp", [P, 4, 512])
        bt = s.sb("bias", [DC + 1, HC])
        idt, neg, one = s.sb("id", [P, P]), s.sb("neg", [P, P]), s.sb("one", [P, 1])
        zb = [s.ps(f"z{n}", [P, 512]) for n in range(4)]
        tb = [s.ps(f"t{n}", [P, 512]) for n in range(2)]
        ob = [s.ps(f"ob{n}", [P, 512]) for n in range(2)]
        cst, rows = s.sem("cst"), s.sem("rows")
        per_slot = ("kv_in", "scaled", "brow", "gate", "gated", "stored")
        slot = {n: [s.sem(f"{n}{q}") for q in (0, 1)] for n in per_slot}
        sem = {n: s.sem(n) for n in ("z_pe", "e1", "cl", "ln", "mx", "sc", "arg", "e2", "t_pe", "t_ev")}
        o_pe, o_ev, held = s.sem("o_pe"), s.sem("o_ev"), s.sem("held")
        NSTEP = len(STEPS)
        block = s.block()
        LAST = [n for n, (i, g) in enumerate(STEPS) if g == 0]
        keys = lambda i, g: (min(4 * g + 3, i) - 4 * g + 1) * P

        def at(eng, name, m, n):
            eng.wait_ge(sem[name], m * 2 * NSTEP + n + 1)

        @block.sync
        def _(sp):
            sp.dma_start(idt[:, :], const["ident"]).then_inc(cst, 16)
            sp.dma_start(neg[:, :], const["neg"]).then_inc(cst, 16)
            sp.dma_start(bt[DC:DC + 1, :], bias).then_inc(cst, 16)
            with sp.Fori(0, HC // 2) as m:
                sp.wait_ge(slot["stored"][0], 16 * m)
                sp.wait_ge(slot["stored"][1], 16 * m)
                for q in (0, 1):
                    r = slice(64 * q, 64 * q + 64)
                    pick = lambda base: z[ds(m + base, 1), r, 0:SEQ].rearrange("o p c -> p (o c)")
                    sp.dma_start(kT[q][0:DC, :], pick(4)).then_inc(slot["kv_in"][q], 16)
                    sp.dma_start(qT[q][0:DC, :], pick(0)).then_inc(slot["kv_in"][q], 16)
                    sp.dma_start(vt[q][:, :, :], v[0:TT, :, ds(m * 2 * DC + q * DC, DC)]
                                 .rearrange("t p c -> p t c")).then_inc(slot["kv_in"][q], 16)
                    sp.dma_start(gt[q][:, :], pick(8)).then_inc(slot["kv_in"][q], 16)
                for q in (0, 1):
                    sp.wait_ge(slot["gated"][q], m + 1)
                    sp.dma_start(cat[ds(m, 1), 64 * q:64 * q + 64, 0:SEQ].rearrange("o p c -> p (o c)"),
                                 oT[q][:, :]).then_inc(slot["stored"][q], 16)
            sp.wait_ge(slot["stored"][0], 16 * HC // 2)
            sp.wait_ge(slot["stored"][1], 16 * HC // 2)

        @block.tensor
        def _(pe):
            pe.wait_ge(cst, 48)
            with pe.Fori(0, HC // 2) as m:
                def scores(n):
                    q, (i, g) = n // NSTEP, STEPS[n % NSTEP]
                    if n % NSTEP == 0:
                        pe.wait_ge(slot["scaled"][q], m + 1)
                        pe.wait_ge(slot["brow"][q], m + 1)
                    if n >= 4:
                        at(pe, "arg", m, n - 4)
                    else:
                        at(pe, "arg", m, -1)
                    w, bank = keys(i, g), zb[n % 4]
                    diag = g == i // 4
                    mm = pe.matmul(bank[:, 0:w], qT[q][:, i * P:(i + 1) * P], kT[q][:, 4 * g * P:4 * g * P + w],
                                   start=True, stop=not diag)
                    if diag:
                        mm = pe.matmul(bank[:, w - P:w], idt[:, :], neg[:, :], start=False, stop=True)
                    mm.then_inc(sem["z_pe"], 1)

                def flip(n):
                    i, g = STEPS[n % NSTEP]
                    at(pe, "e2", m, n)
                    at(pe, "t_ev", m, n - 2 if n >= 2 else -1)
                    for b in range(keys(i, g) // P):
                        mm = pe.transpose(tb[n % 2][:, b * P:(b + 1) * P], att[:, n % 4, b * P:(b + 1) * P], idt[:, :])
                    mm.then_inc(sem["t_pe"], 1)

                def values(n):
                    q, (i, g) = n // NSTEP, STEPS[n % NSTEP]
                    at(pe, "t_ev", m, n)
                    tile = q * TT + i
                    if g == i // 4:
                        pe.wait_ge(o_ev, m * 2 * TT + (tile - 1 if tile >= 2 else 0))
                    nb = keys(i, g) // P
                    for b in range(nb):
                        mm = pe.matmul(ob[i % 2][0:DC, 0:P], vt[q][:, 4 * g + b, :], aT[:, n % 4, b * P:(b + 1) * P],
                                       start=(g == i // 4 and b == 0), stop=(g == 0 and b == nb - 1))
                    if g == 0:
                        mm.then_inc(o_pe, 1)
                for n in range(2 * NSTEP + 5):
                    if n < 2 * NSTEP:
                        scores(n)
                    if 0 <= n - 4 < 2 * NSTEP:
                        flip(n - 4)
                    if 0 <= n - 5 < 2 * NSTEP:
                        values(n - 5)

        @block.scalar
        def _(act):
            with act.Fori(0, HC // 2) as m:
                for q in (0, 1):
                    act.wait_ge(slot["kv_in"][q], 64 * m + 64)
                    act.mul(qT[q][0:DC, :], qT[q][0:DC, :], DC ** -0.5).then_inc(slot["scaled"][q], 1)
                    act.activation(gt[q][:, :], gt[q][:, :], ACT.Silu).then_inc(slot["gate"][q], 1)
                act.preload_act_table_set(LN_EXP)
                for n in range(2 * NSTEP + 5):
                    if n < 2 * NSTEP:
                        w = keys(*STEPS[n % NSTEP])
                        at(act, "z_pe", m, n)
                        at(act, "mx", m, n - 4 if n >= 4 else -1)
                        act.activation(e[:, n % 4, 0:w], zb[n % 4][:, 0:w], ACT.Exp).then_inc(sem["e1"], 1)
                    k = n - 1
                    if 0 <= k < 2 * NSTEP:
                        w = keys(*STEPS[k % NSTEP])
                        at(act, "cl", m, k)
                        act.activation(e[:, k % 4, 0:w], e[:, k % 4, 0:w], ACT.Ln, bias=1.0).then_inc(sem["ln"], 1)
                    k = n - 3
                    if 0 <= k < 2 * NSTEP:
                        w = keys(*STEPS[k % NSTEP])
                        at(act, "arg", m, k)
                        act.activation(att[:, k % 4, 0:w], sp_[:, k % 4, 0:w], ACT.Exp).then_inc(sem["e2"], 1)
                    k = n - 4
                    if 0 <= k < 2 * NSTEP:
                        w = keys(*STEPS[k % NSTEP])
                        at(act, "t_pe", m, k)
                        act.copy(aT[:, k % 4, 0:w], tb[k % 2][:, 0:w]).then_inc(sem["t_ev"], 1)

        @block.vector
        def _(dve):
            dve.memset(one[:, :], 1.0).then_inc(rows, 1)
            dve.memset(kT[0][DC:DC + 1, :], 1.0).then_inc(rows, 1)
            dve.memset(kT[1][DC:DC + 1, :], 1.0).then_inc(rows, 1)
            dve.wait_ge(cst, 48)
            dve.wait_ge(rows, 3)
            with dve.Fori(0, HC // 2) as m:
                for q in (0, 1):
                    at(dve, "z_pe", m, -1)
                    dve.tensor_scalar(qT[q][DC:DC + 1, :], kT[q][DC:DC + 1, :], bt[DC:DC + 1, ds(m * 2 + q, 1)],
                                      None, ALU.mult).then_inc(slot["brow"][q], 1)

                def collect(tile):
                    i, q = tile % TT, tile // TT
                    dve.wait_ge(o_pe, m * 2 * TT + tile + 1)
                    dve.tensor_copy(oT[q][:, i * P:(i + 1) * P], ob[i % 2][0:DC, 0:P]).then_inc(o_ev, 1)
                tiles = 0
                for n in range(2 * NSTEP + 2):
                    if n < 2 * NSTEP:
                        w = keys(*STEPS[n % NSTEP])
                        at(dve, "ln", m, n)
                        at(dve, "e2", m, n - 4 if n >= 4 else -1)
                        dve.tensor_tensor(sp_[:, n % 4, 0:w], e[:, n % 4, 0:w], zb[n % 4][:, 0:w],
                                          ALU.max).then_inc(sem["mx"], 1)
                    k = n - 1
                    if 0 <= k < 2 * NSTEP:
                        i, g = STEPS[k % NSTEP]
                        w = keys(i, g)
                        at(dve, "mx", m, k)
                        at(dve, "arg", m, k - 4 if k >= 4 else -1)
                        if g == i // 4:
                            start = 0.0
                        else:
                            at(dve, "sc", m, k - 1)
                            start = S[:, (k - 1) % 4, 0:1]
                        dve.tensor_tensor_scan(S[:, k % 4, 0:w][:, ::-1], one[:, 0:1].broadcast_to([P, w]),
                                               sp_[:, k % 4, 0:w][:, ::-1], start, ALU.mult,
                                               ALU.add).then_inc(sem["sc"], 1)
                        at(dve, "sc", m, k)
                        dve.tensor_tensor(sp_[:, k % 4, 0:w], zb[k % 4][:, 0:w], S[:, k % 4, 0:w],
                                          ALU.subtract).then_inc(sem["arg"], 1)
                    while tiles < 2 * TT and n >= (tiles // TT) * NSTEP + LAST[tiles % TT] + 6:
                        collect(tiles)
                        tiles += 1
                for tile in range(tiles, 2 * TT):
                    collect(tile)

        @block.gpsimd
        def _(pool):
            with pool.Fori(0, HC // 2) as m:
                for n in range(2 * NSTEP):
                    w = keys(*STEPS[n % NSTEP])
                    at(pool, "e1", m, n)
                    pool.sem_inc(held, 1)
                    pool.tensor_scalar(e[:, n % 4, 0:w], e[:, n % 4, 0:w], CLAMP, None, ALU.min
                                       ).then_inc(sem["cl"], 1)
                for q in (0, 1):
                    pool.wait_ge(o_ev, m * 2 * TT + (q + 1) * TT)
                    pool.wait_ge(slot["gate"][q], m + 1)
                    pool.tensor_tensor(oT[q][:, :], oT[q][:, :], gt[q][:, :], ALU.mult
                                       ).then_inc(slot["gated"][q], 1)


HD, DK, DV = 4, 64, 128
GLA_TAU = 16.0
G_Q, G_K, G_V = range(3)


def gla_operands(nc, z, alpha_w, alpha_b, const, ops, wc, sample_vecs):
    with Stage(nc, "gp") as s:
        two = lambda n: [s.sb(f"{n}{q}", [P, COLS]) for q in (0, 1)]
        qt, kt, l, c, ep, en, ec = two("q"), two("k"), two("l"), two("c"), two("ep"), two("en"), two("ec")
        ad, mask = s.sb("ad", [P, COLS]), s.sb("mask", [P, COLS])
        wt, bt, nb, idt = s.sb("w", [P, 256]), s.sb("b", [P, 2]), s.sb("nb", [P, 2]), s.sb("id", [P, P])
        wce = s.sb("wce", [P, 2, NCH])
        vec = s.sb("vec", [P, 2, 16, NS])
        vecT = s.sb("vecT", [3 * NS, 2, P])
        acc = s.ps("acc", [P, NBLK, 512])
        trp = s.ps("trp", [P, 2, P])
        names = ("cst", "mm", "e1", "cl", "ln", "ng", "blk", "scan", "ce", "exps", "vecs", "vtr", "vst", "out", "own",
                 "stored", "nbd")
        q_ = {n: s.sem(n) for n in names}
        blocks = [(b * BLK, min(BLK, COLS - b * BLK)) for b in range(NBLK)]
        block = s.block()

        @block.sync
        def _(sp):
            for dst, src in ((ad[:, :], z[20]), (mask[:, :], const["reset"]), (wt[:, :], alpha_w), (bt[:, :], alpha_b),
                             (idt[:, :], const["ident"]), (qt[0][:, :], z[12]), (qt[1][:, :], z[13]),
                             (kt[0][:, :], z[14]), (kt[1][:, :], z[15])):
                sp.dma_start(dst, src).then_inc(q_["cst"], 16)
            for j in (0, 1):
                sp.wait_ge(q_["out"], 3 * j + 3)
                for n, t in enumerate((ep, en, ec)):
                    sp.dma_start(ops[:, n, j, :], t[j][:, 0:SEQ]).then_inc(q_["stored"], 16)
                sp.wait_ge(q_["vst"], j + 1)
                sp.dma_start(sample_vecs[:, :, j * P:(j + 1) * P].rearrange("v b c -> (v b) c"),
                             vecT[:, j, :]).then_inc(q_["stored"], 16)
            sp.dma_start(wc, wce[:, :, :]).then_inc(q_["stored"], 16)
            sp.wait_ge(q_["stored"], 9 * 16)

        @block.tensor
        def _(pe):
            pe.wait_ge(q_["cst"], 144)
            for j in (0, 1):
                for b, (at, width) in enumerate(blocks):
                    if j:
                        pe.wait_ge(q_["blk"], b + 1)
                    pe.matmul(acc[:, b, 0:width], wt[:, j * P:(j + 1) * P], ad[:, at:at + width], start=True,
                              stop=True).then_inc(q_["mm"], 1)
            for j in (0, 1):
                pe.wait_ge(q_["vecs"], j + 1)
                if j:
                    pe.wait_ge(q_["vst"], 1)
                pe.transpose(trp[:, j, :], vec[:, j].rearrange("p v b -> p (v b)"), idt[:, :]).then_inc(q_["vtr"], 1)

        @block.scalar
        def _(act):
            act.wait_ge(q_["nbd"], 1)
            act.preload_act_table_set(LN_EXP)
            for j in (0, 1):
                for b, (at, width) in enumerate(blocks):
                    act.wait_ge(q_["mm"], j * NBLK + b + 1)
                    act.activation(l[j][:, at:at + width], acc[:, b, 0:width], ACT.Exp, scale=-1.0,
                                   bias=nb[:, j:j + 1]).then_inc(q_["e1"], 1)
                act.wait_ge(q_["cl"], j + 1)
                act.activation(l[j][:, :], l[j][:, :], ACT.Ln, bias=1.0).then_inc(q_["ln"], 1)
            for j in (0, 1):
                act.wait_ge(q_["scan"], j + 1)
                act.activation(ep[j][:, :], c[j][:, :], ACT.Exp, scale=1.0 / GLA_TAU).then_inc(q_["exps"], 1)
                act.activation(en[j][:, :], c[j][:, :], ACT.Exp, scale=-1.0 / GLA_TAU).then_inc(q_["exps"], 1)
                act.wait_ge(q_["ce"], j + 1)
                act.activation(ec[j][:, 0:SEQ], ec[j][:, 0:SEQ], ACT.Exp, scale=1.0 / GLA_TAU).then_inc(q_["exps"], 1)
                act.activation(wce[:, j, :], c[j][:, CH - 1:SEQ:CH], ACT.Exp,
                               scale=1.0 / GLA_TAU).then_inc(q_["exps"], 1)
                act.wait_ge(q_["vtr"], j + 1)
                act.copy(vecT[:, j, :], trp[0:3 * NS, j, :]).then_inc(q_["vst"], 1)

        @block.vector
        def _(dve):
            link = Chain(dve, q_["own"])
            link(dve.memset(vec[:, :, :, :], 0.0))
            dve.wait_ge(q_["cst"], 144)
            dve.tensor_scalar(nb[:, :], bt[:, :], -1.0, None, ALU.mult).then_inc(q_["nbd"], 1)
            for j in (0, 1):
                dve.wait_ge(q_["e1"], (j + 1) * NBLK)
                dve.tensor_scalar(l[j][:, :], l[j][:, :], CLAMP, None, ALU.min).then_inc(q_["cl"], 1)
                dve.wait_ge(q_["ln"], j + 1)
                link(dve.tensor_scalar(l[j][:, :], l[j][:, :], -1.0, None, ALU.mult))
                for b, (at, width) in enumerate(blocks):
                    dve.scalar_tensor_tensor(out=l[j][:, at:at + width], in0=acc[:, b, 0:width],
                                             scalar=bt[:, j:j + 1], in1=l[j][:, at:at + width], op0=ALU.add,
                                             op1=ALU.min).then_inc(q_["blk"], 1)
                dve.wait_ge(q_["blk"], (j + 1) * NBLK)
                dve.tensor_tensor_scan(c[j][:, :], mask[:, :], l[j][:, :], 0.0, ALU.mult,
                                       ALU.add).then_inc(q_["scan"], 1)
                dve.wait_ge(q_["scan"], j + 1)
                ends = c[j][:, CH - 1:SEQ:CH].rearrange("p (n o) -> p n o", o=1).broadcast_to([P, NCH, CH])
                dve.tensor_tensor(ec[j][:, 0:SEQ].rearrange("p (n t) -> p n t", t=CH), ends,
                                  c[j][:, 0:SEQ].rearrange("p (n t) -> p n t", t=CH),
                                  ALU.subtract).then_inc(q_["ce"], 1)
            for j in (0, 1):
                dve.wait_ge(q_["exps"], 4 * j + 4)
                dve.tensor_copy(vec[:, j, G_Q, :], qt[j][:, SEQ:COLS])
                dve.tensor_copy(vec[:, j, G_K, :], kt[j][:, SEQ:COLS])
                link(dve.tensor_copy(vec[:, j, G_V, :], ep[j][:, SEQ:COLS]))
                dve.sem_inc(q_["vecs"], 1)
                dve.scalar_tensor_tensor(out=ep[j][:, :], in0=qt[j][:, :], scalar=DK ** -0.5, in1=ep[j][:, :],
                                         op0=ALU.mult, op1=ALU.mult).then_inc(q_["out"], 1)
                dve.tensor_tensor(en[j][:, :], kt[j][:, :], en[j][:, :], ALU.mult).then_inc(q_["out"], 1)
                dve.tensor_tensor(ec[j][:, 0:SEQ], kt[j][:, 0:SEQ], ec[j][:, 0:SEQ], ALU.mult).then_inc(q_["out"], 1)


def gla_chunks(nc, ops, v, wc, const, o, s_out):
    COUNT = dict(ops_in=64, sc_pe=1, kh_pe=1, sc=1, kh=1, o_pe=1, s_pe=1, o_ev=1, o_st=16)
    with Stage(nc, "gc") as s:
        two = lambda n, shape: [s.sb(f"{n}{q}", shape) for q in (0, 1)]
        opx, v2 = two("opx", [P, 3, 2, P]), two("v2", [P, 2, DV])
        sc, kh, ot = two("sc", [P, 2, P]), two("kh", [P, 2, P]), two("ot", [P, HD, CH])
        st = two("st", [P, 2, DV])
        mask, idt, wct = s.sb("mask", [P, P]), s.sb("id", [P, P]), s.sb("wc", [P, 2, NCH])
        bank = [[s.ps(f"bank{q}{n}", [P, 512]) for n in range(4)] for q in (0, 1)]
        sem = {n: [s.sem(f"{n}{q}") for q in (0, 1)] for n in COUNT}
        cst, zero, s_sb, s_st = s.sem("cst"), s.sem("zero"), s.sem("s_sb"), s.sem("s_st")
        block = s.block()
        pair = lambda b: b[:, 0:256].rearrange("p (j c) -> p j c", j=2)

        def wait(eng, name, q, m, k):
            eng.wait_ge(sem[name][q], m * COUNT[name] + k)

        @block.sync
        def _(sp):
            for dst, src in ((mask[:, :], const["mask4"][:, P:2 * P]), (idt[:, :], const["ident"]),
                             (wct[:, :, :], wc)):
                sp.dma_start(dst, src).then_inc(cst, 16)
            sp.wait_ge(zero, 4)
            with sp.Fori(0, NCH // 4) as n:
                for t in (0, 1):
                    m = n * 2 + t
                    for q in (0, 1):
                        wait(sp, "o_pe", q, m, 0)
                        wait(sp, "s_pe", q, m, 0)
                        c = m * 2 + q
                        for h in (0, 1):
                            r = slice(64 * h, 64 * h + 64)
                            sp.dma_start(opx[q][r, :, :, r].rearrange("p n j c -> p (n j) c"),
                                         ops[r, :, :, ds(c * CH, CH)].rearrange("p n j c -> p (n j) c")
                                         ).then_inc(sem["ops_in"][q], 16)
                            src = v[ds(m, 1), 64 * q:64 * q + 64, 512:1024].rearrange("o p c -> p (o c)")
                            sp.dma_start(v2[q][r, :, :], src.rearrange("p (j h c) -> p h j c", j=2, h=2)[:, h]
                                         ).then_inc(sem["ops_in"][q], 16)
            sp.wait_ge(s_sb, NCH + 1)
            sp.dma_start(s_out, st[0][:, :, :]).then_inc(s_st, 16)
            sp.wait_ge(s_st, 16)

        @block.tensor
        def _(pe):
            pe.wait_ge(cst, 48)
            with pe.Fori(0, NCH // 2) as m:
                for q in (0, 1):
                    wait(pe, "ops_in", q, m, 64)
                    wait(pe, "sc", q, m, 0)
                    for j in (0, 1):
                        mm = pe.matmul(bank[q][0][:, j * P:(j + 1) * P], opx[q][:, 1, j, :], opx[q][:, 0, j, :],
                                       start=True, stop=True)
                    mm.then_inc(sem["sc_pe"][q], 1)
                    wait(pe, "kh", q, m, 0)
                    for j in (0, 1):
                        mm = pe.transpose(bank[q][1][:, j * P:(j + 1) * P], opx[q][:, 2, j, :], idt[:, :])
                    mm.then_inc(sem["kh_pe"][q], 1)
                for q in (0, 1):
                    wait(pe, "kh", q, m, 1)
                    pe.wait_ge(s_sb, m * 2 + q + 1)
                    for j in (0, 1):
                        mm = pe.matmul(bank[q][3][:, j * DV:(j + 1) * DV], kh[q][:, j, :], v2[q][:, j, :],
                                       start=True, stop=True)
                    mm.then_inc(sem["s_pe"][q], 1)
                    wait(pe, "sc", q, m, 1)
                    wait(pe, "o_ev", q, m, 0)
                    for j in (0, 1):
                        b = bank[q][2][:, j * P:(j + 1) * P]
                        pe.matmul(b, v2[q][:, j, :], sc[q][:, j, :], start=True, stop=False)
                        mm = pe.matmul(b, st[q][:, j, :], opx[q][:, 0, j, :], start=False, stop=True)
                    mm.then_inc(sem["o_pe"][q], 1)

        @block.scalar
        def _(act):
            with act.Fori(0, NCH // 2) as m:
                for q in (0, 1):
                    wait(act, "kh_pe", q, m, 1)
                    wait(act, "s_pe", q, m, 0)
                    act.copy(kh[q][:, :, :], pair(bank[q][1])).then_inc(sem["kh"][q], 1)
                for q in (0, 1):
                    wait(act, "o_pe", q, m, 1)
                    wait(act, "o_st", q, m, 0)
                    act.copy(ot[q][:, :, :].rearrange("p n c -> p (n c)"), bank[q][2][:, 0:256]
                             ).then_inc(sem["o_ev"][q], 1)
                    wait(act, "o_ev", q, m, 1)
                    act.dma_start(o[:, :, ds((m * 2 + q) * CH, CH)].rearrange("n p c -> p n c"),
                                  ot[q][:, :, :]).then_inc(sem["o_st"][q], 16)
            for q in (0, 1):
                act.wait_ge(sem["o_st"][q], 16 * NCH // 2)

        @block.vector
        def _(dve):
            for q in (0, 1):
                dve.memset(opx[q][:, :, :, :], 0.0).then_inc(zero, 1)
                dve.memset(st[q][:, :, :], 0.0).then_inc(zero, 1)
            dve.wait_ge(zero, 4)
            dve.sem_inc(s_sb, 1)
            dve.wait_ge(cst, 48)
            with dve.Fori(0, NCH // 2) as m:
                for q in (0, 1):
                    wait(dve, "sc_pe", q, m, 1)
                    wait(dve, "o_pe", q, m, 0)
                    dve.tensor_tensor(sc[q][:, :, :], pair(bank[q][0]),
                                      mask[:, :].rearrange("p (o c) -> p o c", o=1).broadcast_to([P, 2, P]),
                                      ALU.mult).then_inc(sem["sc"][q], 1)
                for q in (0, 1):
                    wait(dve, "s_pe", q, m, 1)
                    wait(dve, "o_pe", 1 - q, m, q)
                    dve.wait_ge(s_sb, m * 2 + q + 1)
                    dve.scalar_tensor_tensor(out=st[1 - q][:, 0, :], in0=st[q][:, 0, :],
                                             scalar=wct[:, 0, ds(m * 2 + q, 1)], in1=bank[q][3][:, 0:DV],
                                             op0=ALU.mult, op1=ALU.add)
                    dve.scalar_tensor_tensor(out=st[1 - q][:, 1, :], in0=st[q][:, 1, :],
                                             scalar=wct[:, 1, ds(m * 2 + q, 1)], in1=bank[q][3][:, DV:2 * DV],
                                             op0=ALU.mult, op1=ALU.add).then_inc(s_sb, 1)


def gla_samples(nc, vecs, v, state, ident, state_out, o):
    BH = NS * HD
    with Stage(nc, "gs") as s:
        S, T = s.sb("S", [BH, DK, DV]), s.sb("T", [BH, DK, DV])
        vt, vv, yt = s.sb("vec", [BH, 3, DK]), s.sb("v", [BH, DV]), s.sb("y", [BH, DV])
        yc, idt = s.sb("yc", [P, HD, NS]), s.sb("id", [P, P])
        tr = s.ps("tr", [P, 512])
        ready, own, out, y_done, tr_done, yc_done = (s.sem(n) for n in ("ready", "own", "out", "y_done", "tr", "yc"))
        block = s.block()

        @block.sync
        def _(sp):
            sp.dma_start(S[:, :, :], state).then_inc(ready, 16)
            sp.dma_start(idt[:, :], ident).then_inc(ready, 16)
            sp.dma_start(vt[:, :, :], vecs.rearrange("n b (h c) -> (b h) n c", c=DK)).then_inc(ready, 16)
            for b in range(NS):
                sp.dma_start(vv[b * HD:(b + 1) * HD, :],
                             v[b:b + 1, :].rearrange("o (h c) -> (o h) c", c=DV)).then_inc(ready, 16)
            sp.wait_ge(own, 3)
            sp.dma_start(state_out, S[:, :, :]).then_inc(out, 16)
            sp.wait_ge(yc_done, 1)
            sp.dma_start(o[:, :, SEQ:COLS].rearrange("n p c -> p n c"), yc[:, :, :]).then_inc(out, 16)
            sp.wait_ge(out, 32)

        @block.vector
        def _(dve):
            link = Chain(dve, own)
            col = lambda n: vt[:, n, :].rearrange("p (k o) -> p k o", o=1).broadcast_to([BH, DK, DV])
            row = vv[:, :].rearrange("p (o v) -> p o v", o=1).broadcast_to([BH, DK, DV])
            dve.wait_ge(ready, 16 * (3 + NS))
            dve.tensor_tensor(S[:, :, :], S[:, :, :], col(G_V), ALU.mult)
            link(dve.tensor_tensor(T[:, :, :], row, col(G_K), ALU.mult))
            link(dve.tensor_tensor(S[:, :, :], S[:, :, :], T[:, :, :], ALU.add))
            link(dve.tensor_tensor(T[:, :, :], S[:, :, :], col(G_Q), ALU.mult))
            link(dve.tensor_reduce(yt[:, :], T[:, :, :].rearrange("p k v -> p v k"), AX.X, ALU.add))
            dve.tensor_scalar(yt[:, :], yt[:, :], DK ** -0.5, None, ALU.mult).then_inc(y_done, 1)
            dve.wait_ge(tr_done, 1)
            dve.tensor_copy(yc[:, :, :], tr[:, 0:BH].rearrange("v (b h) -> v h b", h=HD)).then_inc(yc_done, 1)

        @block.tensor
        def _(pe):
            pe.wait_ge(ready, 16 * (3 + NS))
            pe.wait_ge(y_done, 1)
            pe.transpose(tr[:, 0:BH], yt[:, :], idt[0:BH, 0:BH]).then_inc(tr_done, 1)


def gla_output(nc, o, gate, gn, const, cat):
    with Stage(nc, "go") as s:
        two = lambda n: [s.sb(f"{n}{q}", [P, COLS]) for q in (0, 1)]
        ot, gt, sq, rs = two("o"), two("g"), two("sq"), two("rs")
        on, gnt, eps = s.sb("ones", [P, P]), s.sb("gn", [P, 4]), s.sb("eps", [P, 1])
        acc = s.ps("acc", [P, NBLK, 512])
        cst, mm_, free, eset = s.sem("cst"), s.sem("mm"), s.sem("free"), s.sem("eset")
        names = ("in", "sq", "gate", "rstd", "own", "out", "stored")
        sem = {n: [s.sem(f"{n}{q}") for q in (0, 1)] for n in names}
        blocks = [(b * BLK, min(BLK, COLS - b * BLK)) for b in range(NBLK)]
        block = s.block()

        @block.sync
        def _(sp):
            sp.dma_start(gnt[:, :], gn).then_inc(cst, 16)
            for h in range(HD):
                q, m = h % 2, h // 2
                sp.wait_ge(sem["stored"][q], 16 * m)
                sp.dma_start(ot[q][:, :], o[h]).then_inc(sem["in"][q], 16)
                sp.dma_start(gt[q][:, :], gate[h]).then_inc(sem["in"][q], 16)

        @block.tensor
        def _(pe):
            pe.wait_ge(eset, 2)
            for h in range(HD):
                pe.wait_ge(sem["sq"][h % 2], h // 2 + 1)
                for b, (at, width) in enumerate(blocks):
                    if h:
                        pe.wait_ge(free, (h - 1) * NBLK + b + 1)
                    pe.matmul(acc[:, b, 0:width], on[:, :], sq[h % 2][:, at:at + width], start=True,
                              stop=True).then_inc(mm_, 1)

        @block.scalar
        def _(act):
            act.wait_ge(eset, 2)
            for h in range(HD):
                q, m = h % 2, h // 2
                act.wait_ge(sem["in"][q], 32 * (m + 1))
                act.activation(gt[q][:, :], gt[q][:, :], ACT.Silu).then_inc(sem["gate"][q], 1)
                act.activation(sq[q][:, :], ot[q][:, :], ACT.Square).then_inc(sem["sq"][q], 1)
                act.preload_act_table_set(LN_EXP)
                for b, (at, width) in enumerate(blocks):
                    act.wait_ge(mm_, h * NBLK + b + 1)
                    act.activation(rs[q][:, at:at + width], acc[:, b, 0:width], ACT.Ln, scale=1.0 / DV,
                                   bias=eps[:, 0:1]).then_inc(free, 1)
                act.wait_ge(free, (h + 1) * NBLK)
                act.activation(rs[q][:, :], rs[q][:, :], ACT.Exp, scale=-0.5).then_inc(sem["rstd"][q], 1)
                act.wait_ge(sem["out"][q], m + 1)
                act.dma_start(cat[4 + h], ot[q][:, :]).then_inc(sem["stored"][q], 16)
            for q in (0, 1):
                act.wait_ge(sem["stored"][q], 32)

        @block.vector
        def _(dve):
            dve.memset(on[:, :], 1.0).then_inc(eset, 1)
            dve.memset(eps[:, :], RMS_EPS).then_inc(eset, 1)
            dve.wait_ge(cst, 16)
            for h in range(HD):
                q, m = h % 2, h // 2
                dve.wait_ge(sem["rstd"][q], m + 1)
                dve.scalar_tensor_tensor(out=ot[q][:, :], in0=ot[q][:, :], scalar=gnt[:, h:h + 1], in1=rs[q][:, :],
                                         op0=ALU.mult, op1=ALU.mult).then_inc(sem["own"][q], 1)
                dve.wait_ge(sem["own"][q], m + 1)
                dve.wait_ge(sem["gate"][q], m + 1)
                dve.tensor_tensor(ot[q][:, :], ot[q][:, :], gt[q][:, :], ALU.mult).then_inc(sem["out"][q], 1)


GP = 4
NG = PAGES // GP
SLOTS = 4
CW = HC * DC


def stick_samples(nc, z, cache_k, cache_v, table, bias, const, q_rows, cat):
    ALL = NS * HC * PAGES
    with Stage(nc, "sd") as s:
        pg = s.sb("pages", [P, SLOTS, GP, CW])
        prod = s.sb("prod", [P, 2, GP, CW])
        qb = s.sb("q", [P, NS, CW])
        zs, e, sp_, pre = (s.sb(n, [P, NS, HC, PAGES]) for n in ("z", "e", "softplus", "later"))
        att = s.sb("att", [P, 2, HC, PAGES])
        mask = s.sb("mask", [P, NS * HC, PAGES])
        bt, idt = s.sb("bias", [P, HC]), s.sb("id", [P, P])
        tri, one = s.sb("tri", [P, P]), s.sb("ones", [P, P])
        own = s.sb("own", [HC, CW])
        pt = s.sb("pt", [1, NS * PAGES], I32)
        qc, gc, qr = s.sb("qc", [P, 4, NS]), s.sb("gc", [P, 4, NS]), s.sb("qr", [NS, CW])
        om, oc = s.sb("om", [HC, NS, CW]), s.sb("oc", [P, 4, NS])
        within, total = s.ps("within", [P, 4, 512]), s.ps("total", [P, 4, 512])
        names = ("cst", "tab", "q_in", "q_tr", "q_ev", "q_st", "qb_in", "set", "prod_ok", "z_ok", "own", "exp", "cl",
                 "ln", "sp", "tri_pe", "arg", "att_ok", "o_pe", "o_ev", "mm", "gate", "out", "stored")
        q_ = {n: s.sem(n) for n in names}
        k_in = [s.sem(f"k_in{n}") for n in range(SLOTS)]
        v_in = [s.sem(f"v_in{n}") for n in range(SLOTS)]
        k_used, v_used = s.sem("k_used"), s.sem("v_used")
        LAP = NG // SLOTS
        LEAD = NG + SLOTS
        block = s.block()
        flat = lambda t: t[:, :, :, :].rearrange("p b h r -> p (b h r)")

        def load_pages(eng, cache, b, g, sem):
            for j in range(GP):
                page = eng.value_load(pt[0:1, ds(b * PAGES + (PAGES - 1 - GP * g - j), 1)], min_val=0,
                                      max_val=cache.shape[0] - 1)
                eng.dma_start(pg[:, g % SLOTS, j, :], cache[ds(page, 1)].rearrange("o k c -> k (o c)")
                              ).then_inc(sem[g % SLOTS], 16)

        @block.sync
        def _(sp):
            sp.dma_start(pt[:, :], table).then_inc(q_["tab"], 16)
            sp.dma_start(qc[:, :, :], z[0:4, :, SEQ:COLS].rearrange("n p c -> p n c")).then_inc(q_["q_in"], 16)
            sp.dma_start(idt[:, :], const["ident"]).then_inc(q_["q_in"], 16)
            sp.dma_start(tri[:, :], const["tri"]).then_inc(q_["cst"], 16)
            sp.dma_start(own[:, :], const["own"]).then_inc(q_["cst"], 16)
            sp.dma_start(bt[:, :], bias.broadcast_to([P, HC])).then_inc(q_["cst"], 16)
            sp.dma_start(gc[:, :, :], z[8:12, :, SEQ:COLS].rearrange("n p c -> p n c")).then_inc(q_["cst"], 16)
            sp.wait_ge(q_["q_ev"], 1)
            sp.dma_start(q_rows, qr[:, :]).then_inc(q_["q_st"], 16)
            sp.wait_ge(q_["q_st"], 16)
            sp.dma_start(qb[:, :, :], q_rows.rearrange("(o b) c -> o b c", o=1).broadcast_to([P, NS, CW])
                         ).then_inc(q_["qb_in"], 16)
            sp.wait_ge(q_["tab"], 16)
            with sp.Fori(0, NS) as b:
                for g in range(NG):
                    sp.wait_ge(k_used, b * NG + g + 1)
                    load_pages(sp, cache_k, b, g, k_in)
            with sp.Fori(0, NS) as b:
                for g in range(NG):
                    sp.wait_ge(v_used, (b + 1) * NG + g + 1)
                    load_pages(sp, cache_v, b, g, v_in)
            sp.wait_ge(q_["out"], 1)
            sp.dma_start(cat[0:4, :, SEQ:COLS].rearrange("n p c -> p n c"), oc[:, :, :]).then_inc(q_["stored"], 16)
            sp.wait_ge(q_["stored"], 16)

        @block.tensor
        def _(pe):
            pe.wait_ge(q_["q_in"], 32)
            for t in range(4):
                mm = pe.transpose(within[0:NS, 0, t * P:(t + 1) * P], qc[:, t, :], idt[:, :])
            mm.then_inc(q_["q_tr"], 1)
            pe.wait_ge(q_["cst"], 64)
            pe.wait_ge(q_["set"], 4)
            pe.wait_ge(q_["sp"], 1)
            rhs = flat(sp_)
            for n in range(4):
                pe.matmul(within[:, n, :], tri[:, :], rhs[:, n * 512:(n + 1) * 512], start=True, stop=True)
            for n in range(4):
                mm = pe.matmul(total[:, n, :], one[:, :], rhs[:, n * 512:(n + 1) * 512], start=True, stop=True)
            mm.then_inc(q_["tri_pe"], 1)
            pe.wait_ge(q_["arg"], 1)
            with pe.Fori(0, NS // 2) as m:
                for q in (0, 1):
                    pe.wait_ge(q_["att_ok"], m * 2 + q + 1)
                    pe.wait_ge(q_["o_ev"], m * 2 + q)
                    for g in range(NG):
                        pe.wait_ge(v_in[g % SLOTS], (m * 2 * LAP + q * LAP + g // SLOTS + 1) * 16 * GP)
                        for j in range(GP):
                            r = g * GP + j
                            mm = pe.matmul(within[0:HC, q, :], att[:, q, :, r], pg[:, g % SLOTS, j, :],
                                           start=(r == 0), stop=(r == PAGES - 1))
                        mm.then_inc(v_used, 1)
            pe.wait_ge(q_["o_ev"], NS)
            for b in range(NS):
                for t in range(4):
                    mm = pe.matmul(total[:, 0, t * NS + b:t * NS + b + 1], om[:, b, t * P:(t + 1) * P], one[0:HC, 0:1],
                                   start=True, stop=True)
            mm.then_inc(q_["mm"], 1)

        @block.scalar
        def _(act):
            act.wait_ge(q_["cst"], 64)
            act.activation(gc[:, :, :], gc[:, :, :], ACT.Silu).then_inc(q_["gate"], 1)
            act.preload_act_table_set(LN_EXP)
            act.wait_ge(q_["own"], 1)
            act.activation(flat(e), flat(zs), ACT.Exp).then_inc(q_["exp"], 1)
            act.wait_ge(q_["cl"], 1)
            act.activation(flat(sp_), flat(e), ACT.Ln, bias=1.0).then_inc(q_["ln"], 1)
            act.wait_ge(q_["arg"], 1)
            with act.Fori(0, NS // 2) as m:
                for q in (0, 1):
                    act.wait_ge(v_used, (m * 2 + q) * NG + SLOTS)
                    act.activation(att[:, q, :, :].rearrange("p h r -> p (h r)"),
                                   flat(zs)[:, ds((m * 2 + q) * HC * PAGES, HC * PAGES)],
                                   ACT.Exp).then_inc(q_["att_ok"], 1)

        @block.vector
        def _(dve):
            link = Chain(dve, q_["own"])
            dve.memset(one[:, :], 1.0).then_inc(q_["set"], 1)
            dve.memset(mask[:, :, 0:1], 0.0).then_inc(q_["set"], 1)
            dve.memset(mask[:, :, 1:PAGES], 1.0).then_inc(q_["set"], 1)
            dve.memset(pre[:, :, :, :], 0.0).then_inc(q_["set"], 1)
            dve.sem_inc(k_used, SLOTS)
            dve.wait_ge(q_["q_tr"], 1)
            dve.tensor_scalar(qr[:, :], within[0:NS, 0, :], DC ** -0.5, None, ALU.mult).then_inc(q_["q_ev"], 1)
            dve.wait_ge(q_["qb_in"], 16)
            with dve.Fori(0, NS) as b:
                for g in range(NG):
                    dve.wait_ge(k_in[g % SLOTS], (b * LAP + g // SLOTS + 1) * 16 * GP)
                    if g >= 2:
                        dve.wait_ge(q_["z_ok"], b * NG + g - 1)
                    else:
                        dve.wait_ge(q_["z_ok"], b * NG)
                    dve.tensor_tensor(prod[:, g % 2], pg[:, g % SLOTS],
                                      qb[:, ds(b, 1), :].broadcast_to([P, GP, CW]), ALU.mult).then_inc(k_used, 1)
                    dve.wait_ge(k_used, SLOTS + b * NG + g + 1)
                    dve.tensor_reduce(zs[:, ds(b, 1), :, g * GP:(g + 1) * GP].rearrange("p o h r -> p (o r) h"),
                                      prod[:, g % 2].rearrange("p j (h c) -> p j h c", c=DC), AX.X,
                                      ALU.add).then_inc(q_["z_ok"], 1)
            dve.wait_ge(q_["z_ok"], NS * NG)
            dve.sem_inc(v_used, LEAD)
            dve.wait_ge(q_["cst"], 64)
            dve.wait_ge(q_["set"], 4)
            for b in range(NS):
                ins = dve.tensor_tensor(zs[:, b], zs[:, b], bt[:, :].rearrange("p (h o) -> p h o", o=1)
                                        .broadcast_to([P, HC, PAGES]), ALU.add)
            link(ins)
            dve.wait_ge(q_["exp"], 1)
            dve.tensor_scalar(flat(e), flat(e), CLAMP, None, ALU.min).then_inc(q_["cl"], 1)
            dve.wait_ge(q_["ln"], 1)
            dve.tensor_tensor(flat(sp_), flat(sp_), flat(zs), ALU.max).then_inc(q_["sp"], 1)
            dve.wait_ge(q_["tri_pe"], 1)
            dve.tensor_tensor(flat(zs), flat(zs), within[:, :, :].rearrange("p n c -> p (n c)"), ALU.subtract)
            link(dve.tensor_tensor_scan(flat(pre), mask[:, :, :].rearrange("p n r -> p (n r)"),
                                        total[:, :, :].rearrange("p n c -> p (n c)"), 0.0, ALU.mult, ALU.add))
            dve.tensor_tensor(zs[:, :, :, 1:PAGES], zs[:, :, :, 1:PAGES], pre[:, :, :, 0:PAGES - 1],
                              ALU.subtract).then_inc(q_["arg"], 1)
            with dve.Fori(0, NS // 2) as m:
                for q in (0, 1):
                    dve.wait_ge(v_used, LEAD + (m * 2 + q + 1) * NG)
                    dve.tensor_tensor(om[:, ds(m * 2 + q, 1), :].rearrange("h o c -> h (o c)"), within[0:HC, q, :],
                                      own[:, :], ALU.mult).then_inc(q_["o_ev"], 1)
            dve.wait_ge(q_["mm"], 1)
            dve.wait_ge(q_["gate"], 1)
            dve.tensor_tensor(oc[:, :, :].rearrange("p n b -> p (n b)"), total[:, 0, 0:4 * NS],
                              gc[:, :, :].rearrange("p n b -> p (n b)"), ALU.mult).then_inc(q_["out"], 1)


def program(nc, I, O):
    def scratch(name, shape):
        return nc.dram_tensor(f"scratch_{name}", shape, F32).ap()

    z0 = O["z0"]
    project_channels(nc, "pe", I["xT"], I["w_e"], z0, 21)
    u = scratch("u", (TT + 1, P, 512))
    project_tokens(nc, "pu", lambda t, rows: I["xT_u"][ds(t, 1), :, :, 0:rows].rearrange("o p k c -> p (o k) c"),
                   I["w_u"], 512, u)
    ops, wc, vecs = scratch("ops", (P, 7, 4, SEQ)), scratch("wc", (P, 4, NCH)), scratch("vecs", (6, NS, 512))
    bonus, y_a = scratch("bonus", (4, P, COLS)), scratch("y_a", (P, 4, COLS))
    cat0 = scratch("cat0", (KT, P, COLS))
    rwkv_operands(nc, z0, I["z_last"], I["mu_low"], I["prm"], I["w2"], I["a2"], I, ops, wc, bonus, vecs)
    rwkv_chunks(nc, ops, wc, I, y_a, O["rwkv_p"])
    rwkv_samples(nc, vecs, I["state_rwkv"], I["ident"], O["rwkv_s"], y_a)
    rwkv_output(nc, y_a, bonus, z0[13:17], I["prm"], I["bones"], cat0)
    y_b = scratch("y_b", (P, 4, COLS))
    kept_l, kept_m, kept_a = scratch("kl", (P, 32, 16)), scratch("km", (P, 32, 16)), scratch("ka", (P, 2, 32))
    s5_prompt(nc, u, I["s5_par"], I["s5_mats"], I["s5_dcol"], I, y_b, O["s5_p"], kept_l, kept_m, kept_a)
    s5_samples(nc, u[TT, 0:NS, :], I["s5_par"], I["s5_in"], kept_l, kept_m, kept_a, I["s5_drow"], I, y_b, O["s5_s"])
    s5_glu(nc, y_b, z0[17:21], I["glu_w"], I["glu_b"], cat0)
    x1, x1T = scratch("x1", (COLS, D)), scratch("x1T", (P, KT, COLS))
    out_projection(nc, "oe", cat0, I["wo_e"], I["x"], I["ln_g"][0:1], I["ln_b"][0:1], I["ident"], x1, x1T)

    z1, v1 = O["z1"], O["v1"]
    project_channels(nc, "po", x1T, I["w_o"], z1, 21)
    project_tokens(nc, "pv", lambda t, rows: x1T[:, :, ds(t * P, rows)], I["w_v"], 1024, v1)
    cat1 = scratch("cat1", (KT, P, COLS))
    stick_prompt(nc, z1, v1, I["sb_bias"], I, cat1)
    stick_samples(nc, z1, I["cache_k"], I["cache_v"], I["pages"], I["sb_bias"], I, scratch("q_rows", (NS, 512)), cat1)
    gops, gwc, gvecs = scratch("gops", (P, 3, 2, SEQ)), scratch("gwc", (P, 2, NCH)), scratch("gvecs", (3, NS, 256))
    o_d = scratch("o_d", (HD, P, COLS))
    gla_operands(nc, z1, I["alpha_w"], I["alpha_b"], I, gops, gwc, gvecs)
    gla_chunks(nc, gops, v1, gwc, I, o_d, O["gla_p"])
    gla_samples(nc, gvecs, v1[TT, 0:NS, 512:1024], I["state_gla"], I["ident"], O["gla_s"], o_d)
    gla_output(nc, o_d, z1[16:20], I["gla_gn"], I, cat1)
    out_projection(nc, "oo", cat1, I["wo_o"], x1, I["ln_g"][1:2], I["ln_b"][1:2], I["ident"], O["y"], None)


OUTPUTS = {"z0": (21, P, COLS), "rwkv_p": (4, 2, 64, 64), "rwkv_s": (64, 64, 64), "s5_p": (P, 32),
           "s5_s": (P, NS, 32), "z1": (21, P, COLS), "v1": (TT + 1, P, 1024), "gla_p": (P, 2, DV),
           "gla_s": (NS * HD, DK, DV), "y": (COLS, D)}


def constants():
    i = np.arange(P)
    h, t = i // 64, i % 64
    same = h[:, None] == h[None, :]
    before, upto = same & (t[:, None] < t[None, :]), same & (t[:, None] <= t[None, :])
    level = lambda m: (same & (t[:, None] // (2 * m) == t[None, :] // (2 * m))
                       & ((t[:, None] // m) % 2 == 0) & ((t[None, :] // m) % 2 == 1))
    reset = np.ones((P, COLS))
    reset[:, 0:SEQ:CH] = 0
    reset[:, SEQ:] = 0
    jm = np.zeros((P, P))
    jm[64 + np.arange(64), np.arange(64)] = 1
    jm[np.arange(64), 64 + np.arange(64)] = -1
    return {"ident": np.eye(P), "bones": same, "mask4": np.concatenate([before, upto, before, upto], 1),
            "levels": np.stack([level(m) for m in (1, 2, 4, 8, 16, 32)], 1), "reset": reset,
            "neg": np.where(i[None, :] < i[:, None], 0, -1e30), "tri": i[:, None] >= i[None, :],
            "own": np.kron(np.eye(HC), np.ones((1, DC))), "jm": jm,
            "sgn": np.where(i[:, None] < 64, -1, 1)}


def layout(a):
    cat = np.concatenate
    chan = lambda v: v.reshape(-1, P).T
    twice = lambda v: cat([v.T, v.T])
    kpc = lambda w: w.reshape(-1, P, w.shape[-1]).transpose(1, 0, 2)
    tiles = lambda w: w.reshape(KT, P, -1, P).transpose(2, 1, 0, 3)
    x = cat([a["x_prompt"][0], a["x_sample"][:, 0]])
    we, wo = a["w_in_e"][0], a["w_in_o"][0]
    xT = x.T.reshape(KT, P, COLS).transpose(1, 0, 2)
    xT_u = np.zeros((TT + 1, P, KT, P), x.dtype)
    xT_u[:TT] = xT[:, :, :SEQ].reshape(P, KT, 2, P, 8).transpose(2, 4, 0, 1, 3).reshape(TT, P, KT, P)
    xT_u[TT, :, :, :NS] = xT[:, :, SEQ:]
    mu = a["mu_shift"][0]
    vec = lambda n: a[n][0].reshape(-1)
    w2, a2 = np.zeros((2, P, 512), x.dtype)
    w2[:64], a2[64:] = a["rwkv_w2"][0], a["rwkv_a2"][0]
    alpha_w = np.zeros((P, 256), x.dtype)
    alpha_w[:16] = a["gla_alpha_w"][0]
    B = lambda n: a[n][0].transpose(1, 0, 2)
    C = lambda n: a[n][0].transpose(2, 0, 1)
    br, bi, cr, ci = B("s5_b_re"), B("s5_b_im"), C("s5_c_re"), C("s5_c_im")
    hr, hi = (a[n][0].transpose(2, 0, 1) for n in ("state_s5_re", "state_s5_im"))
    e_cols = np.r_[0:2176, 2688:3200]
    o_cols = np.r_[0:1024, 1536:2560, 3088:3600, 3072:3088]
    w_o = np.zeros((D, 21 * P), x.dtype)
    w_o[:, :o_cols.size] = wo[:, o_cols]
    return {
        "xT": xT, "xT_u": xT_u, "x": x, "w_e": tiles(we[:, e_cols]), "w_u": kpc(we[:, 2176:2688]),
        "z_last": a["state_shift"][0].T.reshape(13, P, NS).transpose(1, 0, 2), "mu_low": mu[1536:, None],
        "prm": np.stack([chan(mu[0:512]), chan(mu[512:1024]), chan(mu[1024:1536])] + [chan(vec(n)) for n in (
            "rwkv_w0", "rwkv_a0", "rwkv_k_k", "rwkv_k_a", "rwkv_r_k", "rwkv_gn_g", "rwkv_gn_b")], 2),
        "w2": w2, "a2": a2, "state_rwkv": a["state_rwkv"][0].reshape(64, 64, 64),
        "s5_par": np.stack([twice(a["s5_lambda_re"][0]), twice(a["s5_lambda_im"][0]),
                            np.broadcast_to(a["s5_log_dt"][0], (P, 32))], 1),
        "s5_mats": np.stack([cat([br, bi]), cat([bi, br]), cat([cr, ci]), cat([ci, cr])], 1),
        "s5_dcol": np.tile(a["s5_d"][0].reshape(32, 16).T, (8, 1)), "s5_drow": a["s5_d"],
        "s5_in": np.stack([cat([hr, hi]), cat([hi, hr])], 1), "glu_w": kpc(a["s5_glu_w"][0]),
        "glu_b": chan(vec("s5_glu_b")), "wo_e": kpc(a["w_out_e"][0]), "ln_g": a["ln_g"], "ln_b": a["ln_b"],
        "w_o": tiles(w_o), "w_v": kpc(wo[:, np.r_[1024:1536, 2560:3072]]), "sb_bias": a["sb_bias"],
        "cache_k": a["cache_k"][0].reshape(-1, P, CW), "cache_v": a["cache_v"][0].reshape(-1, P, CW),
        "pages": a["page_table"].reshape(1, -1), "alpha_w": alpha_w, "alpha_b": chan(vec("gla_alpha_b")),
        "state_gla": a["state_gla"][0].reshape(NS * HD, DK, DV), "gla_gn": chan(vec("gla_gn_g")),
        "wo_o": kpc(a["w_out_o"][0])}


def results(r):
    z0, z1, v1, fin, h = r["z0"], r["z1"], r["v1"], r["s5_p"], r["s5_s"]
    z0 = z0[0:13].reshape(13 * P, COLS)
    k = z1[4:8].reshape(CW, COLS).T.reshape(COLS, HC, DC)
    v_p, v_s = v1[0:TT, :, 0:CW].reshape(SEQ, HC, DC), v1[TT, 0:NS, 0:CW].reshape(NS, HC, DC)
    lead = lambda v: v[None]
    return (lead(r["y"][:SEQ]), r["y"][SEQ:][:, None],
            r["rwkv_p"].reshape(1, 1, 8, 64, 64).transpose(0, 1, 2, 4, 3), r["rwkv_s"].reshape(1, NS, 8, 64, 64),
            z0[:, SEQ - 1][None, None], lead(z0[:, SEQ:].T),
            fin[:64].T[None, None], lead(h[:64].transpose(1, 2, 0)), fin[64:].T[None, None],
            lead(h[64:].transpose(1, 2, 0)),
            k[:SEQ][None, None], k[SEQ:][None, :, None], v_p[None, None], v_s[None, :, None],
            r["gla_p"].reshape(2, DK, 2, DV).transpose(2, 0, 1, 3).reshape(1, 1, HD, DK, DV),
            r["gla_s"].reshape(1, NS, HD, DK, DV))


def kernel(**inputs):
    import concourse.bacc as bacc
    from concourse.bass_utils import run_bass_kernel_spmd

    nc = bacc.Bacc("TRN2", target_bir_lowering=False, num_devices=1)
    arrays = {n: np.ascontiguousarray(v) for n, v in layout({n: np.asarray(v) for n, v in inputs.items()}).items()}
    arrays.update({n: np.ascontiguousarray(v.astype(np.float32)) for n, v in constants().items()})
    ins = {n: nc.dram_tensor(f"in_{n}", v.shape, mybir.dt.from_np(v.dtype), kind="ExternalInput").ap()
           for n, v in arrays.items()}
    outs = {n: nc.dram_tensor(f"out_{n}", shape, F32, kind="ExternalOutput").ap() for n, shape in OUTPUTS.items()}
    program(nc, ins, outs)
    r = run_bass_kernel_spmd(nc, [{f"in_{n}": v for n, v in arrays.items()}], core_ids=[0])
    return tuple(np.ascontiguousarray(v) for v in results({n: r.results[0][f"out_{n}"] for n in OUTPUTS}))
```

```python
from contextlib import ExitStack

import numpy as np
import concourse.bass as bass
from concourse import mybir

F32 = mybir.dt.float32
I32 = mybir.dt.int32
F32R = mybir.dt.float32r
ALU = mybir.AluOpType
ACT = mybir.ActivationFunctionType
AX = mybir.AxisListType

P = 128
D = 1024
KT = D // P
SEQ = 2048
NS = 8
COLS = SEQ + NS
TT = SEQ // P
CH = 64
NCH = SEQ // CH
PAGES = 32
BLK = 412
NBLK = -(-COLS // BLK)
ALPHA = 4.0 ** 0.25
LN_EPS = 1e-5
GN_EPS = 64e-5
RMS_EPS = 1e-5
ds = bass.ds
LN_EXP = "natural_log_exp_and_others"


class Chain:

    def __init__(self, eng, sem):
        self.eng, self.sem, self.base, self.n = eng, sem, 0, 0

    def start(self, base):
        self.base, self.n = base, 0

    def __call__(self, ins):
        self.n += 1
        ins.then_inc(self.sem, 1)
        self.eng.wait_ge(self.sem, self.base + self.n)


class Stage:

    def __init__(self, nc, name):
        self.nc, self.name, self.ctx, self.sems = nc, name, ExitStack(), []

    def __enter__(self):
        self.ctx.__enter__()
        return self

    def __exit__(self, *a):
        self.ctx.__exit__(*a)
        self.nc.clear_and_free_semaphores(self.sems)
        self.nc.all_engine_barrier()

    def sb(self, name, shape, dt=F32):
        return self.ctx.enter_context(self.nc.sbuf_tensor(f"{self.name}_{name}", shape, dt))

    def ps(self, name, shape):
        return self.ctx.enter_context(self.nc.psum_tensor(f"{self.name}_{name}", shape, F32))

    def sem(self, name):
        self.sems.append(self.nc.alloc_semaphore(name=f"{self.name}_{name}"))
        return self.sems[-1]

    def block(self):
        return self.ctx.enter_context(self.nc.Block())


def high_part(eng, hi, x):
    return eng.tensor_copy(hi.bitcast(F32R), x)


def low_part(eng, low, x, hi):
    return eng.tensor_tensor(low.bitcast(F32R), x, hi, ALU.subtract)


def product(pe, out, lhs, rhs, start, stop):
    (lh, ll), (rh, rl) = ([t.bitcast(F32R) for t in pair] for pair in (lhs, rhs))
    pe.matmul(out, ll, rh, start=start, stop=False)
    pe.matmul(out, lh, rl, start=False, stop=False)
    return pe.matmul(out, lh, rh, start=False, stop=stop)


def project_channels(nc, name, xT, w, out, n_tiles):
    with Stage(nc, name) as s:
        xh, xl = s.sb("x_high", [P, KT, COLS]), s.sb("x_low", [P, KT, COLS])
        wr, wh, wl = (s.sb(n, [P, 2, KT * P]) for n in ("w", "w_high", "w_low"))
        ot = s.sb("o", [P, 2, COLS])
        acc = s.ps("acc", [P, NBLK, 512])
        x_in = [s.sem(f"x_in{k}") for k in range(KT)]
        x_high = [s.sem(f"x_high{k}") for k in range(KT)]
        x_ready = [s.sem(f"x_ready{k}") for k in range(KT)]
        w_in = [s.sem("w_in0"), s.sem("w_in1")]
        w_high, w_ready = s.sem("w_high"), s.sem("w_ready")
        blk_done, blk_free = s.sem("blk_done"), s.sem("blk_free")
        o_free = [s.sem("o_free0"), s.sem("o_free1")]
        LEAD = 2 * NBLK
        pairs = n_tiles // 2
        assert n_tiles % 2 and n_tiles > 3
        last = n_tiles - 1
        block = s.block()

        at = lambda n, tile: isinstance(n, int) and n == tile

        def loop(eng, step):
            step(0, 0, 0)
            with eng.Fori(0, pairs - 1) as m:
                step(m * 2 + 1, 1, m)
                step(m * 2 + 2, 0, m + 1)
            step(n_tiles - 2, 1, pairs - 1)
            step(last, 0, pairs)

        @block.sync
        def _(sp):
            def step(n, h, m):
                sp.wait_ge(w_ready, n + 1)
                sp.dma_start(wr[:, h], w[ds(n, 1)].rearrange("o p k c -> p (o k c)")).then_inc(w_in[h], 16)
                if at(n, 0):
                    for k in range(KT):
                        if k >= 2:
                            sp.wait_ge(x_ready[k - 2], 1)
                        sp.dma_start(ot[:, k % 2, :], xT[:, k, :]).then_inc(x_in[k], 16)
            loop(sp, step)

        @block.gpsimd
        def _(pool):
            pool.sem_inc(w_ready, 2)
            pool.wait_ge(w_high, 1)
            low_part(pool, wl[:, 0], wr[:, 0], wh[:, 0]).then_inc(w_ready, 1)
            for k in range(1, KT, 3):
                pool.wait_ge(x_high[k], 1)
                low_part(pool, xl[:, k, :], ot[:, k % 2, :], xh[:, k, :]).then_inc(x_ready[k], 1)

            def step(n, h, m):
                if at(n, 0):
                    return
                pool.wait_ge(w_high, n + 1)
                low_part(pool, wl[:, h], wr[:, h], wh[:, h]).then_inc(w_ready, 1)
            loop(pool, step)

        @block.tensor
        def _(pe):
            pe.sem_inc(blk_done, LEAD)

            def part(h, b, k):
                cols, kc = slice(b * BLK, min(COLS, (b + 1) * BLK)), slice(k * P, (k + 1) * P)
                return product(pe, acc[:, b, 0:cols.stop - cols.start], (wh[:, h, kc], wl[:, h, kc]),
                               (xh[:, k, cols], xl[:, k, cols]), k == 0, k == KT - 1)

            def step(n, h, m):
                pe.wait_ge(w_ready, n + 3)
                if at(n, 0):
                    for k in range(KT):
                        pe.wait_ge(x_ready[k], 1)
                        for b in range(NBLK):
                            mm = part(h, b, k)
                            if k == KT - 1:
                                mm.then_inc(blk_done, 1)
                    return
                for b in range(NBLK):
                    pe.wait_ge(blk_free, n * NBLK + b + 1)
                    for k in range(KT):
                        mm = part(h, b, k)
                    mm.then_inc(blk_done, 1)
            loop(pe, step)

        @block.vector
        def _(dve):
            dve.sem_inc(blk_free, NBLK)
            dve.sem_inc(o_free[0], 16)
            dve.sem_inc(o_free[1], 16)
            dve.wait_ge(w_in[0], 16)
            high_part(dve, wh[:, 0], wr[:, 0]).then_inc(w_high, 1)
            for k in range(KT):
                dve.wait_ge(x_in[k], 16)
                high_part(dve, xh[:, k, :], ot[:, k % 2, :]).then_inc(x_high[k], 1)
                if k % 3 != 1:
                    dve.wait_ge(x_high[k], 1)
                    low_part(dve, xl[:, k, :], ot[:, k % 2, :], xh[:, k, :]).then_inc(x_ready[k], 1)

            def step(n, h, m):
                dve.wait_ge(o_free[h], 16 * m + 16)
                for b in range(NBLK):
                    if b == 3 and not at(n, last):
                        dve.wait_ge(w_in[1 - h], 16 * m + 16 + 16 * h)
                        high_part(dve, wh[:, 1 - h], wr[:, 1 - h]).then_inc(w_high, 1)
                    width = min(BLK, COLS - b * BLK)
                    dve.wait_ge(blk_done, LEAD + n * NBLK + b + 1)
                    cp = dve.tensor_copy(ot[:, h, b * BLK:b * BLK + width], acc[:, b, 0:width])
                    cp.then_inc(blk_free, 1)
            loop(dve, step)

        @block.scalar
        def _(act):
            def step(n, h, m):
                act.wait_ge(blk_free, NBLK + (n + 1) * NBLK)
                act.dma_start(out[ds(n, 1)].rearrange("o p c -> p (o c)"), ot[:, h, :]).then_inc(o_free[h], 16)
            loop(act, step)
            act.wait_ge(o_free[0], 16 * (2 + pairs))
            act.wait_ge(o_free[1], 16 * (1 + pairs))


def token_tiles(eng, step):
    with eng.Fori(0, TT // 2) as m:
        for h in (0, 1):
            step(m * 2 + h, h, m, P)
    step(TT, 0, TT // 2, NS)


def project_tokens(nc, name, src, w, width, out):
    halves = width // 512
    with Stage(nc, name) as s:
        wr, wh, wl = (s.sb(n, [P, KT, width]) for n in ("w", "w_high", "w_low"))
        xr, xh, xl = (s.sb(n, [P, 2, KT, P]) for n in ("x", "x_high", "x_low"))
        ot = s.sb("o", [P, 2, width])
        acc = s.ps("acc", [P, 2, halves, 512])
        w_in, w_high = [s.sem(f"w_in{k}") for k in range(KT)], s.sem("w_high")
        w_ready = s.sem("w_ready")
        x_in = [s.sem("x_in0"), s.sem("x_in1")]
        x_high, x_ready = s.sem("x_high"), s.sem("x_ready")
        acc_done, acc_free = s.sem("acc_done"), s.sem("acc_free")
        o_free = [s.sem("o_free0"), s.sem("o_free1")]
        block = s.block()
        flat = lambda t, h: t[:, h].rearrange("p k c -> p (k c)")

        @block.sync
        def _(sp):
            for k in range(KT):
                sp.dma_start(wr[:, k, :], w[:, k, :]).then_inc(w_in[k], 16)

            def step(t, h, u, rows):
                sp.wait_ge(x_ready, t + 1)
                sp.dma_start(xr[:, h, :, 0:rows], src(t, rows)).then_inc(x_in[h], 16)
            token_tiles(sp, step)

        @block.gpsimd
        def _(pool):
            pool.sem_inc(x_ready, 2)
            for k in range(0, KT, 2):
                pool.wait_ge(w_high, k + 1)
                low_part(pool, wl[:, k], wr[:, k], wh[:, k]).then_inc(w_ready, 1)

            def step(t, h, u, rows):
                pool.wait_ge(x_high, t + 1)
                low_part(pool, flat(xl, h), flat(xr, h), flat(xh, h)).then_inc(x_ready, 1)
            token_tiles(pool, step)

        @block.tensor
        def _(pe):
            pe.sem_inc(acc_done, 2)
            pe.wait_ge(w_ready, KT)

            def step(t, h, u, rows):
                pe.wait_ge(x_ready, t + 3)
                pe.wait_ge(acc_free, t + 1)
                for q in range(halves):
                    c = slice(q * 512, q * 512 + 512)
                    for k in range(KT):
                        mm = product(pe, acc[0:rows, h, q, :], (xh[:, h, k, 0:rows], xl[:, h, k, 0:rows]),
                                     (wh[:, k, c], wl[:, k, c]), k == 0, k == KT - 1)
                mm.then_inc(acc_done, 1)
            token_tiles(pe, step)

        @block.vector
        def _(dve):
            dve.sem_inc(acc_free, 2)
            dve.sem_inc(o_free[0], 16)
            dve.sem_inc(o_free[1], 16)
            for k in range(KT):
                dve.wait_ge(w_in[k], 16)
                high_part(dve, wh[:, k], wr[:, k]).then_inc(w_high, 1)
                if k % 2:
                    dve.wait_ge(w_high, k + 1)
                    low_part(dve, wl[:, k], wr[:, k], wh[:, k]).then_inc(w_ready, 1)
            dve.wait_ge(x_in[0], 16)
            high_part(dve, flat(xh, 0), flat(xr, 0)).then_inc(x_high, 1)

            def step(t, h, u, rows):
                if rows == P:
                    dve.wait_ge(x_in[1 - h], 16 * (u + h) + 16)
                    dve.wait_ge(acc_done, t + 2)
                    high_part(dve, flat(xh, 1 - h), flat(xr, 1 - h)).then_inc(x_high, 1)
                dve.wait_ge(acc_done, 2 + t + 1)
                dve.wait_ge(o_free[h], 16 * u + 16)
                cp = dve.tensor_copy(ot[0:rows, h, :], acc[0:rows, h].rearrange("p q c -> p (q c)"))
                cp.then_inc(acc_free, 1)
            token_tiles(dve, step)

        @block.scalar
        def _(act):
            def step(t, h, u, rows):
                act.wait_ge(acc_free, 2 + t + 1)
                act.dma_start(out[ds(t, 1), 0:rows].rearrange("o p c -> p (o c)"),
                              ot[0:rows, h, :]).then_inc(o_free[h], 16)
            token_tiles(act, step)
            act.wait_ge(o_free[0], 16 * (TT // 2 + 2))
            act.wait_ge(o_free[1], 16 * (TT // 2 + 1))


def skewed_tiles(eng, step):
    step(0, 0, 0, P)
    with eng.Fori(0, TT // 2 - 1) as m:
        step(m * 2 + 1, 1, m, P)
        step(m * 2 + 2, 0, m + 1, P)
    step(TT - 1, 1, TT // 2 - 1, P)
    step(TT, 0, TT // 2, NS)


def out_projection(nc, name, catT, w, x_res, gain, shift, ident, y_tok, xT_out):
    both = xT_out is not None
    with Stage(nc, name) as s:
        wr, wh, wl = (s.sb(n, [P, KT, D]) for n in ("w", "w_high", "w_low"))
        idt = s.sb("ident", [P, P])
        g, b = s.sb("gain", [P, D]), s.sb("shift", [P, D])
        cr, ch, cl = (s.sb(n, [P, 2, KT, P]) for n in ("cat", "cat_high", "cat_low"))
        xr, y = s.sb("res", [P, 2, D]), s.sb("y", [P, 2, D])
        st, mv, sd = s.sb("stats", [P, 2, 2, 6]), s.sb("mean_var", [P, 2, 2]), s.sb("std", [P, 2, 2])
        yT = s.sb("yT", [P, 2, KT, P])
        acc, tr = s.ps("acc", [P, 2, 2, 512]), s.ps("tr", [P, 2, 2, 512])
        w_in, w_high, w_ready, cst = [s.sem(f"w_in{k}") for k in range(KT)], s.sem("w_high"), s.sem("w_ready"), s.sem("cst")
        c_in, r_in = [s.sem("c_in0"), s.sem("c_in1")], [s.sem("r_in0"), s.sem("r_in1")]
        c_high, c_ready, r_free = s.sem("c_high"), s.sem("c_ready"), s.sem("r_free")
        acc_done, acc_free = s.sem("acc_done"), s.sem("acc_free")
        var_ready, std_ready, y_ready = s.sem("var_ready"), s.sem("std_ready"), s.sem("y_ready")
        y_free, yT_free = [s.sem("y_free0"), s.sem("y_free1")], [s.sem("yT_free0"), s.sem("yT_free1")]
        tr_done, yT_ready, own = s.sem("tr_done"), s.sem("yT_ready"), s.sem("own")
        block = s.block()
        flat = lambda t, h: t[:, h].rearrange("p k c -> p (k c)")

        @block.sync
        def _(sp):
            def step(t, h, u, rows):
                sp.wait_ge(c_ready, t + 1)
                sp.dma_start(cr[:, h, :, 0:rows],
                             catT[:, :, ds(t * P, rows)].rearrange("k p c -> p k c")).then_inc(c_in[h], 16)
                sp.wait_ge(r_free, t + 1)
                sp.dma_start(xr[0:rows, h, :], x_res[ds(t * P, rows), :]).then_inc(r_in[h], 16)
                if rows == P and isinstance(t, int) and t == 0:
                    for k in range(KT):
                        sp.dma_start(wr[:, k, :], w[:, k, :]).then_inc(w_in[k], 16)
                    for dst, src in ((g[:, :], gain.broadcast_to([P, D])), (b[:, :], shift.broadcast_to([P, D])),
                                     (idt[:, :], ident)):
                        sp.dma_start(dst, src).then_inc(cst, 16)
            skewed_tiles(sp, step)

        @block.gpsimd
        def _(pool):
            pool.sem_inc(c_ready, 2)
            pool.wait_ge(c_high, 1)
            low_part(pool, flat(cl, 0), flat(cr, 0), flat(ch, 0)).then_inc(c_ready, 1)
            for k in range(0, KT, 2):
                pool.wait_ge(w_high, k + 1)
                low_part(pool, wl[:, k], wr[:, k], wh[:, k]).then_inc(w_ready, 1)

            def step(t, h, u, rows):
                if rows == P:
                    pool.wait_ge(c_high, t + 2)
                    low_part(pool, flat(cl, 1 - h), flat(cr, 1 - h), flat(ch, 1 - h)).then_inc(c_ready, 1)
            skewed_tiles(pool, step)

        @block.tensor
        def _(pe):
            pe.sem_inc(acc_done, 2)
            pe.wait_ge(w_ready, KT)
            pe.wait_ge(cst, 48)

            def transpose(t, h, rows):
                pe.wait_ge(y_ready, t + 1)
                pe.wait_ge(yT_ready, t + 1)
                for k in range(KT):
                    mm = pe.transpose(tr[:, h, k // 4, (k % 4) * P:(k % 4) * P + rows],
                                      y[0:rows, h, k * P:(k + 1) * P], idt[0:rows, 0:rows])
                mm.then_inc(tr_done, 1)

            def step(t, h, u, rows):
                pe.wait_ge(c_ready, t + 3)
                pe.wait_ge(acc_free, t + 1)
                for q in range(2):
                    c = slice(q * 512, q * 512 + 512)
                    for k in range(KT):
                        mm = product(pe, acc[0:rows, h, q, :], (ch[:, h, k, 0:rows], cl[:, h, k, 0:rows]),
                                     (wh[:, k, c], wl[:, k, c]), k == 0, k == KT - 1)
                mm.then_inc(acc_done, 1)
                if both and not (isinstance(t, int) and t == 0):
                    transpose(t - 1, 1 - h, P)
            skewed_tiles(pe, step)
            if both:
                transpose(TT, 0, NS)

        K = 6

        @block.vector
        def _(dve):
            link = Chain(dve, own)
            dve.sem_inc(acc_free, 2)
            dve.sem_inc(r_free, 2)
            dve.wait_ge(c_in[0], 16)
            high_part(dve, flat(ch, 0), flat(cr, 0)).then_inc(c_high, 1)
            for k in range(KT):
                dve.wait_ge(w_in[k], 16)
                high_part(dve, wh[:, k], wr[:, k]).then_inc(w_high, 1)
                if k % 2:
                    dve.wait_ge(w_high, k + 1)
                    low_part(dve, wl[:, k], wr[:, k], wh[:, k]).then_inc(w_ready, 1)
            dve.wait_ge(cst, 48)

            def step(t, h, u, rows):
                link.start(t * K)
                if rows == P:
                    dve.wait_ge(c_in[1 - h], 16 * (u + h) + 16)
                    dve.wait_ge(acc_done, t + 2)
                    high_part(dve, flat(ch, 1 - h), flat(cr, 1 - h)).then_inc(c_high, 1)
                dve.wait_ge(acc_done, 2 + t + 1)
                dve.wait_ge(r_in[h], 16 * u + 16)
                dve.wait_ge(y_free[h], 16 * u + 16)
                r = slice(0, rows)
                link(dve.scalar_tensor_tensor(out=y[r, h, :], in0=xr[r, h, :], scalar=ALPHA,
                                              in1=acc[r, h].rearrange("p q c -> p (q c)"),
                                              op0=ALU.mult, op1=ALU.add))
                dve.bn_stats(st[r, h, 0, :], y[r, h, 0:512])
                link(dve.bn_stats(st[r, h, 1, :], y[r, h, 512:1024]))
                dve.sem_inc(acc_free, 1)
                dve.sem_inc(r_free, 1)
                link(dve.bn_aggr(mv[r, h, :], st[r, h].rearrange("p a b -> p (a b)")))
                dve.tensor_scalar(sd[r, h, 0:1], mv[r, h, 1:2], LN_EPS, None, ALU.add).then_inc(var_ready, 1)
                dve.wait_ge(std_ready, t + 1)
                link(dve.reciprocal(sd[r, h, 0:1], sd[r, h, 1:2]))
                link(dve.tensor_scalar(y[r, h, :], y[r, h, :], mv[r, h, 0:1], sd[r, h, 0:1],
                                       ALU.subtract, ALU.mult))
                link(dve.tensor_tensor(y[r, h, :], y[r, h, :], g[r, :], ALU.mult))
                assert link.n == K
                dve.tensor_tensor(y[r, h, :], y[r, h, :], b[r, :], ALU.add).then_inc(y_ready, 1)
            skewed_tiles(dve, step)

        @block.scalar
        def _(act):
            for q in (0, 1):
                act.sem_inc(y_free[q], 16)
                act.sem_inc(yT_free[q], 16)
            act.sem_inc(yT_ready, 2)

            def flipped(t, h, u, rows):
                act.wait_ge(tr_done, t + 1)
                act.wait_ge(yT_free[h], 16 * u + 16)
                act.copy(yT[:, h, :, 0:rows],
                         tr[:, h].rearrange("p q (k c) -> p (q k) c", c=P)[:, :, 0:rows]).then_inc(yT_ready, 1)
                act.wait_ge(yT_ready, t + 3)
                act.dma_start(xT_out[:, :, ds(t * P, rows)], yT[:, h, :, 0:rows]).then_inc(yT_free[h], 16)

            def step(t, h, u, rows):
                r = slice(0, rows)
                act.wait_ge(var_ready, t + 1)
                act.activation(sd[r, h, 1:2], sd[r, h, 0:1], ACT.Sqrt).then_inc(std_ready, 1)
                if both and not (isinstance(t, int) and t == 0):
                    flipped(t - 1, 1 - h, u if h else u - 1, P)
                act.wait_ge(y_ready, t + 1)
                act.dma_start(y_tok[ds(t * P, rows), :], y[0:rows, h, :]).then_inc(y_free[h], 16)
            skewed_tiles(act, step)
            if both:
                flipped(TT, 0, TT // 2, NS)
            for q in (0, 1):
                act.wait_ge(y_free[q], 16 * (TT // 2 + 2 - q))
                if both:
                    act.wait_ge(yT_free[q], 16 * (TT // 2 + 2 - q))


A_T, R_T, B_T, K_T, V_, B_H, K_H = range(7)
MU_R, MU_K, MU_V, W0, A0, KK_, KA_, RK_, GN_G, GN_B = range(10)
S_R, S_W, S_B, S_K, S_A, S_V = range(6)
NEG_EXP_HALF = -float(np.exp(-0.5))


def rwkv_operands(nc, z, z_last, mu_low, prm, w2, a2, const, ops, wc, bonus, sample_vecs):
    with Stage(nc, "rp") as s:
        big = lambda n: s.sb(n, [P, COLS])
        low, mask = big("low"), big("mask")
        r, k, v, t1, t2, t3, a, ld, c = (big(n) for n in ("r", "k", "v", "t1", "t2", "t3", "a", "ld", "c"))
        ep, en, ec, kk, kp, ka, rk = (big(n) for n in ("ep", "en", "ec", "kk", "kp", "ka", "rk"))
        pr = s.sb("prm", [P, 4, 10])
        pj = s.sb("prj", [P, 10])
        omka = s.sb("omka", [P, 1])
        mul = s.sb("mul", [P, 1])
        w2t, a2t, ones, idt = s.sb("w2", [P, 512]), s.sb("a2", [P, 512]), s.sb("ones", [P, P]), s.sb("id", [P, P])
        w2j, a2j = s.sb("w2j", [P, P]), s.sb("a2j", [P, P])
        vec = s.sb("vec", [P, 16, NS])
        vecT = s.sb("vecT", [6 * NS, P])
        wce = s.sb("wce", [P, NCH])
        acc = s.ps("acc", [P, NBLK, 512])
        acb = s.ps("acb", [P, 2, 512])
        trp = s.ps("trp", [P, 512])
        names = ("cst", "low_in", "low_z", "low_t", "zin", "pool_d", "rkv", "mm", "mm_free", "scan", "pool_cw",
                 "sq", "ce", "exps", "kkp", "rkr", "bmm", "bfree", "pout", "dout", "vecs", "vtr", "vst",
                 "stored", "own", "lora", "init", "held")
        q = {n: s.sem(n) for n in names}
        blocks = [(b * BLK, min(BLK, COLS - b * BLK)) for b in range(NBLK)]
        block = s.block()
        NST = 10

        @block.sync
        def _(sp):
            for dst, src in ((pr[:, :, :], prm), (mul[:, :], mu_low), (w2t[:, :], w2), (a2t[:, :], a2),
                             (ones[:, :], const["bones"]), (idt[:, :], const["ident"]), (mask[:, :], const["reset"])):
                sp.dma_start(dst, src).then_inc(q["cst"], 16)
            sp.wait_ge(q["init"], 1)
            sp.dma_start(low[:, :], z[12]).then_inc(q["low_in"], 16)
            sp.dma_start(c[:, 1:SEQ], z[12][:, 0:SEQ - 1]).then_inc(q["low_in"], 16)
            sp.dma_start(c[:, SEQ:COLS], z_last[:, 12, :]).then_inc(q["low_in"], 16)
            with sp.Fori(0, 4) as j:
                sp.wait_ge(q["stored"], j * 16 * NST)
                for n, (t, d) in enumerate(((r, t1), (k, t2), (v, t3))):
                    sp.dma_start(t[:, :], z[ds(j + 4 * n, 1)].rearrange("o p c -> p (o c)")).then_inc(q["zin"], 16)
                    sp.dma_start(d[:, 1:SEQ], z[ds(j + 4 * n, 1), :, 0:SEQ - 1]
                                 .rearrange("o p c -> p (o c)")).then_inc(q["zin"], 16)
                    sp.dma_start(d[:, SEQ:COLS], z_last[:, ds(j + 4 * n, 1), :]
                                 .rearrange("p o c -> p (o c)")).then_inc(q["zin"], 16)

                def store(n, t):
                    sp.sem_inc(q["held"], 1)
                    sp.dma_start(ops[:, n, ds(j, 1), :].rearrange("p o c -> p (o c)"),
                                 t[:, 0:SEQ]).then_inc(q["stored"], 16)
                sp.wait_ge(q["rkv"], 3 * j + 3)
                store(V_, v)
                sp.wait_ge(q["exps"], 5 * j + 5)
                sp.sem_inc(q["held"], 1)
                sp.dma_start(wc[:, ds(j, 1), :].rearrange("p o c -> p (o c)"), wce[:, :]).then_inc(q["stored"], 16)
                sp.wait_ge(q["dout"], 4 * j + 1)
                store(A_T, t3)
                sp.wait_ge(q["dout"], 4 * j + 2)
                store(B_T, t1)
                sp.wait_ge(q["pout"], 3 * j + 1)
                store(R_T, ep)
                sp.wait_ge(q["dout"], 4 * j + 3)
                store(B_H, ka)
                sp.wait_ge(q["pout"], 3 * j + 2)
                store(K_T, en)
                sp.wait_ge(q["dout"], 4 * j + 4)
                sp.sem_inc(q["held"], 1)
                sp.dma_start(bonus[ds(j, 1)].rearrange("o p c -> p (o c)"), ld[:, :]).then_inc(q["stored"], 16)
                sp.wait_ge(q["pout"], 3 * j + 3)
                store(K_H, ec)
                sp.wait_ge(q["vst"], j + 1)
                sp.sem_inc(q["held"], 1)
                sp.dma_start(sample_vecs[:, :, ds(j * P, P)].rearrange("v b c -> (v b) c"),
                             vecT[:, :]).then_inc(q["stored"], 16)
            sp.wait_ge(q["stored"], 4 * 16 * NST)

        @block.tensor
        def _(pe):
            pe.sem_inc(q["mm_free"], NBLK)
            pe.sem_inc(q["bfree"], 2)
            pe.wait_ge(q["cst"], 7 * 16)
            pe.wait_ge(q["low_t"], 1)
            with pe.Fori(0, 4) as j:
                def product(n, w, x):
                    for b, (at, width) in enumerate(blocks):
                        pe.wait_ge(q["mm_free"], j * 3 * NBLK + n * NBLK + b + 1)
                        pe.matmul(acc[:, b, 0:width], w, x[:, at:at + width], start=True,
                                  stop=True).then_inc(q["mm"], 1)
                pe.wait_ge(q["lora"], 2 * j + 2)
                product(0, w2j[:, :], low)
                product(1, a2j[:, :], low)
                pe.wait_ge(q["sq"], j + 1)
                product(2, ones[:, :], t1)
                pe.wait_ge(q["rkr"], j + 1)
                for b, (at, width) in enumerate(blocks):
                    pe.wait_ge(q["bfree"], j * NBLK + b + 1)
                    pe.matmul(acb[:, b % 2, 0:width], ones[:, :], rk[:, at:at + width], start=True,
                              stop=True).then_inc(q["bmm"], 1)
                pe.wait_ge(q["vecs"], j + 1)
                pe.transpose(trp[:, 0:P], vec[:, :, :].rearrange("p v b -> p (v b)"),
                             idt[:, :]).then_inc(q["vtr"], 1)

        @block.scalar
        def _(act):
            act.wait_ge(q["cst"], 7 * 16)
            act.wait_ge(q["low_z"], 1)
            act.activation(low[0:64, :], low[0:64, :], ACT.Tanh).then_inc(q["low_t"], 1)
            with act.Fori(0, 4) as j:

                def blocks_of(n, func, dst, bias):
                    for b, (at, width) in enumerate(blocks):
                        act.wait_ge(q["mm"], j * 3 * NBLK + n * NBLK + b + 1)
                        act.activation(dst[:, at:at + width], acc[:, b, 0:width], func,
                                       bias=bias).then_inc(q["mm_free"], 1)
                act.wait_ge(q["rkv"], 3 * j + 3)
                blocks_of(0, ACT.Sigmoid, ld, pj[:, W0:W0 + 1])
                blocks_of(1, ACT.Sigmoid, a, pj[:, A0:A0 + 1])
                act.activation(t1[:, :], k[:, :], ACT.Square, scale=pj[:, KK_:KK_ + 1]).then_inc(q["sq"], 1)
                blocks_of(2, ACT.Sqrt, t2, 0.0)
                act.wait_ge(q["scan"], j + 1)
                act.activation(ep[:, :], c[:, :], ACT.Exp).then_inc(q["exps"], 1)
                act.activation(en[:, :], c[:, :], ACT.Exp, scale=-1.0).then_inc(q["exps"], 1)
                act.wait_ge(q["pool_cw"], j + 1)
                act.activation(t3[:, :], t3[:, :], ACT.Exp).then_inc(q["exps"], 1)
                act.wait_ge(q["ce"], j + 1)
                act.activation(ec[:, :], ec[:, :], ACT.Exp).then_inc(q["exps"], 1)
                act.activation(wce[:, :], c[:, CH - 1:SEQ:CH], ACT.Exp).then_inc(q["exps"], 1)
                act.wait_ge(q["vtr"], j + 1)
                act.copy(vecT[:, :], trp[0:6 * NS, 0:P]).then_inc(q["vst"], 1)

        @block.vector
        def _(dve):
            link = Chain(dve, q["own"])
            link.start(0)
            dve.memset(c[:, 0:1], 0.0)
            link(dve.memset(vec[:, :, :], 0.0))
            dve.sem_inc(q["init"], 1)
            dve.wait_ge(q["cst"], 7 * 16)
            dve.wait_ge(q["low_in"], 48)
            link(dve.tensor_tensor(c[:, :], c[:, :], low[:, :], ALU.subtract))
            dve.scalar_tensor_tensor(out=low[:, :], in0=c[:, :], scalar=mul[:, 0:1], in1=low[:, :],
                                     op0=ALU.mult, op1=ALU.add).then_inc(q["low_z"], 1)
            FIRST, K = 2, 11
            assert link.n == FIRST
            with dve.Fori(0, 4) as j:
                link.start(FIRST + j * K)
                dve.wait_ge(q["stored"], j * 16 * NST)
                link(dve.tensor_copy(pj[:, :], pr[:, ds(j, 1), :].rearrange("p o c -> p (o c)")))
                link(dve.tensor_scalar(omka[:, :], pj[:, KA_:KA_ + 1], -1.0, 1.0, ALU.mult, ALU.add))
                dve.tensor_copy(w2j[:, :], w2t[:, ds(j * P, P)]).then_inc(q["lora"], 1)
                dve.tensor_copy(a2j[:, :], a2t[:, ds(j * P, P)]).then_inc(q["lora"], 1)
                for n, (t, d) in enumerate(((r, t1), (k, t2), (v, t3))):
                    dve.wait_ge(q["pool_d"], 3 * j + n + 1)
                    dve.scalar_tensor_tensor(out=t[:, :], in0=d[:, :], scalar=pj[:, MU_R + n:MU_R + n + 1], in1=t[:, :],
                                             op0=ALU.mult, op1=ALU.add).then_inc(q["rkv"], 1)
                dve.wait_ge(q["mm_free"], NBLK + j * 3 * NBLK + NBLK)
                link(dve.tensor_scalar(ld[:, :], ld[:, :], NEG_EXP_HALF, None, ALU.mult))
                dve.tensor_tensor_scan(c[:, :], mask[:, :], ld[:, :], 0.0, ALU.mult,
                                       ALU.add).then_inc(q["scan"], 1)
                dve.wait_ge(q["scan"], j + 1)
                ends = c[:, CH - 1:SEQ:CH].rearrange("p (n o) -> p n o", o=1).broadcast_to([P, NCH, CH])
                link(dve.tensor_tensor(ec[:, 0:SEQ].rearrange("p (n t) -> p n t", t=CH), ends,
                                       c[:, 0:SEQ].rearrange("p (n t) -> p n t", t=CH), ALU.subtract))
                dve.memset(ec[:, SEQ:COLS], 0.0).then_inc(q["ce"], 1)
                dve.wait_ge(q["mm_free"], NBLK + j * 3 * NBLK + 2 * NBLK)
                link(dve.tensor_scalar(kp[:, :], a[:, :], pj[:, KA_:KA_ + 1], omka[:, 0:1], ALU.mult, ALU.add))
                link(dve.tensor_tensor(kp[:, :], k[:, :], kp[:, :], ALU.mult))
                dve.scalar_tensor_tensor(out=rk[:, :], in0=r[:, :], scalar=pj[:, RK_:RK_ + 1], in1=kp[:, :],
                                         op0=ALU.mult, op1=ALU.mult).then_inc(q["rkr"], 1)
                dve.wait_ge(q["mm_free"], NBLK + j * 3 * NBLK + 3 * NBLK)
                link(dve.tensor_scalar(t2[:, :], t2[:, :], 1e-12, None, ALU.max))
                link(dve.reciprocal(t2[:, :], t2[:, :]))
                link(dve.scalar_tensor_tensor(out=kk[:, :], in0=k[:, :], scalar=pj[:, KK_:KK_ + 1], in1=t2[:, :],
                                              op0=ALU.mult, op1=ALU.mult))
                link(dve.tensor_tensor(ka[:, :], kk[:, :], a[:, :], ALU.mult))
                dve.sem_inc(q["kkp"], 1)
                dve.wait_ge(q["exps"], 5 * j + 5)
                dve.tensor_copy(vec[:, S_R, :], r[:, SEQ:COLS])
                link(dve.tensor_copy(vec[:, S_W, :], ep[:, SEQ:COLS]))
                dve.sem_inc(q["kkp"], 1)
                dve.scalar_tensor_tensor(out=t3[:, :], in0=kk[:, :], scalar=-1.0, in1=t3[:, :],
                                         op0=ALU.mult, op1=ALU.mult).then_inc(q["dout"], 1)
                dve.tensor_tensor(t1[:, :], ka[:, :], en[:, :], ALU.mult).then_inc(q["dout"], 1)
                dve.wait_ge(q["dout"], 4 * j + 2)
                dve.tensor_copy(vec[:, S_B, :], ka[:, SEQ:COLS])
                dve.tensor_copy(vec[:, S_K, :], kp[:, SEQ:COLS])
                dve.tensor_copy(vec[:, S_A, :], t3[:, SEQ:COLS])
                dve.tensor_copy(vec[:, S_V, :], v[:, SEQ:COLS]).then_inc(q["vecs"], 1)
                dve.wait_ge(q["vecs"], j + 1)
                dve.tensor_tensor(ka[:, :], ka[:, :], ec[:, :], ALU.mult).then_inc(q["dout"], 1)
                for b, (at, width) in enumerate(blocks):
                    dve.wait_ge(q["bmm"], j * NBLK + b + 1)
                    cp = dve.tensor_tensor(ld[:, at:at + width], acb[:, b % 2, 0:width], v[:, at:at + width],
                                           ALU.mult)
                    if b < NBLK - 1:
                        cp.then_inc(q["bfree"], 1)
                    else:
                        cp.then_inc(q["dout"], 1)
                dve.wait_ge(q["dout"], 4 * j + 4)
                dve.sem_inc(q["bfree"], 1)
                assert link.n == K, link.n

        @block.gpsimd
        def _(pool):
            with pool.Fori(0, 4) as j:
                pool.wait_ge(q["zin"], 144 * j + 144)
                for t, d in ((r, t1), (k, t2), (v, t3)):
                    pool.tensor_tensor(d[:, 1:COLS], d[:, 1:COLS], t[:, 1:COLS], ALU.subtract)
                    pool.tensor_scalar(d[:, 0:1], t[:, 0:1], -1.0, None, ALU.mult).then_inc(q["pool_d"], 1)
                pool.wait_ge(q["rkv"], 3 * j + 3)
                pool.wait_ge(q["scan"], j + 1)
                pool.tensor_tensor(t3[:, :], c[:, :], ld[:, :], ALU.subtract).then_inc(q["pool_cw"], 1)
                pool.wait_ge(q["kkp"], 2 * j + 2)
                pool.tensor_tensor(ep[:, :], r[:, :], ep[:, :], ALU.mult).then_inc(q["pout"], 1)
                pool.wait_ge(q["dout"], 4 * j + 2)
                pool.tensor_tensor(en[:, :], kp[:, :], en[:, :], ALU.mult).then_inc(q["pout"], 1)
                pool.wait_ge(q["dout"], 4 * j + 3)
                pool.tensor_tensor(ec[:, :], kp[:, :], ec[:, :], ALU.mult).then_inc(q["pout"], 1)


LEVELS = 5


def rwkv_chunks(nc, ops, wc, const, y, s_out):
    COUNT = dict(ops_in=32, m4_pe=4, m4=4, tm_pe=4, tm=4, ct=LEVELS, xt_sb=LEVELS + 1, xt_pe=LEVELS,
                 x_pe=LEVELS, x_sb=LEVELS, u_pe=LEVELS, u_sb=LEVELS, w_pe=1, w_sb=1, gh_pe=2, gh_sb=2,
                 g5_pe=2, rp=2, mt=4, y_pe=1, s_pe=1, y_sb=1, y_st=16, own=1)
    with Stage(nc, "rc") as s:
        two = lambda n, shape: [s.sb(f"{n}{q}", shape) for q in (0, 1)]
        opx = two("opx", [P, 7, 4, P])
        m4 = two("m4", [P, 4, 4, P])
        aw = two("aw", [P, 4, 2, P])
        vbk = two("vbk", [P, 4, 3, P])
        ct = two("ct", [P, LEVELS, 4, P])
        xt = two("xt", [P, 2, 4, P])
        xx = two("xx", [P, 4, P])
        uu = two("uu", [P, 4, P])
        gh = two("gh", [P, 4, 2, P])
        rpt = two("rpt", [P, 4, P])
        mt = two("mt", [P, 4, P])
        yb = two("yb", [P, 4, CH])
        st = two("st", [P, 4, P])
        mask4 = s.sb("mask4", [P, 4 * P])
        lev = s.sb("lev", [P, 6, P])
        idt = s.sb("id", [P, P])
        wct = s.sb("wc", [P, 4, NCH])
        bank = [[s.ps(f"bank{q}{n}", [P, 512]) for n in range(4)] for q in (0, 1)]
        sem = {n: [s.sem(f"{n}{q}") for q in (0, 1)] for n in COUNT}
        cst, zero, s_sb, s_st = s.sem("cst"), s.sem("zero"), s.sem("s_sb"), s.sem("s_st")
        block = s.block()

        def wait(eng, name, q, m, k):
            eng.wait_ge(sem[name][q], m * COUNT[name] + k)

        four = lambda ap: ap.rearrange("p (j c) -> p j c", j=4)
        every = lambda ap, n: ap.rearrange("p (o c) -> p o c", o=1).broadcast_to([P, n, P])

        @block.sync
        def _(sp):
            for dst, src in ((mask4[:, :], const["mask4"]), (lev[:, :, :], const["levels"]),
                             (idt[:, :], const["ident"]), (wct[:, :, :], wc)):
                sp.dma_start(dst, src).then_inc(cst, 16)
            sp.wait_ge(zero, 4)
            with sp.Fori(0, NCH // 2) as m:
                for q in (0, 1):
                    wait(sp, "mt", q, m, 0)
                    for h in (0, 1):
                        r = slice(64 * h, 64 * h + 64)
                        sp.dma_start(opx[q][r, :, :, r].rearrange("p n j c -> p (n j) c"),
                                     ops[r, :, :, ds((m * 2 + q) * CH, CH)].rearrange("p n j c -> p (n j) c")
                                     ).then_inc(sem["ops_in"][q], 16)
            sp.wait_ge(s_sb, NCH + 1)
            for h in (0, 1):
                r = slice(64 * h, 64 * h + 64)
                sp.dma_start(s_out[:, h].rearrange("j k v -> k j v"), st[0][r, :, r]).then_inc(s_st, 16)
            sp.wait_ge(s_st, 32)

        @block.tensor
        def _(pe):
            pe.wait_ge(cst, 64)
            with pe.Fori(0, NCH // 2) as m:
                for q in (0, 1):
                    wait(pe, "ops_in", q, m, 32)
                    wait(pe, "y_sb", q, m, 0)
                    wait(pe, "rp", q, m, 0)
                    wait(pe, "mt", q, m, 0)
                    pe.wait_ge(s_sb, m * 2 + q)
                    for j in range(4):
                        ar = opx[q][:, A_T:R_T + 1, j, :]
                        pe.matmul(bank[q][j][:, 0:256], opx[q][:, B_T, j, :], ar, start=True, stop=True)
                        pe.matmul(bank[q][j][:, 256:512], opx[q][:, K_T, j, :], ar, start=True,
                                  stop=True).then_inc(sem["m4_pe"][q], 1)
                for q in (0, 1):
                    for j in range(4):
                        wait(pe, "m4", q, m, j + 1)
                        for n, o in enumerate((A_T, V_, B_H, K_H)):
                            mm = pe.transpose(bank[q][j][:, n * P:(n + 1) * P], opx[q][:, o, j, :], idt[:, :])
                        mm.then_inc(sem["tm_pe"][q], 1)
                for q in (0, 1):
                    wait(pe, "xt_sb", q, m, 1)
                    wait(pe, "tm", q, m, 4)
                    for j in range(4):
                        mm = pe.transpose(bank[q][0][:, j * P:(j + 1) * P], xt[q][:, 0, j, :], idt[:, :])
                    mm.then_inc(sem["x_pe"][q], 1)
                    for j in range(4):
                        mm = pe.matmul(bank[q][3][:, j * P:(j + 1) * P], m4[q][:, j, 2, :], vbk[q][:, j, 0, :],
                                       start=True, stop=True)
                    mm.then_inc(sem["w_pe"][q], 1)
                for n in range(LEVELS):
                    for q in (0, 1):
                        wait(pe, "x_sb", q, m, n + 1)
                        wait(pe, "ct", q, m, n + 1)
                        for j in range(4):
                            mm = pe.matmul(bank[q][0][:, j * P:(j + 1) * P], ct[q][:, n, j, :], xx[q][:, j, :],
                                           start=True, stop=True)
                        mm.then_inc(sem["u_pe"][q], 1)
                    for q in (0, 1):
                        wait(pe, "u_sb", q, m, n + 1)
                        wait(pe, "xt_sb", q, m, n + 1)
                        for j in range(4):
                            mm = pe.matmul(bank[q][2][:, j * P:(j + 1) * P], uu[q][:, j, :], xt[q][:, n % 2, j, :],
                                           start=True, stop=True)
                        mm.then_inc(sem["xt_pe"][q], 1)
                        if n < LEVELS - 1:
                            for j in range(4):
                                mm = pe.matmul(bank[q][1][:, j * P:(j + 1) * P], xt[q][:, n % 2, j, :],
                                               uu[q][:, j, :], start=True, stop=True)
                            mm.then_inc(sem["x_pe"][q], 1)
                for q in (0, 1):
                    wait(pe, "xt_sb", q, m, LEVELS + 1)
                    wait(pe, "w_sb", q, m, 1)
                    for j in range(4):
                        mm = pe.matmul(bank[q][j // 2][:, (j % 2) * 256:(j % 2) * 256 + 256],
                                       xt[q][:, LEVELS % 2, j, :], aw[q][:, j, :, :], start=True, stop=True)
                        if j % 2:
                            mm.then_inc(sem["gh_pe"][q], 1)
                for q in (0, 1):
                    for j in range(4):
                        wait(pe, "gh_sb", q, m, j // 2 + 1)
                        at = (j % 2) * 256
                        pe.matmul(bank[q][2 + j // 2][:, at:at + P], gh[q][:, j, 0, :], m4[q][:, j, 1, :],
                                  start=True, stop=True)
                        mm = pe.matmul(bank[q][2 + j // 2][:, at + P:at + 2 * P], gh[q][:, j, 0, :],
                                       vbk[q][:, j, 1, :], start=True, stop=True)
                        if j % 2:
                            mm.then_inc(sem["g5_pe"][q], 1)
                for q in (0, 1):
                    wait(pe, "rp", q, m, 2)
                    wait(pe, "mt", q, m, 4)
                    pe.wait_ge(s_sb, m * 2 + q + 1)
                    for j in range(4):
                        o = bank[q][1][:, j * P:(j + 1) * P]
                        pe.matmul(o, vbk[q][:, j, 1, :], gh[q][:, j, 1, :], start=True, stop=False)
                        pe.matmul(o, vbk[q][:, j, 2, :], vbk[q][:, j, 0, :], start=False, stop=False)
                        mm = pe.matmul(o, mt[q][:, j, :], st[q][:, j, :], start=False, stop=True)
                    mm.then_inc(sem["s_pe"][q], 1)
                    for j in range(4):
                        o = bank[q][0][:, j * P:(j + 1) * P]
                        pe.matmul(o, gh[q][:, j, 1, :], m4[q][:, j, 1, :], start=True, stop=False)
                        pe.matmul(o, vbk[q][:, j, 0, :], m4[q][:, j, 3, :], start=False, stop=False)
                        mm = pe.matmul(o, st[q][:, j, :], rpt[q][:, j, :], start=False, stop=True)
                    mm.then_inc(sem["y_pe"][q], 1)

        @block.scalar
        def _(act):
            with act.Fori(0, NCH // 2) as m:
                for q in (0, 1):
                    wait(act, "y_pe", q, m, 0)
                    for j in range(4):
                        wait(act, "tm_pe", q, m, j + 1)
                        act.copy(aw[q][:, j, 0, :], bank[q][j][:, 0:P])
                        act.copy(vbk[q][:, j].rearrange("p n c -> p (n c)"),
                                 bank[q][j][:, P:4 * P]).then_inc(sem["tm"][q], 1)
                for q in (0, 1):
                    wait(act, "w_pe", q, m, 1)
                    act.copy(aw[q][:, :, 1, :], four(bank[q][3][:, :])).then_inc(sem["w_sb"][q], 1)
                for n in range(LEVELS):
                    for q in (0, 1):
                        wait(act, "u_pe", q, m, n + 1)
                        act.copy(uu[q][:, :, :], four(bank[q][0][:, :])).then_inc(sem["u_sb"][q], 1)
                for q in (0, 1):
                    for h in (0, 1):
                        wait(act, "gh_pe", q, m, h + 1)
                        act.copy(gh[q][:, 2 * h:2 * h + 2].rearrange("p j n c -> p (j n c)"),
                                 bank[q][h][:, :]).then_inc(sem["gh_sb"][q], 1)
                for q in (0, 1):
                    wait(act, "y_pe", q, m, 1)
                    wait(act, "y_st", q, m, 0)
                    act.copy(yb[q][0:64, :, :], four(bank[q][0][0:64, :])[:, :, 0:64])
                    act.copy(yb[q][64:128, :, :], four(bank[q][0][64:128, :])[:, :, 64:128]
                             ).then_inc(sem["y_sb"][q], 1)
                    wait(act, "y_sb", q, m, 1)
                    act.dma_start(y[:, :, ds((m * 2 + q) * CH, CH)], yb[q][:, :, :]).then_inc(sem["y_st"][q], 16)
            for q in (0, 1):
                act.wait_ge(sem["y_st"][q], 16 * NCH // 2)

        @block.vector
        def _(dve):
            dve.memset(opx[0][:, :, :, :], 0.0).then_inc(zero, 1)
            dve.memset(opx[1][:, :, :, :], 0.0).then_inc(zero, 1)
            dve.memset(st[1][:, :, :], 0.0).then_inc(zero, 1)
            dve.memset(st[0][:, :, :], 0.0).then_inc(zero, 1)
            dve.wait_ge(zero, 4)
            dve.sem_inc(s_sb, 1)
            dve.wait_ge(cst, 64)
            with dve.Fori(0, NCH // 2) as m:
                for q in (0, 1):
                    wait(dve, "y_pe", q, m, 0)
                    for j in range(4):
                        wait(dve, "m4_pe", q, m, j + 1)
                        dve.tensor_tensor(m4[q][:, j].rearrange("p n c -> p (n c)"), bank[q][j][:, :],
                                          mask4[:, :], ALU.mult).then_inc(sem["m4"][q], 1)
                for q in (0, 1):
                    wait(dve, "m4", q, m, 4)
                    dve.tensor_tensor(xt[q][:, 0], m4[q][:, :, 0, :], every(lev[:, 0, :], 4),
                                      ALU.mult).then_inc(sem["own"][q], 1)
                    wait(dve, "own", q, m, 1)
                    dve.tensor_tensor(xt[q][:, 0], xt[q][:, 0], every(idt[:, :], 4),
                                      ALU.add).then_inc(sem["xt_sb"][q], 1)
                for q in (0, 1):
                    wait(dve, "x_pe", q, m, 1)
                    dve.tensor_copy(xx[q][:, :, :], four(bank[q][0][:, :])).then_inc(sem["x_sb"][q], 1)
                for n in range(LEVELS):
                    for q in (0, 1):
                        wait(dve, "xt_pe", q, m, n + 1)
                        wait(dve, "xt_sb", q, m, n + 1)
                        dve.tensor_tensor(xt[q][:, (n + 1) % 2], xt[q][:, n % 2], four(bank[q][2][:, :]),
                                          ALU.add).then_inc(sem["xt_sb"][q], 1)
                        if n < LEVELS - 1:
                            wait(dve, "x_pe", q, m, n + 2)
                            wait(dve, "x_sb", q, m, n + 1)
                            dve.tensor_tensor(xx[q][:, :, :], xx[q][:, :, :], four(bank[q][1][:, :]),
                                              ALU.add).then_inc(sem["x_sb"][q], 1)
                for q in (0, 1):
                    for h in (0, 1):
                        wait(dve, "g5_pe", q, m, h + 1)
                        b = bank[q][2 + h][:, :].rearrange("p (j n c) -> p j n c", j=2, n=2)
                        dve.tensor_tensor(rpt[q][:, 2 * h:2 * h + 2, :], opx[q][:, R_T, 2 * h:2 * h + 2, :],
                                          b[:, :, 0, :], ALU.add).then_inc(sem["rp"][q], 1)
                        for j in (0, 1):
                            dve.scalar_tensor_tensor(
                                out=mt[q][:, 2 * h + j, :], in0=idt[:, :],
                                scalar=wct[:, 2 * h + j, ds(m * 2 + q, 1)], in1=b[:, j, 1, :],
                                op0=ALU.mult, op1=ALU.add).then_inc(sem["mt"][q], 1)
                for q in (0, 1):
                    wait(dve, "s_pe", q, m, 1)
                    wait(dve, "y_pe", 1 - q, m, q)
                    dve.tensor_copy(st[1 - q][:, :, :], four(bank[q][1][:, :])).then_inc(s_sb, 1)

        @block.gpsimd
        def _(pool):
            pool.wait_ge(cst, 64)
            with pool.Fori(0, NCH // 2) as m:
                for q in (0, 1):
                    wait(pool, "m4", q, m, 4)
                    wait(pool, "gh_pe", q, m, 0)
                    for n in range(LEVELS):
                        pool.tensor_tensor(ct[q][:, n], m4[q][:, :, 0, :], every(lev[:, n + 1, :], 4),
                                           ALU.mult).then_inc(sem["ct"][q], 1)


def rwkv_samples(nc, vecs, state, ident, state_out, y):
    BH = NS * 8
    with Stage(nc, "rs") as s:
        S = s.sb("S", [BH, 64, 64])
        T = s.sb("T", [BH, 64, 64])
        vt = s.sb("vec", [BH, 6, 64])
        sa, yt = s.sb("sa", [BH, 64]), s.sb("yt", [BH, 64])
        yc = s.sb("yc", [P, 4, NS])
        idt = s.sb("id", [P, P])
        tr = s.ps("tr", [P, 512])
        ready, own, out, y_done, tr_done, yc_done = (s.sem(n) for n in ("ready", "own", "out", "y_done", "tr", "yc"))
        block = s.block()

        @block.sync
        def _(sp):
            sp.dma_start(S[:, :, :], state).then_inc(ready, 16)
            sp.dma_start(idt[:, :], ident).then_inc(ready, 16)
            sp.dma_start(vt[:, :, :], vecs.rearrange("n b (h c) -> (b h) n c", c=64)).then_inc(ready, 16)
            sp.wait_ge(own, 7)
            sp.dma_start(state_out, S[:, :, :]).then_inc(out, 16)
            sp.wait_ge(yc_done, 2)
            sp.dma_start(y[:, :, SEQ:COLS], yc[:, :, :]).then_inc(out, 16)
            sp.wait_ge(out, 32)

        @block.vector
        def _(dve):
            link = Chain(dve, own)
            row = lambda n: vt[:, n:n + 1, :].broadcast_to([BH, 64, 64])
            col = lambda ap: ap.rearrange("p (v o) -> p v o", o=1).broadcast_to([BH, 64, 64])
            dve.wait_ge(ready, 48)
            link(dve.tensor_tensor(T[:, :, :], S[:, :, :], row(S_A), ALU.mult))
            link(dve.tensor_reduce(sa[:, :], T[:, :, :], AX.X, ALU.add))
            link(dve.tensor_tensor(S[:, :, :], S[:, :, :], row(S_W), ALU.mult))
            link(dve.tensor_tensor(T[:, :, :], col(sa[:, :]), row(S_B), ALU.mult))
            link(dve.tensor_tensor(S[:, :, :], S[:, :, :], T[:, :, :], ALU.add))
            link(dve.tensor_tensor(T[:, :, :], col(vt[:, S_V, :]), row(S_K), ALU.mult))
            link(dve.tensor_tensor(S[:, :, :], S[:, :, :], T[:, :, :], ALU.add))
            link(dve.tensor_tensor(T[:, :, :], S[:, :, :], row(S_R), ALU.mult))
            dve.tensor_reduce(yt[:, :], T[:, :, :], AX.X, ALU.add).then_inc(y_done, 1)
            dve.wait_ge(tr_done, 1)
            for h in (0, 1):
                src = tr[0:64, 0:BH].rearrange("v (b j h) -> v h j b", j=4, h=2)[:, h]
                dve.tensor_copy(yc[64 * h:64 * h + 64, :, :], src).then_inc(yc_done, 1)

        @block.tensor
        def _(pe):
            pe.wait_ge(ready, 48)
            pe.wait_ge(y_done, 1)
            pe.transpose(tr[0:64, 0:BH], yt[:, :], idt[0:BH, 0:BH]).then_inc(tr_done, 1)


def rwkv_output(nc, y, bonus, gate, prm, ones, cat):
    with Stage(nc, "ro") as s:
        two = lambda n: [s.sb(f"{n}{q}", [P, COLS]) for q in (0, 1)]
        yt, bt, gt, sq, rs = two("y"), two("b"), two("g"), two("sq"), two("rs")
        pr = s.sb("prm", [P, 4, 10])
        on = s.sb("ones", [P, P])
        acc = s.ps("acc", [P, NBLK, 512])
        cst = s.sem("cst")
        names = ("in", "mm", "sq", "rstd", "gate", "own", "out", "stored", "biased")
        sem = {n: [s.sem(f"{n}{q}") for q in (0, 1)] for n in names}
        free = s.sem("free")
        blocks = [(b * BLK, min(BLK, COLS - b * BLK)) for b in range(NBLK)]
        block = s.block()
        eps = s.sb("eps", [P, 1])
        eps_set = s.sem("eps_set")

        @block.sync
        def _(sp):
            sp.dma_start(pr[:, :, :], prm).then_inc(cst, 16)
            sp.dma_start(on[:, :], ones).then_inc(cst, 16)

            def store(j):
                q, m = j % 2, j // 2
                sp.wait_ge(sem["out"][q], m + 1)
                sp.dma_start(cat[j], yt[q][:, :]).then_inc(sem["stored"][q], 16)
            for j in range(4):
                q, m = j % 2, j // 2
                if m:
                    store(j - 2)
                    sp.wait_ge(sem["stored"][q], 16 * m)
                for t, src in ((yt, y[:, j, :]), (bt, bonus[j]), (gt, gate[j])):
                    sp.dma_start(t[q][:, :], src).then_inc(sem["in"][q], 16)
            for j in (2, 3):
                store(j)
            for q in (0, 1):
                sp.wait_ge(sem["stored"][q], 32)

        @block.tensor
        def _(pe):
            pe.wait_ge(cst, 32)
            for j in range(4):
                q, m = j % 2, j // 2
                for n, (x, ready, count) in enumerate(((yt, "in", 48), (sq, "sq", 1))):
                    pe.wait_ge(sem[ready][q], count * (m + 1))
                    for b, (at, width) in enumerate(blocks):
                        if j or n:
                            pe.wait_ge(free, (2 * j + n - 1) * NBLK + b + 1)
                        pe.matmul(acc[:, b, 0:width], on[:, :], x[q][:, at:at + width], start=True,
                                  stop=True).then_inc(sem["mm"][q], 1)

        @block.vector
        def _(dve):
            dve.memset(eps[:, :], GN_EPS).then_inc(eps_set, 1)
            dve.wait_ge(cst, 32)
            for j in range(4):
                q, m = j % 2, j // 2
                pj = lambda n: pr[:, j, n:n + 1]
                dve.wait_ge(sem["in"][q], 48 * (m + 1))
                for b, (at, width) in enumerate(blocks):
                    dve.wait_ge(sem["mm"][q], m * 2 * NBLK + b + 1)
                    dve.scalar_tensor_tensor(out=yt[q][:, at:at + width], in0=acc[:, b, 0:width], scalar=-1.0 / 64,
                                             in1=yt[q][:, at:at + width], op0=ALU.mult,
                                             op1=ALU.add).then_inc(free, 1)
                dve.wait_ge(sem["rstd"][q], m + 1)
                dve.tensor_tensor(yt[q][:, :], yt[q][:, :], rs[q][:, :], ALU.mult).then_inc(sem["own"][q], 1)
                dve.wait_ge(sem["own"][q], 2 * m + 1)
                dve.tensor_scalar(yt[q][:, :], yt[q][:, :], pj(GN_G), pj(GN_B), ALU.mult,
                                  ALU.add).then_inc(sem["own"][q], 1)
                dve.wait_ge(sem["biased"][q], m + 1)
                dve.wait_ge(sem["gate"][q], m + 1)
                dve.tensor_tensor(yt[q][:, :], yt[q][:, :], gt[q][:, :], ALU.mult).then_inc(sem["out"][q], 1)

        @block.gpsimd
        def _(pool):
            for j in range(4):
                q, m = j % 2, j // 2
                pool.wait_ge(sem["own"][q], 2 * m + 2)
                pool.tensor_tensor(yt[q][:, :], yt[q][:, :], bt[q][:, :], ALU.add).then_inc(sem["biased"][q], 1)

        @block.scalar
        def _(act):
            act.wait_ge(eps_set, 1)
            for j in range(4):
                q, m = j % 2, j // 2
                act.wait_ge(sem["in"][q], 48 * (m + 1))
                act.activation(gt[q][:, :], gt[q][:, :], ACT.Silu).then_inc(sem["gate"][q], 1)
                act.wait_ge(free, 2 * j * NBLK + NBLK)
                act.activation(sq[q][:, :], yt[q][:, :], ACT.Square).then_inc(sem["sq"][q], 1)
                act.preload_act_table_set(LN_EXP)
                for b, (at, width) in enumerate(blocks):
                    act.wait_ge(sem["mm"][q], m * 2 * NBLK + NBLK + b + 1)
                    act.activation(rs[q][:, at:at + width], acc[:, b, 0:width], ACT.Ln, scale=1.0 / 64,
                                   bias=eps[:, 0:1]).then_inc(free, 1)
                act.wait_ge(free, 2 * (j + 1) * NBLK)
                act.activation(rs[q][:, :], rs[q][:, :], ACT.Exp, scale=-0.5).then_inc(sem["rstd"][q], 1)


G, SP_, GC = 32, 64, 16
T8 = 8
NC8 = SEQ // T8
TWO_PI = (6.28125, 1.93500518798828125e-3, 3.0199159819e-7)
ROUND = 1.5 * 2.0 ** 23


def s5_prompt(nc, u, par, mats, dcol, const, yT, fin, kept_l, kept_m,
              kept_a):
    with Stage(nc, "s5") as s:
        ut = s.sb("u", [P, 2, T8, 512])
        co, si = s.sb("cos", [P, G, NC8]), s.sb("sin", [P, G, NC8])
        L = s.sb("L", [P, G, T8, GC])
        D1, D2 = s.sb("D1", [P, G, T8, GC]), s.sb("D2", [P, G, T8, GC])
        jl = s.sb("jl", [P, 2, G, GC])
        tmp = s.sb("tmp", [P, 2, G, GC])
        m1, m2 = s.sb("m1", [P, G, GC]), s.sb("m2", [P, G, GC])
        pt = s.sb("par", [P, 3, G])
        raw = s.sb("raw", [P, 2, G, GC])
        sc = s.sb("sc", [P, 24, G])
        dc = s.sb("dcol", [P, G])
        sg = s.sb("sgn", [P, 1])
        idt, jm = s.sb("id", [P, P]), s.sb("jm", [P, P])
        lx = [s.sb(f"lx{q}", [P, 15, GC]) for q in (0, 1)]
        xg = [s.sb(f"xg{q}", [P, 2, T8, GC]) for q in (0, 1)]
        xT = [s.sb(f"xT{q}", [P, NC8]) for q in (0, 1)]
        tp = [s.sb(f"tp{q}", [P, P]) for q in (0, 1)]
        bi = [s.sb(f"bi{q}", [P, 2, P]) for q in (0, 1)]
        xr = [s.sb(f"xr{q}", [P, 2, NC8]) for q in (0, 1)]
        gs = [s.sb(f"gs{q}", [P, NC8]) for q in (0, 1)]
        hc = [s.sb(f"hc{q}", [P, NC8]) for q in (0, 1)]
        hs = [s.sb(f"hs{q}", [P, NC8]) for q in (0, 1)]
        gl = s.sb("glast", [P, G])
        fo = s.sb("fo", [P, 4, G])
        ye = co[:, :, :].rearrange("p g n -> p (g n)").rearrange("p (k c) -> p k c", k=4)
        bk = [[s.ps(f"bk{q}{n}", [P, 512]) for n in range(4)] for q in (0, 1)]
        COUNT = dict(cp=1, cpl=1, xT_pe=1, tb_pe=1, tb=2, xT=1, x_pe=1, rot=1, scan=1, hc=1, hs=1, y_pe=1, y=1, own=1)
        sem = {n: [s.sem(f"{n}{q}") for q in (0, 1)] for n in COUNT}
        (cst, u_in, own, pown, angles, trig, tab_v, tab_p, mats_v, mats_p, zed, act0, ftr, fout, gel, ytr, yev,
         kst, flast, held) = (s.sem(n) for n in (
             "cst", "u_in", "own", "pown", "angles", "trig", "tab_v", "tab_p", "mats_v", "mats_p", "zed", "act0",
             "ftr", "fout", "gel", "ytr", "yev", "kst", "flast", "held"))
        block = s.block()
        c_ = lambda n: sc[:, n, :]
        (DT, MAG, TH, KR, R_, SI, SH, CO, AR, AI, DEN, FR, FI, NR, X0, X1, PC, PS, PC2, PS2, RHO, X2, X3, X4) = range(24)
        gb = lambda ap: ap.rearrange("p (g o) -> p g o", o=1).broadcast_to([P, G, GC])

        def wait(eng, name, q, m, k):
            eng.wait_ge(sem[name][q], m * COUNT[name] + k)

        @block.sync
        def _(sp):
            for dst, src in ((pt[:, :, :], par), (raw[:, :, :, :], mats[:, 0:2]), (m1[:, :, :], mats[:, 2]),
                             (m2[:, :, :], mats[:, 3]), (dc[:, :], dcol), (sg[:, :], const["sgn"]),
                             (idt[:, :], const["ident"]), (jm[:, :], const["jm"])):
                sp.dma_start(dst, src).then_inc(cst, 16)
            sp.dma_start(ut[:, :, :, :].rearrange("p b s c -> p (b s) c"),
                         u[0:TT].rearrange("t p c -> p t c")).then_inc(u_in, 16)
            sp.wait_ge(mats_v, 1)
            for dst, src in ((kept_l, L[:, :, T8 - 1, :]), (kept_m, m1[:, :, :]), (kept_a, sc[:, AR:AI + 1, :])):
                sp.dma_start(dst, src).then_inc(kst, 16)
            sp.wait_ge(fout, 1)
            sp.dma_start(fin, fo[:, 3, :]).then_inc(kst, 16)
            sp.wait_ge(yev, 2 * T8)
            sp.dma_start(yT[:, :, 0:SEQ], ye).then_inc(kst, 16)
            sp.wait_ge(kst, 80)

        @block.scalar
        def _(act):
            act.wait_ge(cst, 128)
            act.activation(c_(DT), pt[:, 2, :], ACT.Exp).then_inc(act0, 1)
            act.wait_ge(angles, 1)
            act.activation(c_(MAG), c_(X0), ACT.Exp)
            act.activation(c_(RHO), c_(X0), ACT.Exp, scale=float(T8)).then_inc(act0, 1)
            act.wait_ge(angles, 2)
            act.activation(c_(SI), c_(R_), ACT.Sin)
            act.activation(c_(SH), c_(R_), ACT.Sin, scale=0.5).then_inc(act0, 1)
            act.wait_ge(u_in, 16)
            with act.Fori(0, G // 2) as m:
                for q in (0, 1):
                    g = m * 2 + q
                    wait(act, "xT_pe", q, m, 0)
                    act.sem_inc(held, 1)
                    act.copy(xg[q][:, :, :, :].rearrange("p b s c -> p (b s) c"),
                             ut[:, :, :, ds(g * GC, GC)].rearrange("p b s c -> p (b s) c")
                             ).then_inc(sem["cp"][q], 1)
                for q in (0, 1):
                    wait(act, "tb_pe", q, m, 1)
                    wait(act, "y_pe", q, m, 0)
                    act.copy(xT[q][:, :], bk[q][0][:, 0:NC8]).then_inc(sem["xT"][q], 1)
                    act.copy(bi[q][:, :, :].rearrange("p a c -> p (a c)"), bk[q][0][:, NC8:2 * NC8]
                             ).then_inc(sem["tb"][q], 1)
                for q in (0, 1):
                    g = m * 2 + q
                    wait(act, "y_pe", q, m, 1)
                    act.sem_inc(held, 1)
                    act.copy(ut[:, :, :, ds(g * GC, GC)].rearrange("p b s c -> p (b s) c"),
                             bk[q][3][:, 0:2 * P].rearrange("p (n c) -> p n c", c=GC)).then_inc(sem["y"][q], 1)
            for q in (0, 1):
                act.wait_ge(sem["y"][q], G // 2)
            for b in (0, 1):
                act.activation(ut[:, b].rearrange("p s c -> p (s c)"), ut[:, b].rearrange("p s c -> p (s c)"),
                               ACT.Gelu_apprx_tanh).then_inc(gel, 1)

        @block.vector
        def _(dve):
            link = Chain(dve, own)
            tt = lambda o, a, b, op: link(dve.tensor_tensor(o, a, b, op))
            ts = lambda o, a, s1, s2, o1, o2=ALU.bypass: link(
                dve.tensor_scalar(o, a, s1, s2, o1, o2) if s2 is not None else dve.tensor_scalar(o, a, s1, None, o1))
            for q in (0, 1):
                dve.memset(lx[q][:, :, :], 0.0).then_inc(zed, 1)
                dve.memset(hc[q][:, :], 0.0).then_inc(zed, 1)
                dve.memset(hs[q][:, :], 0.0).then_inc(zed, 1)
            link(dve.memset(co[:, :, 0:1], 1.0))
            link(dve.memset(si[:, :, 0:1], 0.0))
            dve.wait_ge(cst, 128)
            dve.wait_ge(act0, 1)
            dve.tensor_tensor(c_(X0), pt[:, 0, :], c_(DT), ALU.mult).then_inc(angles, 1)
            tt(c_(TH), pt[:, 1, :], c_(DT), ALU.mult)
            ts(c_(KR), c_(TH), 1.0 / (2 * np.pi), None, ALU.mult)
            ts(c_(KR), c_(KR), ROUND, None, ALU.add)
            ts(c_(KR), c_(KR), -ROUND, None, ALU.add)
            for part in TWO_PI:
                src = c_(TH) if part == TWO_PI[0] else c_(R_)
                link(dve.scalar_tensor_tensor(out=c_(R_), in0=c_(KR), scalar=-part, in1=src, op0=ALU.mult,
                                              op1=ALU.add))
            ts(c_(R_), c_(R_), 3.1415925, -3.1415925, ALU.min, ALU.max)
            dve.sem_inc(angles, 1)
            dve.wait_ge(act0, 3)
            tt(c_(CO), c_(SH), c_(SH), ALU.mult)
            ts(c_(CO), c_(CO), -2.0, 1.0, ALU.mult, ALU.add)
            tt(c_(AR), c_(MAG), c_(CO), ALU.mult)
            tt(c_(AI), c_(MAG), c_(SI), ALU.mult)
            pc, ps = CO, SI
            for _n in range(3):
                tt(c_(X1), c_(pc), c_(pc), ALU.mult)
                tt(c_(X2), c_(ps), c_(ps), ALU.mult)
                tt(c_(X3), c_(pc), c_(ps), ALU.mult)
                tt(c_(PC), c_(X1), c_(X2), ALU.subtract)
                ts(c_(PS), c_(X3), 2.0, None, ALU.mult)
                pc, ps = PC, PS
            for n in range(8):
                w = 1 << n
                b = lambda x: c_(x).rearrange("p (g o) -> p g o", o=1).broadcast_to([P, G, w])
                t = D1[:, :, :, :].rearrange("p g s c -> p g (s c)")[:, :, 0:w]
                if n:
                    dve.wait_ge(tab_p, n)
                    tt(c_(X1), c_(PC), c_(PC), ALU.mult)
                    tt(c_(X2), c_(PS), c_(PS), ALU.mult)
                    tt(c_(X3), c_(PC), c_(PS), ALU.mult)
                    tt(c_(PC), c_(X1), c_(X2), ALU.subtract)
                    ts(c_(PS), c_(X3), 2.0, None, ALU.mult)
                dve.sem_inc(tab_v, 1)
                dve.tensor_tensor(co[:, :, w:2 * w], co[:, :, 0:w], b(PC), ALU.mult)
                tt(t, si[:, :, 0:w], b(PS), ALU.mult)
                tt(co[:, :, w:2 * w], co[:, :, w:2 * w], t, ALU.subtract)
            ts(c_(NR), c_(AR), -1.0, None, ALU.add)
            tt(c_(X1), pt[:, 0, :], pt[:, 0, :], ALU.mult)
            tt(c_(X2), pt[:, 1, :], pt[:, 1, :], ALU.mult)
            tt(c_(DEN), c_(X1), c_(X2), ALU.add)
            link(dve.reciprocal(c_(DEN), c_(DEN)))
            tt(c_(X1), c_(NR), pt[:, 0, :], ALU.mult)
            tt(c_(X2), c_(AI), pt[:, 1, :], ALU.mult)
            tt(c_(X1), c_(X1), c_(X2), ALU.add)
            tt(c_(FR), c_(X1), c_(DEN), ALU.mult)
            tt(c_(X1), c_(AI), pt[:, 0, :], ALU.mult)
            tt(c_(X2), c_(NR), pt[:, 1, :], ALU.mult)
            tt(c_(X1), c_(X1), c_(X2), ALU.subtract)
            tt(c_(FI), c_(X1), c_(DEN), ALU.mult)
            link(dve.tensor_scalar(raw[:, 1], raw[:, 1], sg[:, 0:1], None, ALU.mult))
            link(dve.tensor_scalar(m1[:, :, :], m1[:, :, :], sg[:, 0:1], -1.0, ALU.mult, ALU.mult))
            ts(m2[:, :, :], m2[:, :, :], -1.0, None, ALU.mult)

            def turn(re, im, x, jx, ox, ojx):
                dve.tensor_tensor(tmp[:, 0], x, gb(re), ALU.mult)
                tt(tmp[:, 1], jx, gb(im), ALU.mult)
                tt(ox, tmp[:, 0], tmp[:, 1], ALU.add)
                dve.tensor_tensor(tmp[:, 0], jx, gb(re), ALU.mult)
                tt(tmp[:, 1], x, gb(im), ALU.mult)
                tt(ojx, tmp[:, 0], tmp[:, 1], ALU.subtract)
            turn(c_(FR), c_(FI), raw[:, 0], raw[:, 1], L[:, :, 7, :], jl[:, 0])
            for n in range(1, T8):
                turn(c_(AR), c_(AI), L[:, :, 8 - n, :], jl[:, (n - 1) % 2], L[:, :, 7 - n, :], jl[:, n % 2])
            dve.wait_ge(tab_p, 8)
            turn(c_(AR), c_(AI), m1[:, :, :], m2[:, :, :], D1[:, :, 0, :], D2[:, :, 0, :])
            for n in range(1, T8):
                turn(c_(AR), c_(AI), D1[:, :, n - 1, :], D2[:, :, n - 1, :], D1[:, :, n, :], D2[:, :, n, :])
            dve.sem_inc(mats_v, 1)
            with dve.Fori(0, G // 2) as m:
                for q in (0, 1):
                    g = m * 2 + q
                    wait(dve, "tb_pe", q, m, 1)
                    wait(dve, "y_pe", q, m, 0)
                    dve.scalar_tensor_tensor(out=tp[q][:, :], in0=idt[:, :], scalar=dc[:, ds(g, 1)],
                                             in1=bk[q][1][:, 0:P], op0=ALU.mult, op1=ALU.add
                                             ).then_inc(sem["tb"][q], 1)
                for q in (0, 1):
                    g = m * 2 + q
                    tab = lambda t: t[:, ds(g, 1), :].rearrange("p o c -> p (o c)")
                    wait(dve, "x_pe", q, m, 1)
                    dve.tensor_tensor(xr[q][:, 0, :], bk[q][2][:, 0:NC8], tab(co), ALU.mult)
                    dve.tensor_tensor(xr[q][:, 1, :], bk[q][2][:, NC8:2 * NC8], tab(si), ALU.mult
                                      ).then_inc(sem["rot"][q], 1)
                    wait(dve, "rot", q, m, 1)
                    dve.tensor_tensor(xr[q][:, 0, :], xr[q][:, 0, :], xr[q][:, 1, :], ALU.add
                                      ).then_inc(sem["own"][q], 1)
                    wait(dve, "own", q, m, 1)
                    wait(dve, "hs", q, m, 0)
                    dve.tensor_tensor_scan(gs[q][:, :], c_(RHO)[:, ds(g, 1)].broadcast_to([P, NC8]), xr[q][:, 0, :],
                                           0.0, ALU.mult, ALU.add).then_inc(sem["scan"][q], 1)
                    wait(dve, "scan", q, m, 1)
                    wait(dve, "y_pe", q, m, 0)
                    dve.tensor_tensor(hc[q][:, 1:NC8], gs[q][:, 0:NC8 - 1], tab(co)[:, 0:NC8 - 1], ALU.mult)
                    dve.tensor_copy(gl[:, ds(g, 1)], gs[q][:, NC8 - 1:NC8]).then_inc(sem["hc"][q], 1)
            for q in (0, 1):
                dve.wait_ge(sem["hc"][q], G // 2)
            dve.tensor_tensor(fo[:, 0, :], gl[:, :], co[:, :, NC8 - 1], ALU.mult).then_inc(flast, 1)
            dve.tensor_tensor(fo[:, 1, :], gl[:, :], si[:, :, NC8 - 1], ALU.mult).then_inc(flast, 1)
            dve.wait_ge(ftr, 1)
            dve.tensor_tensor(fo[:, 3, :], fo[:, 0, :], bk[0][0][:, 0:G], ALU.subtract).then_inc(fout, 1)
            for n in range(2 * T8):
                b, t = divmod(n, T8)
                dve.wait_ge(ytr, n + 1)
                dve.tensor_copy(ye[:, :, b * SEQ // 2 + t:(b + 1) * SEQ // 2:T8],
                                bk[1][n % 2][:, :].rearrange("p (k c) -> p k c", k=4)).then_inc(yev, 1)

        @block.gpsimd
        def _(pool):
            for n in range(8):
                w = 1 << n
                b = lambda x: c_(x).rearrange("p (g o) -> p g o", o=1).broadcast_to([P, G, w])
                t = D2[:, :, :, :].rearrange("p g s c -> p g (s c)")[:, :, 0:w]
                pool.wait_ge(tab_v, n + 1)
                pool.tensor_tensor(si[:, :, w:2 * w], si[:, :, 0:w], b(PC), ALU.mult).then_inc(pown, 1)
                pool.tensor_tensor(t, co[:, :, 0:w], b(PS), ALU.mult).then_inc(pown, 1)
                pool.wait_ge(pown, 2 * n + 2)
                pool.tensor_tensor(si[:, :, w:2 * w], si[:, :, w:2 * w], t, ALU.add).then_inc(tab_p, 1)
            pool.wait_ge(mats_v, 1)
            pool.wait_ge(zed, 6)
            with pool.Fori(0, G // 2) as m:
                for q in (0, 1):
                    g = m * 2 + q
                    wait(pool, "tb_pe", q, m, 0)
                    pool.tensor_copy(lx[q][:, 0:T8, :], L[:, ds(g, 1), :, :].rearrange("p o s c -> p (o s) c")
                                     ).then_inc(sem["cpl"][q], 1)
                for q in (0, 1):
                    g = m * 2 + q
                    wait(pool, "scan", q, m, 1)
                    wait(pool, "y_pe", q, m, 0)
                    pool.tensor_tensor(hs[q][:, 1:NC8], gs[q][:, 0:NC8 - 1],
                                       si[:, ds(g, 1), 0:NC8 - 1].rearrange("p o c -> p (o c)"),
                                       ALU.mult).then_inc(sem["hs"][q], 1)

        @block.tensor
        def _(pe):
            pe.wait_ge(cst, 128)
            pe.wait_ge(mats_v, 1)
            pe.wait_ge(zed, 6)
            with pe.Fori(0, G // 2) as m:
                for q in (0, 1):
                    g = m * 2 + q
                    wait(pe, "cp", q, m, 1)
                    wait(pe, "xT", q, m, 0)
                    for b in (0, 1):
                        mm = pe.transpose(bk[q][0][:, b * P:(b + 1) * P],
                                          xg[q][:, b].rearrange("p s c -> p (s c)"), idt[:, :])
                    mm.then_inc(sem["xT_pe"][q], 1)
                    wait(pe, "cpl", q, m, 1)
                    wait(pe, "tb", q, m, 0)
                    lf = lx[q][:, :, :].rearrange("p s c -> p (s c)")
                    for t in range(T8):
                        pe.matmul(bk[q][1][:, t * GC:(t + 1) * GC], lf[:, (7 - t) * GC:(7 - t) * GC + P],
                                  m1[:, ds(g, 1), :].rearrange("p o c -> p (o c)"), start=True, stop=True)
                    pe.transpose(bk[q][0][:, NC8:NC8 + P], lf[:, 0:P], idt[:, :])
                    pe.matmul(bk[q][0][:, NC8 + P:2 * NC8], lf[:, 0:P], jm[:, :], start=True,
                              stop=True).then_inc(sem["tb_pe"][q], 1)
                for q in (0, 1):
                    wait(pe, "tb", q, m, 2)
                    wait(pe, "xT", q, m, 1)
                    wait(pe, "rot", q, m, 0)
                    for a in (0, 1):
                        mm = pe.matmul(bk[q][2][:, a * NC8:(a + 1) * NC8], bi[q][:, a, :], xT[q][:, :],
                                       start=True, stop=True)
                    mm.then_inc(sem["x_pe"][q], 1)
                for q in (0, 1):
                    g = m * 2 + q
                    dg = lambda t: t[:, ds(g, 1), :, :].rearrange("p o s c -> p (o s c)")
                    wait(pe, "hc", q, m, 1)
                    wait(pe, "hs", q, m, 1)
                    wait(pe, "y", q, m, 0)
                    for b in (0, 1):
                        o = bk[q][3][:, b * P:(b + 1) * P]
                        r = slice(b * P, (b + 1) * P)
                        pe.matmul(o, xT[q][:, r], tp[q][:, :], start=True, stop=False)
                        pe.matmul(o, hc[q][:, r], dg(D1), start=False, stop=False)
                        mm = pe.matmul(o, hs[q][:, r], dg(D2), start=False, stop=True)
                    mm.then_inc(sem["y_pe"][q], 1)
            pe.wait_ge(flast, 2)
            pe.matmul(bk[0][0][:, 0:G], jm[:, :], fo[:, 1, :], start=True, stop=True).then_inc(ftr, 1)
            for n in range(2 * T8):
                b, t = divmod(n, T8)
                pe.wait_ge(gel, b + 1)
                if n > 1:
                    pe.wait_ge(yev, n - 1)
                for k in range(4):
                    mm = pe.transpose(bk[1][n % 2][:, k * P:(k + 1) * P], ut[:, b, t, k * P:(k + 1) * P], idt[:, :])
                mm.then_inc(ytr, 1)


def s5_samples(nc, u, par, h_in, kept_l, kept_m, kept_a, d_row, const, yT, h_out):
    with Stage(nc, "ss") as s:
        ub = s.sb("u", [P, NS, G, GC])
        t = s.sb("t", [P, NS, G, GC])
        lt, mt, at = s.sb("l", [P, G, GC]), s.sb("m", [P, G, GC]), s.sb("a", [P, 2, G])
        h = s.sb("h", [P, 2, NS, G])
        bu, w = s.sb("bu", [P, NS, G]), s.sb("w", [P, NS, G])
        hn = s.sb("hn", [P, NS, G])
        ur, dr, y = s.sb("ur", [NS, 512]), s.sb("dr", [NS, 512]), s.sb("y", [NS, 512])
        yc = s.sb("yc", [P, 4, NS])
        sg, idt = s.sb("sgn", [P, 1]), s.sb("id", [P, P])
        yp, tr = s.ps("yp", [P, 512]), s.ps("tr", [P, 512])
        ready, own, new, mm_, pre, gel, trd, ycd, out = (s.sem(n) for n in (
            "ready", "own", "new", "mm", "pre", "gel", "trd", "ycd", "out"))
        block = s.block()

        @block.sync
        def _(sp):
            loads = ((ub[:, :, :, :].rearrange("p b g c -> p (b g c)"),
                      u.rearrange("(o b) c -> o (b c)", o=1).broadcast_to([P, NS * 512])),
                     (lt[:, :, :], kept_l), (mt[:, :, :], kept_m), (at[:, :, :], kept_a), (h[:, :, :, :], h_in),
                     (ur[:, :], u), (dr[:, :], d_row.broadcast_to([NS, 512])), (sg[:, :], const["sgn"]),
                     (idt[:, :], const["ident"]))
            for dst, src in loads:
                sp.dma_start(dst, src).then_inc(ready, 16)
            sp.wait_ge(new, 1)
            sp.dma_start(h_out, hn[:, :, :]).then_inc(out, 16)
            sp.wait_ge(ycd, 1)
            sp.dma_start(yT[:, :, SEQ:COLS], yc[:, :, :]).then_inc(out, 16)
            sp.wait_ge(out, 32)

        @block.vector
        def _(dve):
            link = Chain(dve, own)
            tt = lambda o, a, b, op: link(dve.tensor_tensor(o, a, b, op))
            row = lambda ap: ap.rearrange("p (o g) -> p o g", o=1).broadcast_to([P, NS, G])
            dve.wait_ge(ready, 144)
            lb = lt[:, :, :].rearrange("p (o g) c -> p o (g c)", o=1).broadcast_to([P, NS, G * GC])
            tt(t[:, :, :, :].rearrange("p b g c -> p b (g c)"), ub[:, :, :, :].rearrange("p b g c -> p b (g c)"),
               lb, ALU.mult)
            link(dve.tensor_reduce(bu[:, :, :], t[:, :, :, :], AX.X, ALU.add))
            tt(w[:, :, :], h[:, 0], row(at[:, 0, :]), ALU.mult)
            tt(bu[:, :, :], bu[:, :, :], w[:, :, :], ALU.add)
            link(dve.tensor_scalar(h[:, 1], h[:, 1], sg[:, 0:1], None, ALU.mult))
            tt(w[:, :, :], h[:, 1], row(at[:, 1, :]), ALU.mult)
            dve.tensor_tensor(hn[:, :, :], bu[:, :, :], w[:, :, :], ALU.add).then_inc(new, 1)
            tt(ur[:, :], ur[:, :], dr[:, :], ALU.mult)
            dve.wait_ge(mm_, 1)
            dve.tensor_tensor(y[:, :], ur[:, :], yp[0:NS, :], ALU.add).then_inc(pre, 1)
            dve.wait_ge(trd, 1)
            dve.tensor_copy(yc[:, :, :], tr[:, 0:4 * NS].rearrange("p (k b) -> p k b", k=4)).then_inc(ycd, 1)

        @block.tensor
        def _(pe):
            pe.wait_ge(ready, 144)
            pe.wait_ge(new, 1)
            for g in range(G):
                mm = pe.matmul(yp[0:NS, g * GC:(g + 1) * GC], hn[:, :, g], mt[:, g, :], start=True, stop=True)
            mm.then_inc(mm_, 1)
            pe.wait_ge(gel, 1)
            for k in range(4):
                mm = pe.transpose(tr[:, k * NS:(k + 1) * NS], y[:, k * P:(k + 1) * P], idt[0:NS, 0:NS])
            mm.then_inc(trd, 1)

        @block.scalar
        def _(act):
            act.wait_ge(pre, 1)
            act.activation(y[:, :], y[:, :], ACT.Gelu_apprx_tanh).then_inc(gel, 1)


def s5_glu(nc, yT, gate, w, bias, cat):
    with Stage(nc, "sg") as s:
        y = s.sb("y", [P, 4, COLS])
        wt, bt = s.sb("w", [P, 4, 512]), s.sb("b", [P, 4])
        gt = [s.sb(f"g{q}", [P, COLS]) for q in (0, 1)]
        sg = [s.sb(f"s{q}", [P, COLS]) for q in (0, 1)]
        acc = s.ps("acc", [P, NBLK, 512])
        cst, mm_, free, silu, half, outp = (s.sem(n) for n in ("cst", "mm", "free", "silu", "half", "outp"))
        g_in = [s.sem(f"g_in{q}") for q in (0, 1)]
        stored = [s.sem(f"stored{q}") for q in (0, 1)]
        blocks = [(b * BLK, min(BLK, COLS - b * BLK)) for b in range(NBLK)]
        block = s.block()

        @block.sync
        def _(sp):
            for dst, src in ((y[:, :, :], yT), (wt[:, :, :], w), (bt[:, :], bias)):
                sp.dma_start(dst, src).then_inc(cst, 16)
            for n in range(4):
                if n > 1:
                    sp.wait_ge(stored[n % 2], 16 * (n // 2))
                sp.dma_start(gt[n % 2][:, :], gate[n]).then_inc(g_in[n % 2], 16)

        @block.tensor
        def _(pe):
            pe.wait_ge(cst, 48)
            for n in range(4):
                for b, (at, width) in enumerate(blocks):
                    if n:
                        pe.wait_ge(free, (n - 1) * NBLK + b + 1)
                    for k in range(4):
                        mm = pe.matmul(acc[:, b, 0:width], wt[:, k, n * P:(n + 1) * P], y[:, k, at:at + width],
                                       start=(k == 0), stop=(k == 3))
                    mm.then_inc(mm_, 1)

        @block.scalar
        def _(act):
            act.wait_ge(cst, 48)
            for n in range(4):
                q = n % 2
                act.wait_ge(g_in[q], 16 * (n // 2 + 1))
                act.activation(gt[q][:, :], gt[q][:, :], ACT.Silu).then_inc(silu, 1)
                if n > 1:
                    act.wait_ge(outp, n - 1)
                for b, (at, width) in enumerate(blocks):
                    act.wait_ge(mm_, n * NBLK + b + 1)
                    act.activation(sg[q][:, at:at + width], acc[:, b, 0:width], ACT.Sigmoid,
                                   bias=bt[:, n:n + 1]).then_inc(free, 1)

        @block.vector
        def _(dve):
            for n in range(4):
                q = n % 2
                dve.wait_ge(free, (n + 1) * NBLK)
                dve.wait_ge(silu, n + 1)
                dve.tensor_tensor(sg[q][:, :], sg[q][:, :], y[:, n, :], ALU.mult).then_inc(half, 1)
                dve.wait_ge(half, n + 1)
                if n > 1:
                    dve.wait_ge(stored[q], 16 * (n // 2))
                dve.tensor_tensor(gt[q][:, :], sg[q][:, :], gt[q][:, :], ALU.mult).then_inc(outp, 1)

        @block.gpsimd
        def _(pool):
            for n in range(4):
                pool.wait_ge(outp, n + 1)
                pool.dma_start(cat[4 + n], gt[n % 2][:, :]).then_inc(stored[n % 2], 16)
            for q in (0, 1):
                pool.wait_ge(stored[q], 32)


HC, DC = 8, 64
STEPS = [(i, g) for i in range(TT) for g in range(i // 4, -1, -1)]
FLIP = 6
CLAMP = 2.0 ** 60


def stick_prompt(nc, z, v, bias, const, cat):
    with Stage(nc, "sp") as s:
        two = lambda n, shape: [s.sb(f"{n}{q}", shape) for q in (0, 1)]
        kr, qr = s.sb("k", [DC + 1, SEQ]), s.sb("q", [DC + 1, SEQ])
        kh, qh = two("k_high", [DC + 1, SEQ]), two("q_high", [DC + 1, SEQ])
        kl, ql = two("k_low", [DC + 1, SEQ]), two("q_low", [DC + 1, SEQ])
        vt, oT, gt = two("v", [P, TT, DC]), two("o", [DC, SEQ]), two("g", [DC, SEQ])
        e, S, att, aT = (s.sb(n, [P, 4, 512]) for n in ("e", "S", "att", "aT"))
        sp_ = s.sb("sp", [P, 4, 512])
        bt = s.sb("bias", [DC + 1, HC + 2])
        idt, neg, one = s.sb("id", [P, P]), s.sb("neg", [P, P]), s.sb("one", [P, 1])
        zb = [s.ps(f"z{n}", [P, 512]) for n in range(4)]
        tb = [s.ps(f"t{n}", [P, 512]) for n in range(2)]
        ob = [s.ps(f"ob{n}", [P, 512]) for n in range(2)]
        cst, rows = s.sem("cst"), s.sem("rows")
        per_slot = ("kv_in", "scaled", "brow", "high", "split", "gate", "gated", "stored")
        slot = {n: [s.sem(f"{n}{q}") for q in (0, 1)] for n in per_slot}
        sem = {n: s.sem(n) for n in ("z_pe", "e1", "cl", "ln", "mx", "sc", "arg", "e2", "t_pe", "t_ev")}
        o_pe, o_ev, held = s.sem("o_pe"), s.sem("o_ev"), s.sem("held")
        NSTEP = len(STEPS)
        block = s.block()
        LAST = [n for n, (i, g) in enumerate(STEPS) if g == 0]
        keys = lambda i, g: (min(4 * g + 3, i) - 4 * g + 1) * P

        def at(eng, name, m, n):
            eng.wait_ge(sem[name], m * 2 * NSTEP + n + 1)

        @block.sync
        def _(sp):
            sp.dma_start(idt[:, :], const["ident"]).then_inc(cst, 16)
            sp.dma_start(neg[:, :], const["neg"]).then_inc(cst, 16)
            sp.dma_start(bt[DC:DC + 1, 0:HC], bias).then_inc(cst, 16)

            def load(m, q):
                r = slice(64 * q, 64 * q + 64)
                pick = lambda base: z[ds(m + base, 1), r, 0:SEQ].rearrange("o p c -> p (o c)")
                sp.wait_ge(slot["stored"][q], 16 * m + 16)
                sp.sem_inc(held, 1)
                if not (isinstance(m, int) and q == 0):
                    sp.wait_ge(slot["split"][1 - q], (m if q == 0 else m + 1) * 4)
                    sp.sem_inc(held, 1)
                sp.dma_start(kr[0:DC, :], pick(4)).then_inc(slot["kv_in"][q], 16)
                sp.dma_start(qr[0:DC, :], pick(0)).then_inc(slot["kv_in"][q], 16)
                sp.dma_start(vt[q][:, :, :], v[0:TT, :, ds(m * 2 * DC + q * DC, DC)]
                             .rearrange("t p c -> p t c")).then_inc(slot["kv_in"][q], 16)
                sp.dma_start(gt[q][:, :], pick(8)).then_inc(slot["kv_in"][q], 16)

            def store(m, q):
                sp.wait_ge(slot["gated"][q], m + 1)
                sp.sem_inc(held, 1)
                sp.dma_start(cat[ds(m, 1), 64 * q:64 * q + 64, 0:SEQ].rearrange("o p c -> p (o c)"),
                             oT[q][:, :]).then_inc(slot["stored"][q], 16)
            load(0, 0)
            with sp.Fori(0, HC // 2) as m:
                load(m, 1)
                store(m, 0)
                load(m + 1, 0)
                store(m, 1)
            sp.wait_ge(slot["stored"][0], 16 * (HC // 2 + 1))
            sp.wait_ge(slot["stored"][1], 16 * (HC // 2 + 1))
            sp.wait_ge(slot["kv_in"][0], 64 * (HC // 2 + 1))

        def splits(q, c):
            return ((qh[q][:, c], ql[q][:, c], qr[:, c]), (kh[q][:, c], kl[q][:, c], kr[:, c]))

        @block.tensor
        def _(pe):
            pe.wait_ge(cst, 48)
            with pe.Fori(0, HC // 2) as m:
                def scores(n):
                    q, (i, g) = n // NSTEP, STEPS[n % NSTEP]
                    if n % NSTEP == 0:
                        pe.wait_ge(slot["split"][q], 4 * m + 4)
                    if n >= 4:
                        at(pe, "arg", m, n - 4)
                    else:
                        at(pe, "arg", m, -1)
                    w, bank = keys(i, g), zb[n % 4]
                    diag = g == i // 4
                    cq, ck = slice(i * P, (i + 1) * P), slice(4 * g * P, 4 * g * P + w)
                    mm = product(pe, bank[:, 0:w], (qh[q][:, cq], ql[q][:, cq]), (kh[q][:, ck], kl[q][:, ck]),
                                 True, not diag)
                    if diag:
                        mm = pe.matmul(bank[:, w - P:w], idt[:, :], neg[:, :], start=False, stop=True)
                    mm.then_inc(sem["z_pe"], 1)

                def flip(n):
                    i, g = STEPS[n % NSTEP]
                    at(pe, "e2", m, n)
                    at(pe, "t_ev", m, n - 2 if n >= 2 else -1)
                    for b in range(keys(i, g) // P):
                        mm = pe.transpose(tb[n % 2][:, b * P:(b + 1) * P], att[:, n % 4, b * P:(b + 1) * P], idt[:, :])
                    mm.then_inc(sem["t_pe"], 1)

                def values(n):
                    q, (i, g) = n // NSTEP, STEPS[n % NSTEP]
                    at(pe, "t_ev", m, n)
                    tile = q * TT + i
                    if g == i // 4:
                        pe.wait_ge(o_ev, m * 2 * TT + (tile - 1 if tile >= 2 else 0))
                    nb = keys(i, g) // P
                    for b in range(nb):
                        mm = pe.matmul(ob[i % 2][0:DC, 0:P], vt[q][:, 4 * g + b, :], aT[:, n % 4, b * P:(b + 1) * P],
                                       start=(g == i // 4 and b == 0), stop=(g == 0 and b == nb - 1))
                    if g == 0:
                        mm.then_inc(o_pe, 1)
                for n in range(2 * NSTEP + FLIP + 1):
                    if n < 2 * NSTEP:
                        scores(n)
                    if 0 <= n - FLIP < 2 * NSTEP:
                        flip(n - FLIP)
                    if 0 <= n - FLIP - 1 < 2 * NSTEP:
                        values(n - FLIP - 1)

        @block.scalar
        def _(act):
            for q in (0, 1):
                act.sem_inc(slot["stored"][q], 16)

            def scale(m, q):
                act.wait_ge(slot["kv_in"][q], 64 * m + 64)
                act.mul(qr[0:DC, :], qr[0:DC, :], DC ** -0.5).then_inc(slot["scaled"][q], 1)

            def gate(m, q):
                act.activation(gt[q][:, :], gt[q][:, :], ACT.Silu).then_inc(slot["gate"][q], 1)
                act.preload_act_table_set(LN_EXP)
            scale(0, 0)
            gate(0, 0)
            with act.Fori(0, HC // 2) as m:
                for n in range(2 * NSTEP + FLIP + 1):
                    if n == NSTEP - 20:
                        scale(m, 1)
                    if n == NSTEP - 8:
                        gate(m, 1)
                    if n == 2 * NSTEP - 20:
                        scale(m + 1, 0)
                    if n == 2 * NSTEP - 8:
                        gate(m + 1, 0)
                    if n < 2 * NSTEP:
                        w = keys(*STEPS[n % NSTEP])
                        at(act, "z_pe", m, n)
                        at(act, "mx", m, n - 4 if n >= 4 else -1)
                        act.activation(e[:, n % 4, 0:w], zb[n % 4][:, 0:w], ACT.Exp).then_inc(sem["e1"], 1)
                    k = n - 1
                    if 0 <= k < 2 * NSTEP:
                        w = keys(*STEPS[k % NSTEP])
                        at(act, "cl", m, k)
                        act.activation(e[:, k % 4, 0:w], e[:, k % 4, 0:w], ACT.Ln, bias=1.0).then_inc(sem["ln"], 1)
                    k = n - FLIP
                    if 0 <= k < 2 * NSTEP:
                        w = keys(*STEPS[k % NSTEP])
                        at(act, "t_pe", m, k)
                        act.copy(aT[:, k % 4, 0:w], tb[k % 2][:, 0:w]).then_inc(sem["t_ev"], 1)

                    k = n - 4
                    if 0 <= k < 2 * NSTEP:
                        w = keys(*STEPS[k % NSTEP])
                        at(act, "arg", m, k)
                        act.activation(att[:, k % 4, 0:w], sp_[:, k % 4, 0:w], ACT.Exp).then_inc(sem["e2"], 1)

        @block.vector
        def _(dve):
            dve.memset(one[:, :], 1.0).then_inc(rows, 1)
            dve.memset(kr[DC:DC + 1, :], 1.0).then_inc(rows, 1)
            dve.memset(bt[DC:DC + 1, HC:HC + 2], 0.0).then_inc(rows, 1)
            dve.wait_ge(cst, 48)
            dve.wait_ge(rows, 3)

            def split(m, q, part):
                if part == 0:
                    dve.wait_ge(slot["scaled"][q], m + 1)
                    dve.tensor_scalar(qr[DC:DC + 1, :], kr[DC:DC + 1, :], bt[DC:DC + 1, ds(m * 2 + q, 1)],
                                      None, ALU.mult).then_inc(slot["brow"][q], 1)
                    return
                n = part - 1
                half, low, which = n // 4, n % 4 // 2, n % 2
                hi, low_, x = splits(q, slice(half * SEQ // 2, (half + 1) * SEQ // 2))[which]
                if low:
                    dve.wait_ge(slot["high"][q], 4 * m + 2 * half + which + 1)
                    low_part(dve, low_, x, hi).then_inc(slot["split"][q], 1)
                else:
                    dve.wait_ge(slot["brow"][q], m + 1)
                    high_part(dve, hi, x).then_inc(slot["high"][q], 1)
            for part in range(9):
                split(0, 0, part)
            with dve.Fori(0, HC // 2) as m:

                def collect(tile):
                    i, q = tile % TT, tile // TT
                    dve.wait_ge(o_pe, m * 2 * TT + tile + 1)
                    dve.tensor_copy(oT[q][:, i * P:(i + 1) * P], ob[i % 2][0:DC, 0:P]).then_inc(o_ev, 1)
                tiles = 0
                for n in range(2 * NSTEP + 2):
                    if 0 <= n - (NSTEP - 14) < 9:
                        split(m, 1, n - (NSTEP - 14))
                    if 0 <= n - (2 * NSTEP - 14) < 9:
                        split(m + 1, 0, n - (2 * NSTEP - 14))
                    k = n - 1
                    if 0 <= k < 2 * NSTEP:
                        i, g = STEPS[k % NSTEP]
                        w = keys(i, g)
                        at(dve, "mx", m, k)
                        at(dve, "arg", m, k - 4 if k >= 4 else -1)
                        if g == i // 4:
                            start = 0.0
                        else:
                            at(dve, "sc", m, k - 1)
                            start = S[:, (k - 1) % 4, 0:1]
                        dve.tensor_tensor_scan(S[:, k % 4, 0:w][:, ::-1], one[:, 0:1].broadcast_to([P, w]),
                                               sp_[:, k % 4, 0:w][:, ::-1], start, ALU.mult,
                                               ALU.add).then_inc(sem["sc"], 1)
                        at(dve, "sc", m, k)
                        dve.tensor_tensor(sp_[:, k % 4, 0:w], zb[k % 4][:, 0:w], S[:, k % 4, 0:w],
                                          ALU.subtract).then_inc(sem["arg"], 1)
                    if n < 2 * NSTEP:
                        w = keys(*STEPS[n % NSTEP])
                        at(dve, "ln", m, n)
                        at(dve, "e2", m, n - 4 if n >= 4 else -1)
                        dve.tensor_tensor(sp_[:, n % 4, 0:w], e[:, n % 4, 0:w], zb[n % 4][:, 0:w],
                                          ALU.max).then_inc(sem["mx"], 1)
                    while tiles < 2 * TT and n >= (tiles // TT) * NSTEP + LAST[tiles % TT] + FLIP + 2:
                        collect(tiles)
                        tiles += 1
                for tile in range(tiles, 2 * TT):
                    collect(tile)

        @block.gpsimd
        def _(pool):
            with pool.Fori(0, HC // 2) as m:
                def gated(q):
                    pool.wait_ge(o_ev, m * 2 * TT + (q + 1) * TT)
                    pool.wait_ge(slot["gate"][q], m + 1)
                    pool.tensor_tensor(oT[q][:, :], oT[q][:, :], gt[q][:, :], ALU.mult
                                       ).then_inc(slot["gated"][q], 1)
                for n in range(2 * NSTEP):
                    if n == NSTEP + 10:
                        gated(0)
                    w = keys(*STEPS[n % NSTEP])
                    at(pool, "e1", m, n)
                    pool.sem_inc(held, 1)
                    pool.tensor_scalar(e[:, n % 4, 0:w], e[:, n % 4, 0:w], CLAMP, None, ALU.min
                                       ).then_inc(sem["cl"], 1)
                gated(1)


HD, DK, DV = 4, 64, 128
GLA_TAU = 16.0
G_Q, G_K, G_V = range(3)


def gla_operands(nc, z, alpha_w, alpha_b, const, ops, wc, sample_vecs):
    with Stage(nc, "gp") as s:
        two = lambda n: [s.sb(f"{n}{q}", [P, COLS]) for q in (0, 1)]
        qt, kt, l, c, ep, en, ec = two("q"), two("k"), two("l"), two("c"), two("ep"), two("en"), two("ec")
        ad, mask = s.sb("ad", [P, COLS]), s.sb("mask", [P, COLS])
        wt, bt, nb, idt = s.sb("w", [P, 256]), s.sb("b", [P, 2]), s.sb("nb", [P, 2]), s.sb("id", [P, P])
        wce = s.sb("wce", [P, 2, NCH])
        vec = s.sb("vec", [P, 2, 16, NS])
        vecT = s.sb("vecT", [3 * NS, 2, P])
        acc = s.ps("acc", [P, NBLK, 512])
        trp = s.ps("trp", [P, 2, P])
        names = ("cst", "mm", "e1", "cl", "ln", "blk", "scan", "ce", "exps", "vecs", "vtr", "vst", "out", "own",
                 "stored", "nbd")
        q_ = {n: s.sem(n) for n in names}
        blocks = [(b * BLK, min(BLK, COLS - b * BLK)) for b in range(NBLK)]
        block = s.block()

        @block.sync
        def _(sp):
            for dst, src in ((ad[:, :], z[20]), (mask[:, :], const["reset"]), (wt[:, :], alpha_w), (bt[:, :], alpha_b),
                             (idt[:, :], const["ident"]), (qt[0][:, :], z[12]), (qt[1][:, :], z[13]),
                             (kt[0][:, :], z[14]), (kt[1][:, :], z[15])):
                sp.dma_start(dst, src).then_inc(q_["cst"], 16)
            for j in (0, 1):
                sp.wait_ge(q_["out"], 3 * j + 3)
                for n, t in enumerate((ep, en, ec)):
                    sp.dma_start(ops[:, n, j, :], t[j][:, 0:SEQ]).then_inc(q_["stored"], 16)
                sp.wait_ge(q_["vst"], j + 1)
                sp.dma_start(sample_vecs[:, :, j * P:(j + 1) * P].rearrange("v b c -> (v b) c"),
                             vecT[:, j, :]).then_inc(q_["stored"], 16)
            sp.dma_start(wc, wce[:, :, :]).then_inc(q_["stored"], 16)
            sp.wait_ge(q_["stored"], 9 * 16)

        @block.tensor
        def _(pe):
            pe.wait_ge(q_["cst"], 144)
            for j in (0, 1):
                for b, (at, width) in enumerate(blocks):
                    if j:
                        pe.wait_ge(q_["blk"], b + 1)
                    pe.matmul(acc[:, b, 0:width], wt[:, j * P:(j + 1) * P], ad[:, at:at + width], start=True,
                              stop=True).then_inc(q_["mm"], 1)
            for j in (0, 1):
                pe.wait_ge(q_["vecs"], j + 1)
                if j:
                    pe.wait_ge(q_["vst"], 1)
                pe.transpose(trp[:, j, :], vec[:, j].rearrange("p v b -> p (v b)"), idt[:, :]).then_inc(q_["vtr"], 1)

        @block.scalar
        def _(act):
            act.wait_ge(q_["nbd"], 1)
            act.preload_act_table_set(LN_EXP)
            for j in (0, 1):
                for b, (at, width) in enumerate(blocks):
                    act.wait_ge(q_["mm"], j * NBLK + b + 1)
                    act.activation(l[j][:, at:at + width], acc[:, b, 0:width], ACT.Exp, scale=-1.0,
                                   bias=nb[:, j:j + 1]).then_inc(q_["e1"], 1)
                act.wait_ge(q_["cl"], j + 1)
                act.activation(l[j][:, :], l[j][:, :], ACT.Ln, bias=1.0).then_inc(q_["ln"], 1)
            for j in (0, 1):
                act.wait_ge(q_["scan"], j + 1)
                act.activation(ep[j][:, :], c[j][:, :], ACT.Exp, scale=1.0 / GLA_TAU).then_inc(q_["exps"], 1)
                act.activation(en[j][:, :], c[j][:, :], ACT.Exp, scale=-1.0 / GLA_TAU).then_inc(q_["exps"], 1)
                act.wait_ge(q_["ce"], j + 1)
                act.activation(ec[j][:, 0:SEQ], ec[j][:, 0:SEQ], ACT.Exp, scale=1.0 / GLA_TAU).then_inc(q_["exps"], 1)
                act.activation(wce[:, j, :], c[j][:, CH - 1:SEQ:CH], ACT.Exp,
                               scale=1.0 / GLA_TAU).then_inc(q_["exps"], 1)
                act.wait_ge(q_["vtr"], j + 1)
                act.copy(vecT[:, j, :], trp[0:3 * NS, j, :]).then_inc(q_["vst"], 1)

        @block.vector
        def _(dve):
            link = Chain(dve, q_["own"])
            link(dve.memset(vec[:, :, :, :], 0.0))
            dve.wait_ge(q_["cst"], 144)
            dve.tensor_scalar(nb[:, :], bt[:, :], -1.0, None, ALU.mult).then_inc(q_["nbd"], 1)
            for j in (0, 1):
                dve.wait_ge(q_["e1"], (j + 1) * NBLK)
                dve.tensor_scalar(l[j][:, :], l[j][:, :], CLAMP, None, ALU.min).then_inc(q_["cl"], 1)
                dve.wait_ge(q_["ln"], j + 1)
                link(dve.tensor_scalar(l[j][:, :], l[j][:, :], -1.0, None, ALU.mult))
                for b, (at, width) in enumerate(blocks):
                    dve.scalar_tensor_tensor(out=l[j][:, at:at + width], in0=acc[:, b, 0:width],
                                             scalar=bt[:, j:j + 1], in1=l[j][:, at:at + width], op0=ALU.add,
                                             op1=ALU.min).then_inc(q_["blk"], 1)
                dve.wait_ge(q_["blk"], (j + 1) * NBLK)
                dve.tensor_tensor_scan(c[j][:, :], mask[:, :], l[j][:, :], 0.0, ALU.mult,
                                       ALU.add).then_inc(q_["scan"], 1)
                dve.wait_ge(q_["scan"], j + 1)
                ends = c[j][:, CH - 1:SEQ:CH].rearrange("p (n o) -> p n o", o=1).broadcast_to([P, NCH, CH])
                dve.tensor_tensor(ec[j][:, 0:SEQ].rearrange("p (n t) -> p n t", t=CH), ends,
                                  c[j][:, 0:SEQ].rearrange("p (n t) -> p n t", t=CH),
                                  ALU.subtract).then_inc(q_["ce"], 1)
            for j in (0, 1):
                dve.wait_ge(q_["exps"], 4 * j + 4)
                dve.tensor_copy(vec[:, j, G_Q, :], qt[j][:, SEQ:COLS])
                dve.tensor_copy(vec[:, j, G_K, :], kt[j][:, SEQ:COLS])
                link(dve.tensor_copy(vec[:, j, G_V, :], ep[j][:, SEQ:COLS]))
                dve.sem_inc(q_["vecs"], 1)
                dve.scalar_tensor_tensor(out=ep[j][:, :], in0=qt[j][:, :], scalar=DK ** -0.5, in1=ep[j][:, :],
                                         op0=ALU.mult, op1=ALU.mult).then_inc(q_["out"], 1)
                dve.tensor_tensor(en[j][:, :], kt[j][:, :], en[j][:, :], ALU.mult).then_inc(q_["out"], 1)
                dve.tensor_tensor(ec[j][:, 0:SEQ], kt[j][:, 0:SEQ], ec[j][:, 0:SEQ], ALU.mult).then_inc(q_["out"], 1)


def gla_chunks(nc, ops, v, wc, const, o, s_out):
    COUNT = dict(ops_in=64, sc_pe=1, kh_pe=1, sc=1, kh=1, o_pe=1, s_pe=1, o_ev=1, o_st=16)
    with Stage(nc, "gc") as s:
        two = lambda n, shape: [s.sb(f"{n}{q}", shape) for q in (0, 1)]
        opx, v2 = two("opx", [P, 3, 2, P]), two("v2", [P, 2, DV])
        sc, kh, ot = two("sc", [P, 2, P]), two("kh", [P, 2, P]), two("ot", [P, HD, CH])
        st = two("st", [P, 2, DV])
        mask, idt, wct = s.sb("mask", [P, P]), s.sb("id", [P, P]), s.sb("wc", [P, 2, NCH])
        bank = [[s.ps(f"bank{q}{n}", [P, 512]) for n in range(4)] for q in (0, 1)]
        sem = {n: [s.sem(f"{n}{q}") for q in (0, 1)] for n in COUNT}
        cst, zero, s_sb, s_st = s.sem("cst"), s.sem("zero"), s.sem("s_sb"), s.sem("s_st")
        block = s.block()
        pair = lambda b: b[:, 0:256].rearrange("p (j c) -> p j c", j=2)

        def wait(eng, name, q, m, k):
            eng.wait_ge(sem[name][q], m * COUNT[name] + k)

        @block.sync
        def _(sp):
            for dst, src in ((mask[:, :], const["mask4"][:, P:2 * P]), (idt[:, :], const["ident"]),
                             (wct[:, :, :], wc)):
                sp.dma_start(dst, src).then_inc(cst, 16)
            sp.wait_ge(zero, 4)
            with sp.Fori(0, NCH // 4) as n:
                for t in (0, 1):
                    m = n * 2 + t
                    for q in (0, 1):
                        wait(sp, "o_pe", q, m, 0)
                        wait(sp, "s_pe", q, m, 0)
                        c = m * 2 + q
                        for h in (0, 1):
                            r = slice(64 * h, 64 * h + 64)
                            sp.dma_start(opx[q][r, :, :, r].rearrange("p n j c -> p (n j) c"),
                                         ops[r, :, :, ds(c * CH, CH)].rearrange("p n j c -> p (n j) c")
                                         ).then_inc(sem["ops_in"][q], 16)
                            src = v[ds(m, 1), 64 * q:64 * q + 64, 512:1024].rearrange("o p c -> p (o c)")
                            sp.dma_start(v2[q][r, :, :], src.rearrange("p (j h c) -> p h j c", j=2, h=2)[:, h]
                                         ).then_inc(sem["ops_in"][q], 16)
            sp.wait_ge(s_sb, NCH + 1)
            sp.dma_start(s_out, st[0][:, :, :]).then_inc(s_st, 16)
            sp.wait_ge(s_st, 16)

        @block.tensor
        def _(pe):
            pe.wait_ge(cst, 48)
            with pe.Fori(0, NCH // 2) as m:
                for q in (0, 1):
                    wait(pe, "ops_in", q, m, 64)
                    wait(pe, "sc", q, m, 0)
                    for j in (0, 1):
                        mm = pe.matmul(bank[q][0][:, j * P:(j + 1) * P], opx[q][:, 1, j, :], opx[q][:, 0, j, :],
                                       start=True, stop=True)
                    mm.then_inc(sem["sc_pe"][q], 1)
                    wait(pe, "kh", q, m, 0)
                    for j in (0, 1):
                        mm = pe.transpose(bank[q][1][:, j * P:(j + 1) * P], opx[q][:, 2, j, :], idt[:, :])
                    mm.then_inc(sem["kh_pe"][q], 1)
                for q in (0, 1):
                    wait(pe, "kh", q, m, 1)
                    pe.wait_ge(s_sb, m * 2 + q + 1)
                    for j in (0, 1):
                        mm = pe.matmul(bank[q][3][:, j * DV:(j + 1) * DV], kh[q][:, j, :], v2[q][:, j, :],
                                       start=True, stop=True)
                    mm.then_inc(sem["s_pe"][q], 1)
                    wait(pe, "sc", q, m, 1)
                    wait(pe, "o_ev", q, m, 0)
                    for j in (0, 1):
                        b = bank[q][2][:, j * P:(j + 1) * P]
                        pe.matmul(b, v2[q][:, j, :], sc[q][:, j, :], start=True, stop=False)
                        mm = pe.matmul(b, st[q][:, j, :], opx[q][:, 0, j, :], start=False, stop=True)
                    mm.then_inc(sem["o_pe"][q], 1)

        @block.scalar
        def _(act):
            with act.Fori(0, NCH // 2) as m:
                for q in (0, 1):
                    wait(act, "kh_pe", q, m, 1)
                    wait(act, "s_pe", q, m, 0)
                    act.copy(kh[q][:, :, :], pair(bank[q][1])).then_inc(sem["kh"][q], 1)
                for q in (0, 1):
                    wait(act, "o_pe", q, m, 1)
                    wait(act, "o_st", q, m, 0)
                    act.copy(ot[q][:, :, :].rearrange("p n c -> p (n c)"), bank[q][2][:, 0:256]
                             ).then_inc(sem["o_ev"][q], 1)
                    wait(act, "o_ev", q, m, 1)
                    act.dma_start(o[:, :, ds((m * 2 + q) * CH, CH)].rearrange("n p c -> p n c"),
                                  ot[q][:, :, :]).then_inc(sem["o_st"][q], 16)
            for q in (0, 1):
                act.wait_ge(sem["o_st"][q], 16 * NCH // 2)

        @block.vector
        def _(dve):
            for q in (0, 1):
                dve.memset(opx[q][:, :, :, :], 0.0).then_inc(zero, 1)
                dve.memset(st[q][:, :, :], 0.0).then_inc(zero, 1)
            dve.wait_ge(zero, 4)
            dve.sem_inc(s_sb, 1)
            dve.wait_ge(cst, 48)
            with dve.Fori(0, NCH // 2) as m:
                for q in (0, 1):
                    wait(dve, "sc_pe", q, m, 1)
                    wait(dve, "o_pe", q, m, 0)
                    dve.tensor_tensor(sc[q][:, :, :], pair(bank[q][0]),
                                      mask[:, :].rearrange("p (o c) -> p o c", o=1).broadcast_to([P, 2, P]),
                                      ALU.mult).then_inc(sem["sc"][q], 1)
                for q in (0, 1):
                    wait(dve, "s_pe", q, m, 1)
                    wait(dve, "o_pe", 1 - q, m, q)
                    dve.wait_ge(s_sb, m * 2 + q + 1)
                    dve.scalar_tensor_tensor(out=st[1 - q][:, 0, :], in0=st[q][:, 0, :],
                                             scalar=wct[:, 0, ds(m * 2 + q, 1)], in1=bank[q][3][:, 0:DV],
                                             op0=ALU.mult, op1=ALU.add)
                    dve.scalar_tensor_tensor(out=st[1 - q][:, 1, :], in0=st[q][:, 1, :],
                                             scalar=wct[:, 1, ds(m * 2 + q, 1)], in1=bank[q][3][:, DV:2 * DV],
                                             op0=ALU.mult, op1=ALU.add).then_inc(s_sb, 1)


def gla_samples(nc, vecs, v, state, ident, state_out, o):
    BH = NS * HD
    with Stage(nc, "gs") as s:
        S, T = s.sb("S", [BH, DK, DV]), s.sb("T", [BH, DK, DV])
        vt, vv, yt = s.sb("vec", [BH, 3, DK]), s.sb("v", [BH, DV]), s.sb("y", [BH, DV])
        yc, idt = s.sb("yc", [P, HD, NS]), s.sb("id", [P, P])
        tr = s.ps("tr", [P, 512])
        ready, own, out, y_done, tr_done, yc_done = (s.sem(n) for n in ("ready", "own", "out", "y_done", "tr", "yc"))
        block = s.block()

        @block.sync
        def _(sp):
            sp.dma_start(S[:, :, :], state).then_inc(ready, 16)
            sp.dma_start(idt[:, :], ident).then_inc(ready, 16)
            sp.dma_start(vt[:, :, :], vecs.rearrange("n b (h c) -> (b h) n c", c=DK)).then_inc(ready, 16)
            for b in range(NS):
                sp.dma_start(vv[b * HD:(b + 1) * HD, :],
                             v[b:b + 1, :].rearrange("o (h c) -> (o h) c", c=DV)).then_inc(ready, 16)
            sp.wait_ge(own, 3)
            sp.dma_start(state_out, S[:, :, :]).then_inc(out, 16)
            sp.wait_ge(yc_done, 1)
            sp.dma_start(o[:, :, SEQ:COLS].rearrange("n p c -> p n c"), yc[:, :, :]).then_inc(out, 16)
            sp.wait_ge(out, 32)

        @block.vector
        def _(dve):
            link = Chain(dve, own)
            col = lambda n: vt[:, n, :].rearrange("p (k o) -> p k o", o=1).broadcast_to([BH, DK, DV])
            row = vv[:, :].rearrange("p (o v) -> p o v", o=1).broadcast_to([BH, DK, DV])
            dve.wait_ge(ready, 16 * (3 + NS))
            dve.tensor_tensor(S[:, :, :], S[:, :, :], col(G_V), ALU.mult)
            link(dve.tensor_tensor(T[:, :, :], row, col(G_K), ALU.mult))
            link(dve.tensor_tensor(S[:, :, :], S[:, :, :], T[:, :, :], ALU.add))
            link(dve.tensor_tensor(T[:, :, :], S[:, :, :], col(G_Q), ALU.mult))
            link(dve.tensor_reduce(yt[:, :], T[:, :, :].rearrange("p k v -> p v k"), AX.X, ALU.add))
            dve.tensor_scalar(yt[:, :], yt[:, :], DK ** -0.5, None, ALU.mult).then_inc(y_done, 1)
            dve.wait_ge(tr_done, 1)
            dve.tensor_copy(yc[:, :, :], tr[:, 0:BH].rearrange("v (b h) -> v h b", h=HD)).then_inc(yc_done, 1)

        @block.tensor
        def _(pe):
            pe.wait_ge(ready, 16 * (3 + NS))
            pe.wait_ge(y_done, 1)
            pe.transpose(tr[:, 0:BH], yt[:, :], idt[0:BH, 0:BH]).then_inc(tr_done, 1)


def gla_output(nc, o, gate, gn, const, cat):
    with Stage(nc, "go") as s:
        two = lambda n: [s.sb(f"{n}{q}", [P, COLS]) for q in (0, 1)]
        ot, gt, sq, rs = two("o"), two("g"), two("sq"), two("rs")
        on, gnt, eps = s.sb("ones", [P, P]), s.sb("gn", [P, 4]), s.sb("eps", [P, 1])
        acc = s.ps("acc", [P, NBLK, 512])
        cst, mm_, free, eset = s.sem("cst"), s.sem("mm"), s.sem("free"), s.sem("eset")
        names = ("in", "sq", "gate", "rstd", "own", "out", "stored")
        sem = {n: [s.sem(f"{n}{q}") for q in (0, 1)] for n in names}
        blocks = [(b * BLK, min(BLK, COLS - b * BLK)) for b in range(NBLK)]
        block = s.block()

        @block.sync
        def _(sp):
            sp.dma_start(gnt[:, :], gn).then_inc(cst, 16)

            def store(h):
                q, m = h % 2, h // 2
                sp.wait_ge(sem["out"][q], m + 1)
                sp.dma_start(cat[4 + h], ot[q][:, :]).then_inc(sem["stored"][q], 16)
            for h in range(HD):
                q, m = h % 2, h // 2
                if m:
                    store(h - 2)
                    sp.wait_ge(sem["stored"][q], 16 * m)
                sp.dma_start(ot[q][:, :], o[h]).then_inc(sem["in"][q], 16)
                sp.dma_start(gt[q][:, :], gate[h]).then_inc(sem["in"][q], 16)
            for h in (HD - 2, HD - 1):
                store(h)
            for q in (0, 1):
                sp.wait_ge(sem["stored"][q], 32)

        @block.tensor
        def _(pe):
            pe.wait_ge(eset, 2)
            for h in range(HD):
                pe.wait_ge(sem["sq"][h % 2], h // 2 + 1)
                for b, (at, width) in enumerate(blocks):
                    if h:
                        pe.wait_ge(free, (h - 1) * NBLK + b + 1)
                    pe.matmul(acc[:, b, 0:width], on[:, :], sq[h % 2][:, at:at + width], start=True,
                              stop=True).then_inc(mm_, 1)

        @block.scalar
        def _(act):
            act.wait_ge(eset, 2)
            for h in range(HD):
                q, m = h % 2, h // 2
                act.wait_ge(sem["in"][q], 32 * (m + 1))
                act.activation(gt[q][:, :], gt[q][:, :], ACT.Silu).then_inc(sem["gate"][q], 1)
                act.activation(sq[q][:, :], ot[q][:, :], ACT.Square).then_inc(sem["sq"][q], 1)
                act.preload_act_table_set(LN_EXP)
                for b, (at, width) in enumerate(blocks):
                    act.wait_ge(mm_, h * NBLK + b + 1)
                    act.activation(rs[q][:, at:at + width], acc[:, b, 0:width], ACT.Ln, scale=1.0 / DV,
                                   bias=eps[:, 0:1]).then_inc(free, 1)
                act.wait_ge(free, (h + 1) * NBLK)
                act.activation(rs[q][:, :], rs[q][:, :], ACT.Exp, scale=-0.5).then_inc(sem["rstd"][q], 1)

        @block.vector
        def _(dve):
            dve.memset(on[:, :], 1.0).then_inc(eset, 1)
            dve.memset(eps[:, :], RMS_EPS).then_inc(eset, 1)
            dve.wait_ge(cst, 16)
            for h in range(HD):
                q, m = h % 2, h // 2
                dve.wait_ge(sem["rstd"][q], m + 1)
                dve.scalar_tensor_tensor(out=ot[q][:, :], in0=ot[q][:, :], scalar=gnt[:, h:h + 1], in1=rs[q][:, :],
                                         op0=ALU.mult, op1=ALU.mult).then_inc(sem["own"][q], 1)
                dve.wait_ge(sem["own"][q], m + 1)
                dve.wait_ge(sem["gate"][q], m + 1)
                dve.tensor_tensor(ot[q][:, :], ot[q][:, :], gt[q][:, :], ALU.mult).then_inc(sem["out"][q], 1)


GP = 4
NG = PAGES // GP
SLOTS = 4
CW = HC * DC


def stick_samples(nc, z, cache_k, cache_v, table, bias, const, q_rows, cat):
    HR = HC * PAGES
    with Stage(nc, "sd") as s:
        kp, vp = s.sb("k", [P, SLOTS, GP, CW]), s.sb("v", [P, SLOTS, GP, CW])
        prod = s.sb("prod", [P, 2, GP, CW])
        qb = s.sb("q", [P, NS, CW])
        zs = s.sb("scores", [P, 2, HC, PAGES])
        zb, e, sp_, pre = (s.sb(n, [P, HC, PAGES]) for n in ("z", "e", "softplus", "later"))
        att = s.sb("att", [P, HC, PAGES])
        mask = s.sb("mask", [P, HC, PAGES])
        bt, idt = s.sb("bias", [P, HC]), s.sb("id", [P, P])
        tri, one = s.sb("tri", [P, P]), s.sb("ones", [P, P])
        own = s.sb("own", [HC, CW])
        pt = s.sb("pt", [1, NS * PAGES], I32)
        qc, gc, qr = s.sb("qc", [P, 4, NS]), s.sb("gc", [P, 4, NS]), s.sb("qr", [NS, CW])
        om, oc = s.sb("om", [HC, NS, CW]), s.sb("oc", [P, 4, NS])
        within, total, sums, trp = (s.ps(n, [P, 512]) for n in ("within", "total", "sums", "trp"))
        names = ("cst", "tab", "q_in", "q_tr", "q_ev", "q_st", "qb_in", "set", "z_ok", "biased", "exp", "cl", "ln",
                 "sp", "tri_pe", "own", "arg", "att_ok", "o_ev", "mm", "gate", "out", "stored")
        q_ = {n: s.sem(n) for n in names}
        k_in = [s.sem(f"k_in{n}") for n in range(SLOTS)]
        v_in = [s.sem(f"v_in{n}") for n in range(SLOTS)]
        k_used, v_used = s.sem("k_used"), s.sem("v_used")
        LAP = NG // SLOTS
        block = s.block()
        flat = lambda t: t[:, :, :].rearrange("p h r -> p (h r)")

        def load_pages(eng, pages, cache, b, g, sem):
            for j in range(GP):
                page = eng.value_load(pt[0:1, ds(b * PAGES + (PAGES - 1 - GP * g - j), 1)], min_val=0,
                                      max_val=cache.shape[0] - 1)
                eng.dma_start(pages[:, g % SLOTS, j, :], cache[ds(page, 1)].rearrange("o k c -> k (o c)")
                              ).then_inc(sem[g % SLOTS], 16)

        def pipeline(eng, step):
            step(0, None, None)
            step(1, 0, None)
            with eng.Fori(0, NS - 2) as m:
                step(m + 2, m + 1, m)
            step(None, NS - 1, NS - 2)
            step(None, None, NS - 1)

        @block.sync
        def _(sp):
            sp.dma_start(pt[:, :], table).then_inc(q_["tab"], 16)
            sp.dma_start(qc[:, :, :], z[0:4, :, SEQ:COLS].rearrange("n p c -> p n c")).then_inc(q_["q_in"], 16)
            sp.dma_start(idt[:, :], const["ident"]).then_inc(q_["q_in"], 16)
            sp.dma_start(tri[:, :], const["tri"]).then_inc(q_["cst"], 16)
            sp.dma_start(own[:, :], const["own"]).then_inc(q_["cst"], 16)
            sp.dma_start(bt[:, :], bias.broadcast_to([P, HC])).then_inc(q_["cst"], 16)
            sp.dma_start(gc[:, :, :], z[8:12, :, SEQ:COLS].rearrange("n p c -> p n c")).then_inc(q_["cst"], 16)
            sp.wait_ge(q_["q_ev"], 1)
            sp.dma_start(q_rows, qr[:, :]).then_inc(q_["q_st"], 16)
            sp.wait_ge(q_["q_st"], 16)
            sp.dma_start(qb[:, :, :], q_rows.rearrange("(o b) c -> o b c", o=1).broadcast_to([P, NS, CW])
                         ).then_inc(q_["qb_in"], 16)
            sp.wait_ge(q_["tab"], 16)
            with sp.Fori(0, NS) as b:
                for g in range(NG):
                    sp.wait_ge(k_used, b * NG + g + 1)
                    load_pages(sp, kp, cache_k, b, g, k_in)
            sp.wait_ge(q_["out"], 1)
            sp.dma_start(cat[0:4, :, SEQ:COLS].rearrange("n p c -> p n c"), oc[:, :, :]).then_inc(q_["stored"], 16)
            sp.wait_ge(q_["stored"], 16)

        @block.tensor
        def _(pe):
            pe.wait_ge(q_["q_in"], 32)
            for t in range(4):
                mm = pe.transpose(trp[0:NS, t * P:(t + 1) * P], qc[:, t, :], idt[:, :])
            mm.then_inc(q_["q_tr"], 1)
            pe.wait_ge(q_["cst"], 64)
            pe.wait_ge(q_["set"], 3)
            with pe.Fori(0, NS) as b:
                pe.wait_ge(q_["sp"], b + 1)
                pe.matmul(within[:, 0:HR], tri[:, :], flat(sp_), start=True, stop=True)
                pe.matmul(total[:, 0:HR], one[:, :], flat(sp_), start=True, stop=True).then_inc(q_["tri_pe"], 1)
                pe.wait_ge(q_["att_ok"], b + 1)
                pe.wait_ge(q_["o_ev"], b + 1)
                for g in range(NG):
                    pe.wait_ge(v_in[g % SLOTS], (b * LAP + g // SLOTS + 1) * 16 * GP)
                    for j in range(GP):
                        r = g * GP + j
                        mm = pe.matmul(sums[0:HC, :], att[:, :, r], vp[:, g % SLOTS, j, :],
                                       start=(r == 0), stop=(r == PAGES - 1))
                    mm.then_inc(v_used, 1)
            pe.wait_ge(q_["o_ev"], NS + 1)
            for b in range(NS):
                for t in range(4):
                    mm = pe.matmul(total[:, t * NS + b:t * NS + b + 1], om[:, b, t * P:(t + 1) * P], one[0:HC, 0:1],
                                   start=True, stop=True)
            mm.then_inc(q_["mm"], 1)

        @block.scalar
        def _(act):
            act.wait_ge(q_["cst"], 64)
            act.activation(gc[:, :, :], gc[:, :, :], ACT.Silu).then_inc(q_["gate"], 1)
            act.preload_act_table_set(LN_EXP)
            act.wait_ge(q_["tab"], 16)
            with act.Fori(0, NS) as b:
                def values(groups):
                    for g in groups:
                        act.wait_ge(v_used, b * NG + g + 1)
                        load_pages(act, vp, cache_v, b, g, v_in)
                values(range(2))
                act.wait_ge(q_["biased"], b + 1)
                act.activation(flat(e), flat(zb), ACT.Exp).then_inc(q_["exp"], 1)
                act.wait_ge(q_["cl"], b + 1)
                act.activation(flat(sp_), flat(e), ACT.Ln, bias=1.0).then_inc(q_["ln"], 1)
                values(range(2, 3))
                act.wait_ge(q_["arg"], b + 1)
                act.activation(flat(att), flat(zb), ACT.Exp).then_inc(q_["att_ok"], 1)
                values(range(3, NG))

        @block.vector
        def _(dve):
            link = Chain(dve, q_["own"])
            dve.memset(one[:, :], 1.0).then_inc(q_["set"], 1)
            dve.memset(mask[:, :, 0:1], 0.0).then_inc(q_["set"], 1)
            dve.memset(mask[:, :, 1:PAGES], 1.0).then_inc(q_["set"], 1)
            dve.sem_inc(k_used, SLOTS)
            dve.sem_inc(v_used, SLOTS)
            dve.sem_inc(q_["z_ok"], 2)
            dve.sem_inc(q_["o_ev"], 1)
            dve.wait_ge(q_["q_tr"], 1)
            dve.tensor_scalar(qr[:, :], trp[0:NS, :], DC ** -0.5, None, ALU.mult).then_inc(q_["q_ev"], 1)
            dve.wait_ge(q_["cst"], 64)
            dve.wait_ge(q_["set"], 3)
            dve.wait_ge(q_["qb_in"], 16)

            def scores(b, g):
                dve.wait_ge(k_in[g % SLOTS], (b * LAP + g // SLOTS + 1) * 16 * GP)
                dve.wait_ge(q_["z_ok"], b * NG + g + 1)
                dve.tensor_tensor(prod[:, g % 2], kp[:, g % SLOTS],
                                  qb[:, ds(b, 1), :].broadcast_to([P, GP, CW]), ALU.mult).then_inc(k_used, 1)
                dve.wait_ge(k_used, SLOTS + b * NG + g + 1)
                dve.tensor_reduce(zs[:, 0, :, g * GP:(g + 1) * GP].rearrange("p h r -> p r h"),
                                  prod[:, g % 2].rearrange("p j (h c) -> p j h c", c=DC), AX.X,
                                  ALU.add).then_inc(q_["z_ok"], 1)

            def biased(b):
                dve.wait_ge(q_["z_ok"], 2 + (b + 1) * NG)
                if not (isinstance(b, int) and b == 0):
                    dve.wait_ge(q_["att_ok"], b)
                dve.tensor_tensor(zb[:, :, :], zs[:, 0], bt[:, :].rearrange("p (h o) -> p h o", o=1)
                                  .broadcast_to([P, HC, PAGES]), ALU.add).then_inc(q_["biased"], 1)
                dve.wait_ge(q_["biased"], b + 1)

            def clamp(b):
                dve.wait_ge(q_["exp"], b + 1)
                dve.tensor_scalar(flat(e), flat(e), CLAMP, None, ALU.min).then_inc(q_["cl"], 1)

            def softplus(b):
                dve.wait_ge(q_["ln"], b + 1)
                dve.tensor_tensor(flat(sp_), flat(sp_), flat(zb), ALU.max).then_inc(q_["sp"], 1)

            def argument(b):
                dve.wait_ge(q_["tri_pe"], b + 1)
                link.start(b * 1)
                dve.tensor_tensor(flat(zb), flat(zb), within[:, 0:HR], ALU.subtract)
                link(dve.tensor_tensor_scan(flat(pre), mask[:, :, :].rearrange("p n r -> p (n r)"), total[:, 0:HR],
                                            0.0, ALU.mult, ALU.add))
                dve.tensor_tensor(zb[:, :, 1:PAGES], zb[:, :, 1:PAGES], pre[:, :, 0:PAGES - 1],
                                  ALU.subtract).then_inc(q_["arg"], 1)

            def diagonal(b):
                dve.wait_ge(v_used, SLOTS + (b + 1) * NG)
                dve.tensor_tensor(om[:, ds(b, 1), :].rearrange("h o c -> h (o c)"), sums[0:HC, :], own[:, :],
                                  ALU.mult).then_inc(q_["o_ev"], 1)

            def step(b, last, done):
                after = {0: clamp, 1: softplus, 2: argument}
                if last is not None:
                    biased(last)
                for g in range(NG):
                    if b is not None:
                        scores(b, g)
                    if last is not None and g in after:
                        after[g](last)
                    if done is not None and g == 2:
                        diagonal(done)
            pipeline(dve, step)
            dve.wait_ge(q_["mm"], 1)
            dve.wait_ge(q_["gate"], 1)
            dve.tensor_tensor(oc[:, :, :].rearrange("p n b -> p (n b)"), total[:, 0:4 * NS],
                              gc[:, :, :].rearrange("p n b -> p (n b)"), ALU.mult).then_inc(q_["out"], 1)


def program(nc, I, O):
    def scratch(name, shape):
        return nc.dram_tensor(f"scratch_{name}", shape, F32).ap()

    z0 = O["z0"]
    project_channels(nc, "pe", I["xT"], I["w_e"], z0, 21)
    u = scratch("u", (TT + 1, P, 512))
    project_tokens(nc, "pu", lambda t, rows: I["xT_u"][ds(t, 1), :, :, 0:rows].rearrange("o p k c -> p (o k) c"),
                   I["w_u"], 512, u)
    ops, wc, vecs = scratch("ops", (P, 7, 4, SEQ)), scratch("wc", (P, 4, NCH)), scratch("vecs", (6, NS, 512))
    bonus, y_a = scratch("bonus", (4, P, COLS)), scratch("y_a", (P, 4, COLS))
    cat0 = scratch("cat0", (KT, P, COLS))
    rwkv_operands(nc, z0, I["z_last"], I["mu_low"], I["prm"], I["w2"], I["a2"], I, ops, wc, bonus, vecs)
    rwkv_chunks(nc, ops, wc, I, y_a, O["rwkv_p"])
    rwkv_samples(nc, vecs, I["state_rwkv"], I["ident"], O["rwkv_s"], y_a)
    rwkv_output(nc, y_a, bonus, z0[13:17], I["prm"], I["bones"], cat0)
    y_b = scratch("y_b", (P, 4, COLS))
    kept_l, kept_m, kept_a = scratch("kl", (P, 32, 16)), scratch("km", (P, 32, 16)), scratch("ka", (P, 2, 32))
    s5_prompt(nc, u, I["s5_par"], I["s5_mats"], I["s5_dcol"], I, y_b, O["s5_p"], kept_l, kept_m, kept_a)
    s5_samples(nc, u[TT, 0:NS, :], I["s5_par"], I["s5_in"], kept_l, kept_m, kept_a, I["s5_drow"], I, y_b, O["s5_s"])
    s5_glu(nc, y_b, z0[17:21], I["glu_w"], I["glu_b"], cat0)
    x1, x1T = scratch("x1", (COLS, D)), scratch("x1T", (P, KT, COLS))
    out_projection(nc, "oe", cat0, I["wo_e"], I["x"], I["ln_g"][0:1], I["ln_b"][0:1], I["ident"], x1, x1T)

    z1, v1 = O["z1"], O["v1"]
    project_channels(nc, "po", x1T, I["w_o"], z1, 21)
    project_tokens(nc, "pv", lambda t, rows: x1T[:, :, ds(t * P, rows)], I["w_v"], 1024, v1)
    cat1 = scratch("cat1", (KT, P, COLS))
    stick_prompt(nc, z1, v1, I["sb_bias"], I, cat1)
    stick_samples(nc, z1, I["cache_k"], I["cache_v"], I["pages"], I["sb_bias"], I, scratch("q_rows", (NS, 512)), cat1)
    gops, gwc, gvecs = scratch("gops", (P, 3, 2, SEQ)), scratch("gwc", (P, 2, NCH)), scratch("gvecs", (3, NS, 256))
    o_d = scratch("o_d", (HD, P, COLS))
    gla_operands(nc, z1, I["alpha_w"], I["alpha_b"], I, gops, gwc, gvecs)
    gla_chunks(nc, gops, v1, gwc, I, o_d, O["gla_p"])
    gla_samples(nc, gvecs, v1[TT, 0:NS, 512:1024], I["state_gla"], I["ident"], O["gla_s"], o_d)
    gla_output(nc, o_d, z1[16:20], I["gla_gn"], I, cat1)
    out_projection(nc, "oo", cat1, I["wo_o"], x1, I["ln_g"][1:2], I["ln_b"][1:2], I["ident"], O["y"], None)


OUTPUTS = {"z0": (21, P, COLS), "rwkv_p": (4, 2, 64, 64), "rwkv_s": (64, 64, 64), "s5_p": (P, 32),
           "s5_s": (P, NS, 32), "z1": (21, P, COLS), "v1": (TT + 1, P, 1024), "gla_p": (P, 2, DV),
           "gla_s": (NS * HD, DK, DV), "y": (COLS, D)}


def constants():
    i = np.arange(P)
    h, t = i // 64, i % 64
    same = h[:, None] == h[None, :]
    before, upto = same & (t[:, None] < t[None, :]), same & (t[:, None] <= t[None, :])
    level = lambda m: (same & (t[:, None] // (2 * m) == t[None, :] // (2 * m))
                       & ((t[:, None] // m) % 2 == 0) & ((t[None, :] // m) % 2 == 1))
    reset = np.ones((P, COLS))
    reset[:, 0:SEQ:CH] = 0
    reset[:, SEQ:] = 0
    jm = np.zeros((P, P))
    jm[64 + np.arange(64), np.arange(64)] = 1
    jm[np.arange(64), 64 + np.arange(64)] = -1
    return {"ident": np.eye(P), "bones": same, "mask4": np.concatenate([before, upto, before, upto], 1),
            "levels": np.stack([level(m) for m in (1, 2, 4, 8, 16, 32)], 1), "reset": reset,
            "neg": np.where(i[None, :] < i[:, None], 0, -1e30), "tri": i[:, None] >= i[None, :],
            "own": np.kron(np.eye(HC), np.ones((1, DC))), "jm": jm,
            "sgn": np.where(i[:, None] < 64, -1, 1)}


def layout(a):
    cat = np.concatenate
    chan = lambda v: v.reshape(-1, P).T
    twice = lambda v: cat([v.T, v.T])
    kpc = lambda w: w.reshape(-1, P, w.shape[-1]).transpose(1, 0, 2)
    tiles = lambda w: w.reshape(KT, P, -1, P).transpose(2, 1, 0, 3)
    x = cat([a["x_prompt"][0], a["x_sample"][:, 0]])
    we, wo = a["w_in_e"][0], a["w_in_o"][0]
    xT = x.T.reshape(KT, P, COLS).transpose(1, 0, 2)
    xT_u = np.zeros((TT + 1, P, KT, P), x.dtype)
    xT_u[:TT] = xT[:, :, :SEQ].reshape(P, KT, 2, P, 8).transpose(2, 4, 0, 1, 3).reshape(TT, P, KT, P)
    xT_u[TT, :, :, :NS] = xT[:, :, SEQ:]
    mu = a["mu_shift"][0]
    vec = lambda n: a[n][0].reshape(-1)
    w2, a2 = np.zeros((2, P, 512), x.dtype)
    w2[:64], a2[64:] = a["rwkv_w2"][0], a["rwkv_a2"][0]
    alpha_w = np.zeros((P, 256), x.dtype)
    alpha_w[:16] = a["gla_alpha_w"][0]
    B = lambda n: a[n][0].transpose(1, 0, 2)
    C = lambda n: a[n][0].transpose(2, 0, 1)
    br, bi, cr, ci = B("s5_b_re"), B("s5_b_im"), C("s5_c_re"), C("s5_c_im")
    hr, hi = (a[n][0].transpose(2, 0, 1) for n in ("state_s5_re", "state_s5_im"))
    e_cols = np.r_[0:2176, 2688:3200]
    o_cols = np.r_[0:1024, 1536:2560, 3088:3600, 3072:3088]
    w_o = np.zeros((D, 21 * P), x.dtype)
    w_o[:, :o_cols.size] = wo[:, o_cols]
    return {
        "xT": xT, "xT_u": xT_u, "x": x, "w_e": tiles(we[:, e_cols]), "w_u": kpc(we[:, 2176:2688]),
        "z_last": a["state_shift"][0].T.reshape(13, P, NS).transpose(1, 0, 2), "mu_low": mu[1536:, None],
        "prm": np.stack([chan(mu[0:512]), chan(mu[512:1024]), chan(mu[1024:1536])] + [chan(vec(n)) for n in (
            "rwkv_w0", "rwkv_a0", "rwkv_k_k", "rwkv_k_a", "rwkv_r_k", "rwkv_gn_g", "rwkv_gn_b")], 2),
        "w2": w2, "a2": a2, "state_rwkv": a["state_rwkv"][0].reshape(64, 64, 64),
        "s5_par": np.stack([twice(a["s5_lambda_re"][0]), twice(a["s5_lambda_im"][0]),
                            np.broadcast_to(a["s5_log_dt"][0], (P, 32))], 1),
        "s5_mats": np.stack([cat([br, bi]), cat([bi, br]), cat([cr, ci]), cat([ci, cr])], 1),
        "s5_dcol": np.tile(a["s5_d"][0].reshape(32, 16).T, (8, 1)), "s5_drow": a["s5_d"],
        "s5_in": np.stack([cat([hr, hi]), cat([hi, hr])], 1), "glu_w": kpc(a["s5_glu_w"][0]),
        "glu_b": chan(vec("s5_glu_b")), "wo_e": kpc(a["w_out_e"][0]), "ln_g": a["ln_g"], "ln_b": a["ln_b"],
        "w_o": tiles(w_o), "w_v": kpc(wo[:, np.r_[1024:1536, 2560:3072]]), "sb_bias": a["sb_bias"],
        "cache_k": a["cache_k"][0].reshape(-1, P, CW), "cache_v": a["cache_v"][0].reshape(-1, P, CW),
        "pages": a["page_table"].reshape(1, -1), "alpha_w": alpha_w, "alpha_b": chan(vec("gla_alpha_b")),
        "state_gla": a["state_gla"][0].reshape(NS * HD, DK, DV), "gla_gn": chan(vec("gla_gn_g")),
        "wo_o": kpc(a["w_out_o"][0])}


def results(r):
    z0, z1, v1, fin, h = r["z0"], r["z1"], r["v1"], r["s5_p"], r["s5_s"]
    z0 = z0[0:13].reshape(13 * P, COLS)
    k = z1[4:8].reshape(CW, COLS).T.reshape(COLS, HC, DC)
    v_p, v_s = v1[0:TT, :, 0:CW].reshape(SEQ, HC, DC), v1[TT, 0:NS, 0:CW].reshape(NS, HC, DC)
    lead = lambda v: v[None]
    return (lead(r["y"][:SEQ]), r["y"][SEQ:][:, None],
            r["rwkv_p"].reshape(1, 1, 8, 64, 64).transpose(0, 1, 2, 4, 3), r["rwkv_s"].reshape(1, NS, 8, 64, 64),
            z0[:, SEQ - 1][None, None], lead(z0[:, SEQ:].T),
            fin[:64].T[None, None], lead(h[:64].transpose(1, 2, 0)), fin[64:].T[None, None],
            lead(h[64:].transpose(1, 2, 0)),
            k[:SEQ][None, None], k[SEQ:][None, :, None], v_p[None, None], v_s[None, :, None],
            r["gla_p"].reshape(2, DK, 2, DV).transpose(2, 0, 1, 3).reshape(1, 1, HD, DK, DV),
            r["gla_s"].reshape(1, NS, HD, DK, DV))


def kernel(**inputs):
    import concourse.bacc as bacc
    from concourse.bass_utils import run_bass_kernel_spmd

    nc = bacc.Bacc("TRN2", target_bir_lowering=False, num_devices=1)
    arrays = {n: np.ascontiguousarray(v) for n, v in layout({n: np.asarray(v) for n, v in inputs.items()}).items()}
    arrays.update({n: np.ascontiguousarray(v.astype(np.float32)) for n, v in constants().items()})
    ins = {n: nc.dram_tensor(f"in_{n}", v.shape, mybir.dt.from_np(v.dtype), kind="ExternalInput").ap()
           for n, v in arrays.items()}
    outs = {n: nc.dram_tensor(f"out_{n}", shape, F32, kind="ExternalOutput").ap() for n, shape in OUTPUTS.items()}
    program(nc, ins, outs)
    r = run_bass_kernel_spmd(nc, [{f"in_{n}": v for n, v in arrays.items()}], core_ids=[0])
    return tuple(np.ascontiguousarray(v) for v in results({n: r.results[0][f"out_{n}"] for n in OUTPUTS}))
```
